# Optimizing a Trainium2 kernel written in Bass

```python
import math
import jax, jax.numpy as jnp
from jax import lax
import numpy as np

D_MODEL = 1024
BATCH = 1
SEQ = 128
DEPTH = 1
DEC_BATCH = 1
DEC_SEQ = 512
PAST_LEN = 256

GRID_W = 64
HG_WIDTH = D_MODEL // 2
HG_DK = 128
HG_HEADS = HG_WIDTH // HG_DK
HG_DV = HG_WIDTH // HG_HEADS
HY_WIDTH = D_MODEL - HG_WIDTH
N_IN = 5 * HG_WIDTH + 3 * HY_WIDTH
CHUNK = 64
CONV_W = 3
D_FF = 2816
HY_BANDS = 16
HY_EMB = 1 + 2 * HY_BANDS
HY_ORDER = 64
HY_TARGET = 1e-2
HY_FAST = 0.3
HY_SLOW = 1.5
EPS = 1e-6

kernel_name = "hybrid_hgrn2_hyena_diffusion_step"

F32 = jnp.float32

def _rmsnorm(x, w):
    xf = x.astype(F32)
    y = xf * lax.rsqrt(jnp.mean(xf * xf, axis=-1, keepdims=True) + EPS)
    return (y * w.astype(F32)).astype(x.dtype)

def _dwconv3(x, w, rows):
    B, L, C = x.shape
    xr = x.reshape(B, rows, L // rows, C)
    xp = jnp.pad(xr, ((0, 0), (0, 0), (1, 1), (0, 0)))
    y = w[0] * xp[:, :, :-2] + w[1] * xp[:, :, 1:-1] + w[2] * xp[:, :, 2:]
    return y.reshape(B, L, C)

def _lower_bounds(p):
    s = jax.nn.softmax(p.astype(F32), axis=0)
    cs = jnp.cumsum(s, axis=0)
    return cs - cs[0:1]

def _log_forget(x, lb):
    return jnp.logaddexp(jnp.log(lb), jnp.log1p(-lb) + jax.nn.log_sigmoid(x.astype(F32)))

def _chunk_scan(q, k, v, log_f, s0):
    B, L, H, DK = q.shape
    DV = v.shape[-1]
    nc = L // CHUNK

    def to_chunks(a):
        return a.reshape(B, nc, CHUNK, H, a.shape[-1]).transpose(1, 0, 3, 2, 4)

    qc, kc, vc, gc = to_chunks(q), to_chunks(k), to_chunks(v), to_chunks(log_f)
    mask = jnp.tril(jnp.ones((CHUNK, CHUNK), dtype=bool))[None, None, :, :, None]

    def step(S, inp):
        qi, ki, vi, gi = inp
        b = jnp.cumsum(gi, axis=2)
        diff = b[:, :, :, None, :] - b[:, :, None, :, :]
        decay = jnp.exp(jnp.where(mask, diff, -jnp.inf))
        scores = jnp.einsum('bhjd,bhid,bhjid->bhji', qi, ki, decay)
        o = jnp.einsum('bhji,bhiv->bhjv', scores, vi) + jnp.einsum('bhjd,bhdv->bhjv', qi * jnp.exp(b), S)
        b_last = b[:, :, -1:, :]
        S_new = jnp.exp(b_last[:, :, 0, :, None]) * S + jnp.einsum('bhid,bhiv->bhdv', ki * jnp.exp(b_last - b), vi)
        return S_new, o

    s_fin, oc = lax.scan(step, s0.astype(F32), (qc, kc, vc, gc))
    o = oc.transpose(1, 0, 3, 2, 4).reshape(B, L, H, DV)
    return o, s_fin

def _hyena_filter(L, w1, b1, fr1, w2, b2, fr2, w3):
    t = jnp.linspace(0.0, 1.0, L, dtype=F32)[:, None]
    pos = jnp.arange(L, dtype=F32)[:, None]
    bands = jnp.linspace(1e-4, HY_BANDS - 1, HY_BANDS, dtype=F32)[None, :]
    ang = 2.0 * math.pi * pos * bands / L
    feats = jnp.concatenate([t, jnp.cos(ang), jnp.sin(ang)], axis=-1)
    h = jnp.sin(fr1.astype(F32) * (feats @ w1.astype(F32) + b1.astype(F32)))
    h = jnp.sin(fr2.astype(F32) * (h @ w2.astype(F32) + b2.astype(F32)))
    h = h @ w3.astype(F32)
    min_decay = math.log(HY_TARGET) / HY_SLOW
    max_decay = math.log(HY_TARGET) / HY_FAST
    deltas = jnp.abs(jnp.linspace(min_decay, max_decay, HY_WIDTH, dtype=F32))
    deltas = jnp.concatenate([deltas, deltas])
    h = h * jnp.exp(-t * deltas[None, :])
    h_f, h_b = h[:, :HY_WIDTH], h[:, HY_WIDTH:]
    kern = jnp.concatenate([h_f, jnp.zeros((1, HY_WIDTH), F32), h_b[1:][::-1]], axis=0)
    return kern / (jnp.sum(jnp.abs(kern), axis=0, keepdims=True) + EPS)

def _long_conv(u, kern):
    L = u.shape[1]
    uf = jnp.fft.rfft(u.astype(F32), n=2 * L, axis=1)
    kf = jnp.fft.rfft(kern, n=2 * L, axis=0)
    return jnp.fft.irfft(uf * kf[None], n=2 * L, axis=1)[:, :L]

def _mixer(h, rows, s0, l, p):
    B, L, _ = h.shape
    proj = jnp.einsum('bld,de->ble', h, p['w_in'][l])
    cuts = [HG_WIDTH * i for i in range(1, 6)]
    q, ff, fb, iv, g, hy = jnp.split(proj, cuts, axis=-1)

    def heads(a):
        return a.reshape(B, L, HG_HEADS, -1)

    qh = heads(jax.nn.silu(q.astype(F32)) * (HG_DK ** -0.5))
    vh = heads(iv.astype(F32))
    logf_f = heads(_log_forget(ff, _lower_bounds(p['hg_lb_fwd'])[l]))
    logf_b = heads(_log_forget(fb, _lower_bounds(p['hg_lb_bwd'])[l]))
    k_f = -jnp.expm1(logf_f)
    k_b = -jnp.expm1(logf_b)
    o_f, s_f = _chunk_scan(qh, k_f, vh, logf_f, s0[:, 0])
    rev = lambda a: a[:, ::-1]
    o_b, s_b = _chunk_scan(rev(qh), rev(k_b), rev(vh), rev(logf_b), s0[:, 1])
    o = o_f + rev(o_b)
    o = o * lax.rsqrt(jnp.mean(o * o, axis=-1, keepdims=True) + EPS)
    o = o * p['hg_norm_w'][l].astype(F32).reshape(HG_HEADS, HG_DV)
    o_hg = o.reshape(B, L, HG_WIDTH) * jax.nn.silu(g.astype(F32))

    hyc = _dwconv3(hy, p['hy_conv_w'][l], rows).astype(F32)
    v, x1, x2 = jnp.split(hyc, [HY_WIDTH, 2 * HY_WIDTH], axis=-1)
    kern = _hyena_filter(L, p['hy_w1'][l], p['hy_b1'][l], p['hy_freq1'][l],
                         p['hy_w2'][l], p['hy_b2'][l], p['hy_freq2'][l], p['hy_w3'][l])
    u = x1 * v
    z = _long_conv(u, kern) + p['hy_d'][l].astype(F32) * u
    y_hy = x2 * z
    y_hy = y_hy * lax.rsqrt(jnp.mean(y_hy * y_hy, axis=-1, keepdims=True) + EPS) * p['hy_norm_w'][l].astype(F32)

    merged = jnp.concatenate([o_hg, y_hy], axis=-1).astype(h.dtype)
    out = jnp.einsum('ble,ed->bld', merged, p['w_out'][l])
    return out, jnp.stack([s_f, s_b], axis=1)

def _convffn(h, rows, l, p):
    up = jnp.einsum('bld,df->blf', h, p['ffn_w_up'][l])
    up = _dwconv3(up, p['ffn_conv_w'][l], rows)
    gate, val = jnp.split(up, 2, axis=-1)
    return jnp.einsum('blf,fd->bld', jax.nn.silu(gate) * val, p['ffn_w_down'][l])

def _layer(x, cvec, rows, s0, l, p):
    mod = jnp.einsum('bd,de->be', jax.nn.silu(cvec), p['ada_w'][l]) + p['ada_b'][l]
    sh1, sc1, g1, sh2, sc2, g2 = [m[:, None, :] for m in jnp.split(mod, 6, axis=-1)]
    h = _rmsnorm(x, p['norm1_w'][l]) * (1 + sc1) + sh1
    mix, s_fin = _mixer(h, rows, s0, l, p)
    x = x + g1 * mix
    h = _rmsnorm(x, p['norm2_w'][l]) * (1 + sc2) + sh2
    x = x + g2 * _convffn(h, rows, l, p)
    return x.astype(cvec.dtype), s_fin

def setup_inputs(seed: int = 0) -> dict:
    key = jax.random.key(seed)
    ks = jax.random.split(key, 32)
    n = lambda k, s, sc: jax.random.normal(k, s, F32) * sc
    D = D_MODEL
    return {
        "x_prompt": n(ks[0], (BATCH, SEQ, D), 1.0),
        "x_sample": n(ks[1], (DEC_BATCH, DEC_SEQ, D), 1.0),
        "state_hgrn": n(ks[2], (DEC_BATCH, DEPTH, 2, HG_HEADS, HG_DK, HG_DV), 0.5),
        "c": n(ks[3], (DEC_BATCH, D), 1.0),
        "c_ctx": n(ks[4], (D,), 1.0),
        "w_in": n(ks[5], (DEPTH, D, N_IN), D ** -0.5),
        "w_out": n(ks[6], (DEPTH, D, D), D ** -0.5),
        "ada_w": n(ks[7], (DEPTH, D, 6 * D), 0.5 * D ** -0.5),
        "ada_b": n(ks[8], (DEPTH, 6 * D), 0.02),
        "norm1_w": 1.0 + n(ks[9], (DEPTH, D), 0.05),
        "norm2_w": 1.0 + n(ks[10], (DEPTH, D), 0.05),
        "hg_lb_fwd": n(ks[11], (DEPTH, HG_WIDTH), 1.0),
        "hg_lb_bwd": n(ks[12], (DEPTH, HG_WIDTH), 1.0),
        "hg_norm_w": 1.0 + n(ks[13], (DEPTH, HG_WIDTH), 0.05),
        "hy_conv_w": n(ks[14], (DEPTH, CONV_W, 3 * HY_WIDTH), 0.6),
        "hy_w1": n(ks[15], (DEPTH, HY_EMB, HY_ORDER), HY_EMB ** -0.5),
        "hy_b1": n(ks[16], (DEPTH, HY_ORDER), 0.1),
        "hy_freq1": 1.0 + n(ks[17], (DEPTH, HY_ORDER), 0.05),
        "hy_w2": n(ks[18], (DEPTH, HY_ORDER, HY_ORDER), HY_ORDER ** -0.5),
        "hy_b2": n(ks[19], (DEPTH, HY_ORDER), 0.1),
        "hy_freq2": 1.0 + n(ks[20], (DEPTH, HY_ORDER), 0.05),
        "hy_w3": n(ks[21], (DEPTH, HY_ORDER, 2 * HY_WIDTH), HY_ORDER ** -0.5),
        "hy_d": n(ks[22], (DEPTH, HY_WIDTH), 1.0),
        "hy_norm_w": 1.0 + n(ks[23], (DEPTH, HY_WIDTH), 0.05),
        "ffn_w_up": n(ks[24], (DEPTH, D, 2 * D_FF), D ** -0.5),
        "ffn_conv_w": n(ks[25], (DEPTH, CONV_W, 2 * D_FF), 0.6),
        "ffn_w_down": n(ks[26], (DEPTH, D_FF, D), D_FF ** -0.5),
        "final_norm_w": 1.0 + n(ks[27], (D,), 0.05),
    }

def reference(x_prompt, x_sample, state_hgrn, c, c_ctx, w_in, w_out, ada_w, ada_b,
              norm1_w, norm2_w, hg_lb_fwd, hg_lb_bwd, hg_norm_w, hy_conv_w,
              hy_w1, hy_b1, hy_freq1, hy_w2, hy_b2, hy_freq2, hy_w3, hy_d, hy_norm_w,
              ffn_w_up, ffn_conv_w, ffn_w_down, final_norm_w):
    p = dict(w_in=w_in, w_out=w_out, ada_w=ada_w, ada_b=ada_b, norm1_w=norm1_w,
             norm2_w=norm2_w, hg_lb_fwd=hg_lb_fwd, hg_lb_bwd=hg_lb_bwd, hg_norm_w=hg_norm_w,
             hy_conv_w=hy_conv_w, hy_w1=hy_w1, hy_b1=hy_b1, hy_freq1=hy_freq1, hy_w2=hy_w2,
             hy_b2=hy_b2, hy_freq2=hy_freq2, hy_w3=hy_w3, hy_d=hy_d, hy_norm_w=hy_norm_w,
             ffn_w_up=ffn_w_up, ffn_conv_w=ffn_conv_w, ffn_w_down=ffn_w_down)

    bp = x_prompt.shape[0]
    zero_state = jnp.zeros((bp, 2, HG_HEADS, HG_DK, HG_DV), F32)
    cvec_ctx = jnp.broadcast_to(c_ctx[None, :], (bp, c_ctx.shape[0])).astype(x_prompt.dtype)
    xp = x_prompt
    ctx_states = []
    for l in range(DEPTH):
        xp, st = _layer(xp, cvec_ctx, 1, zero_state, l, p)
        ctx_states.append(st)
    y_prompt = _rmsnorm(xp, final_norm_w)
    new_state_hgrn = jnp.stack(ctx_states, axis=1)

    rows = x_sample.shape[1] // GRID_W
    xs = x_sample
    for l in range(DEPTH):
        xs, _ = _layer(xs, c.astype(x_sample.dtype), rows, state_hgrn[:, l], l, p)
    y_sample = _rmsnorm(xs, final_norm_w)
    return (y_prompt, y_sample, new_state_hgrn)


_drawn_inputs = setup_inputs


def setup_inputs(seed=0):
    import zlib

    import numpy as np

    out = dict(_drawn_inputs(seed))
    spreads = {}
    factors = {'state_hgrn': 8.0,
     'norm2_w': 4.025,
     'hg_norm_w': 8.0,
     'hy_b1': 8.0,
     'hy_freq1': 8.0,
     'hy_b2': 7.586,
     'hy_freq2': 8.0,
     'hy_norm_w': 5.827}
    for name, (base, spread) in spreads.items():
        noise = np.random.default_rng([zlib.crc32(name.encode()), seed]).standard_normal(out[name].shape)
        drawn = base * np.exp(spread * noise) if base else spread * noise
        out[name] = __import__('jax').numpy.asarray(drawn.astype(out[name].dtype))
    for name, factor in factors.items():
        out[name] = (out[name] * factor).astype(out[name].dtype)
    return out
```

```python
import math
from contextlib import ExitStack

import numpy as np
import concourse.bass as bass
from concourse import mybir

F32 = mybir.dt.float32
F32R = mybir.dt.float32r
U32 = mybir.dt.uint32
U8 = mybir.dt.uint8
ALU = mybir.AluOpType
ACT = mybir.ActivationFunctionType

P = 128
D = 1024
KD = D // P
TS, TP = 512, 128
T = TS + TP
NT = T // P
HT = T // 2
GRID = 64
ROWS = TS // GRID
PADROW = GRID + 1
PADS = ROWS * PADROW
CONV = PADS + TP
PAD = CONV + 2
HEADS = 4
HW = 512
NC = HW // P
F = 2816
NF = F // P
NHID = 64
NEMB = 33
LEVELS = 7
EPS = 1e-6
SCALE = P ** -0.5
UNIT = 1024
RAW = 2
RAWS = 3
SPLITS = 3
ROUNDS = [(0, 8), (8, 8), (16, 6)]

VEC = {}
_at = 0
for _name, _n in (("c", KD), ("c_ctx", KD), ("norm1", KD), ("norm2", KD), ("ada_b", 6 * KD),
                  ("lb_f", NC), ("lb_b", NC), ("hg_norm", NC), ("hy_d", NC), ("hy_norm", NC),
                  ("hy_conv", 3 * 3 * NC), ("ffn_conv", 3 * 2 * NF),
                  ("b1", 1), ("fr1", 1), ("b2", 1), ("fr2", 1)):
    VEC[_name] = _at
    _at += _n
NVEC = _at

TILES = []
_hy = 0
for _g in range(HEADS + 1):
    _n = (0, 2, 2, 2, 6)[_g]
    TILES += [("hy", _hy + i) for i in range(_n)]
    _hy += _n
    if _g < HEADS:
        TILES += [(k, _g) for k in ("q", "g", "ff", "fb")]
STEPS = 12
FIRST_STEP = 9
DIAG, LEVEL0, KTURN, KV, OUT, NORM = 0, 1, 8, 9, 10, 11


def tile_column(tile):
    kind, i = tile
    if kind == "hy":
        return 5 * HW + (i % 3) * HW + (i // 3) * P
    return {"q": 0, "ff": 1, "fb": 2, "g": 4}[kind] * HW + i * P


ADA1, IV, PROJ, ADA2, WOUT = 8, 2, len(TILES) // 2, 16, 4
SLOT_IV = ADA1
SLOT_PROJ = SLOT_IV + IV
SLOT_ADA2 = SLOT_PROJ + PROJ
SLOT_WOUT = SLOT_ADA2 + ADA2
SLOT_FFN = SLOT_WOUT + WOUT
SLOT_UNITS = [RAW] * SLOT_FFN
for _f0, _nf in ROUNDS:
    SLOT_UNITS += [RAW] * _nf
    for _n in range(2):
        SLOT_UNITS += [min(4, _nf - f) // 2 for f in range(0, _nf, 4)]
NSLOT = len(SLOT_UNITS)
IS_ADA = [s < SLOT_IV or SLOT_ADA2 <= s < SLOT_WOUT for s in range(NSLOT)]
UNITS = [(s, u) for s in range(NSLOT) if not IS_ADA[s] for u in range(SLOT_UNITS[s])]
NU = len(UNITS)
UNIT_TILE = 2 * IV
UNIT_WOUT = UNIT_TILE + len(TILES)
UNIT_FFN = UNIT_WOUT + 2 * WOUT


def unit_last():
    out, plain, down = [], 0, 0

    def token_major(pairs, name, value):
        nonlocal plain
        for _ in range(pairs - 1):
            plain += 1
            out.append(("unit_done", plain))
        out.append((name, value))

    token_major(2 * IV, "v_bank", NT)
    out.extend(("half_made", 2 * t + 2) for t in range(len(TILES)))
    token_major(WOUT, "mixed", NT)
    token_major(WOUT, "mixed", 2 * NT)
    t = len(TILES)
    for _, nf in ROUNDS:
        out.extend(("half_made", 2 * (t + i) + 2) for i in range(2 * nf))
        t += 2 * nf
        for _ in range(2):
            down += NT
            token_major(nf // 2, "down_made", down)
    return out


UNIT_LAST = unit_last()
assert len(UNIT_LAST) == NU


def constants():
    c = {}
    c["ident"] = np.eye(P, dtype=np.float32)
    c["diag"] = (np.eye(P) * SCALE).astype(np.float32)
    i, j = np.arange(P)[:, None], np.arange(P)[None, :]
    c["masks"] = np.stack([((i >> (l + 1)) == (j >> (l + 1))) & ((i >> l) != (j >> l))
                           for l in range(LEVELS)], 1).astype(np.uint32)
    order = np.concatenate([np.arange(0, TS, 2), np.arange(1, TS, 2)])

    def feats(L, pos):
        t = np.linspace(0.0, 1.0, L, dtype=np.float32)[pos]
        bands = np.linspace(1e-4, 15, 16, dtype=np.float32)
        ang = (np.float32(2.0 * math.pi) * pos[:, None].astype(np.float32) * bands[None, :] / np.float32(L)).astype(np.float32)
        return t, np.concatenate([t[:, None], np.cos(ang), np.sin(ang)], 1)

    ts, fs = feats(TS, order)
    tp, fp = feats(TP, np.arange(TP))
    c["feats"] = np.ascontiguousarray(np.concatenate([fs, fp]).T.astype(np.float32))
    deltas = np.abs(np.linspace(math.log(1e-2) / 1.5, math.log(1e-2) / 0.3, HW, dtype=np.float32))
    dec = np.exp(-np.concatenate([ts, tp])[:, None] * deltas[None, :]).astype(np.float32)
    c["decay"] = np.ascontiguousarray(dec.reshape(NT, P, HW).transpose(1, 0, 2))

    th = math.pi * (2 * np.arange(TS // 2) + 1) / (2 * TS)
    n = order.reshape(2, 2, P)

    def tab(shift):
        a = n[..., None] * th if not shift else (n[..., None] + 0.5) * th
        return np.stack([np.cos(a), np.sin(a)], 0)

    c["ktab"] = np.ascontiguousarray(tab(0).transpose(3, 0, 1, 2, 4).astype(np.float32))
    c["utab"] = np.ascontiguousarray(tab(1).transpose(3, 0, 1, 2, 4).astype(np.float32))
    inv = tab(1).reshape(2, 2, 2 * P, 2, P) / TS
    c["itab"] = np.ascontiguousarray(inv.transpose(4, 3, 0, 1, 2).astype(np.float32))
    tg = math.pi * (2 * np.arange(TP) + 1) / (2 * TP)
    m = np.arange(TP)
    k = np.stack([np.cos(m[:, None] * tg), np.sin(m[:, None] * tg)], 1)
    u = np.stack([np.cos((m[:, None] + 0.5) * tg), np.sin((m[:, None] + 0.5) * tg)], 1)
    v = (u.transpose(2, 1, 0)) / TP
    c["ptab"] = np.ascontiguousarray(np.stack([k, u, v], 1).astype(np.float32))
    return c




def ap(t, offset, dims):
    base = t[:]
    return bass.AP(tensor=base.tensor, offset=offset, ap=[base.ap[0], *[list(d) for d in dims]])


def build(nc, io):
    ctx = ExitStack()

    def sb(stack, name, shape, dt=F32):
        return stack.enter_context(nc.sbuf_tensor(name, [P, *shape], dt))

    sems = {}

    def sem(name):
        if name not in sems:
            sems[name] = ctx.enter_context(nc.semaphore(name))
        return sems[name]

    with ctx:
        raw = sb(ctx, "raw", [RAWS, RAW * UNIT])
        w_hi = sb(ctx, "w_hi", [SPLITS, UNIT], F32R)
        w_lo = sb(ctx, "w_lo", [SPLITS, UNIT], F32R)
        h_hi = sb(ctx, "h_hi", [KD, T], F32R)
        h_lo = sb(ctx, "h_lo", [KD, T], F32R)
        vec = sb(ctx, "vec", [NVEC])
        ident = sb(ctx, "ident", [P])
        ones = sb(ctx, "ones", [P])
        eps = sb(ctx, "eps", [1])
        silu_c = sb(ctx, "silu_c", [KD, 2])
        mod = sb(ctx, "mod", [6 * KD, 2])
        gain = sb(ctx, "gain", [2, KD, 2])
        bound = sb(ctx, "bound", [5, 2 * NC])
        stat = sb(ctx, "stat", [3, 2, NT])
        knorm = sb(ctx, "knorm", [2, 2 * NC])

        mid = ExitStack()
        kspec = sb(mid, "kspec", [2, 2, 2, HW])
        kspec_p = sb(mid, "kspec_p", [2, HW])

        early = ExitStack()
        xin = sb(early, "xin", [NT, D])
        hfull = sb(early, "hfull", [2, T])
        feats = sb(early, "feats", [T])
        w1 = sb(early, "w1", [NHID])
        w2 = sb(early, "w2", [NHID])
        w3 = sb(early, "w3", [2 * HW])
        hid = sb(early, "hid", [2, T])
        arg = sb(early, "arg", [2, T])
        decay = sb(early, "decay", [NT, HW])
        filt = sb(early, "filt", [2, NT, HW])
        ktab = sb(early, "ktab", [2, 2, 2, 2 * P])
        ptab_k = sb(early, "ptab_k", [2, TP])
        absf = sb(early, "absf", [2, HW])
        part = sb(early, "part", [2, HW])
        early.close()

        o_hg = sb(mid, "o_hg", [NC, T])
        x2 = sb(mid, "x2", [NC, CONV])
        u_hy = sb(mid, "u_hy", [NC, T])
        hg = ExitStack()
        eyes = sb(hg, "eyes", [P])
        masks = sb(hg, "masks", [LEVELS, P], U8)
        vtok = sb(hg, "vtok", [NT, HW])
        state0 = sb(hg, "state0", [2, HEADS, P])
        qs = sb(hg, "qs", [T])
        gs = sb(hg, "gs", [2, T])
        QQ = sb(hg, "QQ", [2, T])
        KK = sb(hg, "KK", [2, T])
        TT = [sb(hg, "TT", [2 * T]), sb(hg, "TU", [T])]
        kdiag = sb(hg, "kdiag", [T])
        scratch = sb(hg, "scratch", [T])
        scores = sb(hg, "scores", [T])
        ktok = sb(hg, "ktok", [2, 4, P])
        states = sb(hg, "states", [2, 3, P])
        newst = sb(hg, "newst", [2, P])
        padm = sb(hg, "padm", [2, PAD])
        cv = sb(hg, "cv", [2, CONV])
        hg.close()
        hy = ExitStack()
        utab = sb(hy, "utab", [2, 2, 2, 2 * P])
        itab = sb(hy, "itab", [2, 2, 2, 2 * P])
        ptab = sb(hy, "ptab", [2, 2, TP])
        ut = sb(hy, "ut", [NT, HW])
        U = sb(hy, "U", [2, 2, 2, HW])
        Up = sb(hy, "Up", [2, HW])
        prod = sb(hy, "prod", [2, 2, HW])
        zc = sb(hy, "zc", [CONV])
        sq = sb(hy, "sq", [CONV])
        hy.close()
        mid.close()

        late = ExitStack()
        x1 = sb(late, "x1", [NT, D])
        grow = sb(late, "grow", [2, 2, D])
        fnw = sb(late, "fnw", [D])
        tmpd = sb(late, "tmpd", [HW])
        norm2 = ExitStack()
        xn = sb(norm2, "xn", [NT, D])
        hf2 = sb(norm2, "hf2", [2, T])
        norm2.close()
        a_hi = sb(late, "a_hi", [8, T], F32R)
        a_lo = sb(late, "a_lo", [8, T], F32R)
        padf = sb(late, "padf", [2, 2, PAD])
        cf = sb(late, "cf", [2, CONV])
        actf = sb(late, "actf", [T])
        late.close()

        ps = ctx.enter_context(nc.psum_tensor("ps", [P, 8, 512], F32))

        def v(name, i=0, n=1):
            return vec[:, VEC[name] + i:VEC[name] + i + n]

        def banks(b, n=T, off=0):
            return ap(ps, b * 512 + off, [(1, n)])

        def linker(eng, own):
            count = {}

            def link(ins, name=None):
                name = name or own
                count[name] = count.get(name, 0) + 1
                ins.then_inc(sem(name), 1)
                eng.wait_ge(sem(name), count[name])
            return link

        def arrived(eng, s):
            eng.wait_ge(sem(f"raw_in{s % RAWS}"), 16 * (s // RAWS + 1))

        def unit_free(eng, n):
            name, value = UNIT_LAST[n]
            eng.wait_ge(sem(name), value)

        ada_before = [sum(IS_ADA[:s + 1]) for s in range(NSLOT)]
        units_before = [sum(SLOT_UNITS[i] for i in range(s + 1) if not IS_ADA[i]) for s in range(NSLOT)]
        NH = 2 * len(TILES)

        def half_bank(n):
            return n % 4 if n < NH else 5 + (n - NH) % 3

        def step_at(n):
            return divmod(n - FIRST_STEP, STEPS) if FIRST_STEP <= n < FIRST_STEP + HEADS * STEPS else None

        def x_rows(i):
            return io["x_sample"][0][i * P:(i + 1) * P, :] if i < TS // P else io["x_prompt"][0]

        block = ctx.enter_context(nc.Block())

        @block.sync
        def _(eng):
            def load(dst, src, name):
                eng.dma_start(dst, src).then_inc(sem(name), 16)

            def slot(s):
                if s >= RAWS:
                    o = s - RAWS
                    if IS_ADA[o]:
                        eng.wait_ge(sem("ada_used"), ada_before[o])
                    else:
                        eng.wait_ge(sem("hi_ready"), units_before[o])
                        eng.wait_ge(sem("lo_ready"), units_before[o])
                n = SLOT_UNITS[s] * UNIT
                load(raw[:, s % RAWS, 0:n], io["slots"][s, :, 0:n], f"raw_in{s % RAWS}")

            def store_state(h):
                eng.wait_ge(sem("new_states"), h + 1)
                load(io["new_state"][0, 0].rearrange("d h k w -> h k d w")[h], newst[:, :, :], "stored")

            load(vec[:, :], io["vec"], "ld_vec")
            load(feats[0:NEMB, :], io["feats"], "ld_filt")
            load(w1[0:NEMB, :], io["hy_w1"][0], "ld_filt")
            load(w2[0:NHID, :], io["hy_w2"][0], "ld_filt")
            load(w3[0:NHID, :], io["hy_w3"][0], "ld_filt")
            for s in range(RAWS):
                slot(s)
            load(decay[:, :, :], io["decay"], "ld_decay")
            load(ktab[:, :, :, :, :], io["ktab"], "ld_ktab")
            load(ptab_k[:, :, :], io["ptab"][:, 0], "ld_ktab")
            for i in range(NT):
                load(xin[:, i, :], x_rows(i), f"ld_x{i}")
            load(ident[:, :], io["ident"], "ld_ident")
            for s in range(RAWS, ADA1 + 1):
                slot(s)
            eng.wait_ge(sem("h_split"), KD)
            eng.wait_ge(sem("kspec_ready"), 3)
            load(ap(QQ, 0, [(P, LEVELS), (1, P)]).bitcast(U32), io["masks"], "ld_hg")
            load(eyes[:, :], io["diag"], "ld_hg")
            load(state0[:, :, :, :], io["state_hgrn"][0, 0].rearrange("d h k w -> k d h w"), "ld_hg")
            for s in range(ADA1 + 1, SLOT_ADA2 + 2):
                slot(s)
                if s - SLOT_PROJ in (8, 11, 14):
                    store_state((s - SLOT_PROJ - 8) // 3)
            store_state(HEADS - 1)
            eng.wait_ge(sem("heads_done"), HEADS)
            eng.wait_ge(sem("hy_conv"), 3 * NC)
            eng.wait_ge(sem("stored"), 16 * HEADS)
            load(utab[:, :, :, :, :], io["utab"], "ld_utab")
            load(itab[:, :, :, :, :], io["itab"], "ld_utab")
            load(ptab[:, :, :, :], io["ptab"][:, 1:3], "ld_utab")
            for s in range(SLOT_ADA2 + 2, SLOT_WOUT + 2):
                slot(s)
            eng.wait_ge(sem("merged"), 1)
            for i in range(NT):
                load(x1[:, i, :], x_rows(i), "ld_res")
            load(fnw[:, :], io["final_norm_w"].partition_broadcast(P), "ld_fnw")
            for s in range(SLOT_WOUT + 2, NSLOT):
                slot(s)
            for i in range(NT):
                eng.wait_ge(sem("y_ready"), i + 1)
                dst = io["y_sample"][0][i * P:(i + 1) * P, :] if i < TS // P else io["y_prompt"][0]
                load(dst, x1[:, i, :], "stored")
            eng.wait_ge(sem("stored"), 16 * (NT + HEADS))

        @block.scalar
        def _(eng):
            link = linker(eng, "act_own")
            A = nc.scalar.activation

            def split_hi(n):
                if n >= NU:
                    return
                s, u = UNITS[n]
                arrived(eng, s)
                if n >= SPLITS:
                    unit_free(eng, n - SPLITS)
                A(w_hi[:, n % SPLITS, :], raw[:, s % RAWS, u * UNIT:(u + 1) * UNIT],
                  ACT.Copy).then_inc(sem("hi_ready"), 1)

            def spread(src, pad, half, name):
                if half == 0:
                    A(pad[:, 1:1 + 5 * PADROW].rearrange("p (r c) -> p r c", c=PADROW)[:, :, 0:GRID],
                      src.rearrange("p (r c) -> p r c", c=GRID), ACT.Copy).then_inc(sem(name), 1)
                else:
                    A(pad[:, 1 + 5 * PADROW:1 + PADS].rearrange("p (r c) -> p r c", c=PADROW)[:, :, 0:GRID],
                      src[:, 0:3 * GRID].rearrange("p (r c) -> p r c", c=GRID), ACT.Copy)
                    A(pad[:, 1 + PADS:1 + CONV], src[:, 3 * GRID:HT], ACT.Copy).then_inc(sem(name), 1)

            def row_norm(which, i, x, junk):
                link(A(ap(junk, 0, [(1, D)]), x[:, i, :], ACT.Square, accum_out=stat[:, which, 0, i:i + 1]))
                A(stat[:, which, 1, i:i + 1], stat[:, which, 0, i:i + 1], ACT.Sqrt, scale=1.0 / D,
                  bias=eps[:, :]).then_inc(sem("norm_ready"), 1)

            def modulate(which, k):
                buf, sh, b = (hfull, hf2)[which], 3 * KD * which + k, 2 * (k % 2)
                eng.wait_ge(sem("h_turned"), KD * which + k + 1)
                if k >= 2:
                    eng.wait_ge(sem("h_split"), KD * which + k - 1)
                A(buf[:, k % 2, 0:TS], ps[:, b, :], ACT.Identity,
                  scale=gain[:, which, k, 0:1], bias=mod[:, sh, 0:1])
                A(buf[:, k % 2, TS:T], ps[:, b + 1, 0:TP], ACT.Identity,
                  scale=gain[:, which, k, 1:2], bias=mod[:, sh, 1:2]).then_inc(sem("h_full"), 1)

            eng.wait_ge(sem("ones_ready"), 2)
            eng.wait_ge(sem("ld_vec"), 16)
            A(silu_c[:, :, 0], v("c", 0, KD), ACT.Silu)
            A(silu_c[:, :, 1], v("c_ctx", 0, KD), ACT.Silu).then_inc(sem("silu_c"), 1)
            eng.wait_ge(sem("bound_in"), 1)
            A(bound[:, 1, :], bound[:, 0, :], ACT.Exp).then_inc(sem("bound_exp"), 1)
            for i in range(2):
                eng.wait_ge(sem("arg_ready"), i + 1)
                A(hid[0:NHID, i, :], arg[0:NHID, 0, :], ACT.Sin).then_inc(sem("hid_ready"), 1)
            for i in range(NT):
                eng.wait_ge(sem("taps_ready"), i + 1)
                if i:
                    eng.wait_ge(sem("abs_used"), i)
                A(absf[:, :, :], filt[:, :, i, :], ACT.Abs).then_inc(sem("abs_ready"), 1)
            for i in range(NT):
                eng.wait_ge(sem(f"ld_x{i}"), 16)
                row_norm(0, i, xin, hfull)
            for m in range(2):
                eng.wait_ge(sem("kdft"), m + 1)
                if m:
                    eng.wait_ge(sem("kspec_ready"), m)
                for cs in range(2):
                    A(part[:, cs, :], ps[:, 4 * m + 2 * cs + 1, :], ACT.Copy).then_inc(sem("kodd"), 1)
            split_hi(0)
            split_hi(1)
            eng.wait_ge(sem("gain_ready"), 1)
            for k in range(KD):
                modulate(0, k)
            for n in range(2 * IV):
                split_hi(n + 2)
            eng.wait_ge(sem("v_bank"), NT)
            eng.wait_ge(sem("kspec_ready"), 3)
            for i in range(NT):
                A(vtok[:, i, :], ps[:, i, :], ACT.Copy).then_inc(sem("v_ready"), 1)

            def step(h, j):
                if j == KTURN:
                    eng.wait_ge(sem("head_steps"), h * STEPS + KTURN + 1)
                    A(ktok[:, :, :, :], banks(4, 2 * 512), ACT.Copy).then_inc(sem("ktok_ready"), 1)
                if j == OUT:
                    eng.wait_ge(sem("head_steps"), h * STEPS + OUT + 1)
                    A(scratch[:, :], banks(6), ACT.Square).then_inc(sem("osq_ready"), 1)
                if j == NORM:
                    eng.wait_ge(sem("head_steps"), h * STEPS + NORM + 1)
                    A(scratch[:, :], banks(4), ACT.Sqrt, scale=1.0 / P, bias=eps[:, :]).then_inc(sem("rms_ready"), 1)

            for n in range(NH):
                kind, i = TILES[n // 2]
                half = n % 2
                c0 = half * HT
                src = ps[:, half_bank(n), 0:HT]
                if half == 0 and n < NH - 4:
                    split_hi(UNIT_TILE + n // 2 + 2)
                eng.wait_ge(sem("half_made"), n + 1)
                if kind == "q":
                    if i:
                        eng.wait_ge(sem("head_steps"), (i - 1) * STEPS + DIAG + 1)
                    A(qs[:, c0:c0 + HT], src, ACT.Silu).then_inc(sem("half_free"), 1)
                elif kind == "g":
                    if i >= 2:
                        eng.wait_ge(sem("heads_done"), i - 1)
                    A(gs[:, i % 2, c0:c0 + HT], src, ACT.Silu).then_inc(sem("half_free"), 1)
                elif kind in ("ff", "fb"):
                    d = int(kind == "ff")
                    if i:
                        eng.wait_ge(sem("qk_next"), (i - 1) * 8 + 8)
                        eng.wait_ge(sem("head_steps"), (i - 1) * STEPS + KTURN + 1)
                    A(TT[0][:, d * T + c0:d * T + c0 + HT], src, ACT.Sigmoid)
                    A(KK[:, 1 - d, c0:c0 + HT], src, ACT.Sigmoid, scale=-1.0).then_inc(sem("half_free"), 1)
                else:
                    if i < 2:
                        eng.wait_ge(sem("pad_zero"), 1)
                    else:
                        eng.wait_ge(sem("hy_conv"), i - 1)
                    spread(src, padm[:, i % 2, :], half, "half_free")
                if step_at(n):
                    step(*step_at(n))
            for n in range(NH, FIRST_STEP + HEADS * STEPS):
                step(*step_at(n))

            eng.wait_ge(sem("heads_done"), HEADS)
            for i in range(NT):
                eng.wait_ge(sem("u_turned"), i + 1)
                A(ut[:, i, :], ps[:, i, :], ACT.Copy).then_inc(sem("ut_ready"), 1)
            for m in range(2):
                eng.wait_ge(sem("udft"), m + 1)
                if m:
                    eng.wait_ge(sem("uspec_ready"), m)
                for cs in range(2):
                    A(prod[:, cs, 0, :], ps[:, 4 * m + 2 * cs + 1, :], ACT.Copy).then_inc(sem("uodd"), 1)
            eng.wait_ge(sem("udft"), 3)
            A(Up[:, :, :], banks(0, 2 * 512), ACT.Copy).then_inc(sem("up_ready"), 1)
            split_hi(UNIT_WOUT)
            split_hi(UNIT_WOUT + 1)
            for c in range(NC):
                b = 2 * (c % 2)
                eng.wait_ge(sem("z_made"), c + 1)
                if c:
                    eng.wait_ge(sem("yhy_ready"), c)
                else:
                    eng.wait_ge(sem("zc_zero"), 1)
                A(ap(zc, 0, [(1, 2), (PADROW, ROWS), (2, GRID // 2)]),
                  ps[:, b, :].rearrange("p (e r c) -> p e r c", e=2, r=ROWS), ACT.Copy, scale=knorm[:, 1, c:c + 1])
                A(zc[:, PADS:CONV], ps[:, b + 1, 0:TP], ACT.Copy,
                  scale=knorm[:, 1, NC + c:NC + c + 1]).then_inc(sem("z_ready"), 1)
                eng.wait_ge(sem("yhy_ready"), c + 1)
                if c:
                    eng.wait_ge(sem("ysq_used"), c)
                A(sq[:, :], x2[:, c, :], ACT.Square).then_inc(sem("ysq_ready"), 1)
            eng.wait_ge(sem("ysq_used"), NC)
            A(ap(sq, 0, [(CONV // 2, 2), (1, CONV // 2)]), ap(ps, 4 * 512, [(512, 2), (1, CONV // 2)]), ACT.Sqrt,
              scale=1.0 / HW, bias=eps[:, :]).then_inc(sem("rms_ready"), 1)
            eng.wait_ge(sem("merged"), 1)
            for r in range(8):
                eng.wait_ge(sem("row_made"), r + 1)
                A(grow[:, r // 4, (r // 2) % 2, (r % 2) * 512:(r % 2 + 1) * 512], ps[:, 5 + r % 3, :],
                  ACT.Copy).then_inc(sem("row_ready"), 1)
            for n in range(2 * WOUT):
                split_hi(UNIT_WOUT + n + 2)
            for i in range(NT):
                eng.wait_ge(sem("x1_ready"), NT + i + 1)
                row_norm(1, i, x1, hf2)
            eng.wait_ge(sem("gain_ready"), 2)
            for k in range(KD):
                modulate(1, k)
            eng.wait_ge(sem("padf_zero"), 1)
            unit, t = UNIT_FFN, 0
            for r, (f0, nf) in enumerate(ROUNDS):
                for f in range(nf):
                    for gv in range(2):
                        split_hi(unit + 2)
                        unit += 1
                        for half in range(2):
                            n = NH + 4 * t + 2 * gv + half
                            eng.wait_ge(sem("half_made"), n + 1)
                            if t >= 2 and half == 0:
                                eng.wait_ge(sem("fconv"), 2 * (t - 2) + gv + 1)
                            spread(ps[:, half_bank(n), 0:HT], padf[:, t % 2, gv, :], half, "half_free")
                        if gv == 0:
                            eng.wait_ge(sem("fconv"), 2 * t + 1)
                            A(cf[:, 0, :], cf[:, 0, :], ACT.Silu).then_inc(sem("silu_done"), 1)
                    eng.wait_ge(sem("act_ready"), t + 1)
                    if r and f == 0:
                        eng.wait_ge(sem("down_made"), 2 * r * NT)
                    A(a_hi[:, f, :], actf[:, :], ACT.Copy).then_inc(sem("ahi_ready"), 1)
                    t += 1
                for k in range(nf):
                    split_hi(unit + 2)
                    unit += 1
            for i in range(NT):
                eng.wait_ge(sem("down_added"), 5 * NT + i + 1)
                row_norm(2, i, x1, cf)

        @block.vector
        def _(eng):
            link = linker(eng, "dve_own")
            V = nc.vector

            def split_lo(n):
                if n >= NU:
                    return
                s, u = UNITS[n]
                eng.wait_ge(sem("hi_ready"), n + 1)
                if n >= SPLITS:
                    unit_free(eng, n - SPLITS)
                V.tensor_tensor(w_lo[:, n % SPLITS, :], raw[:, s % RAWS, u * UNIT:(u + 1) * UNIT],
                                w_hi[:, n % SPLITS, :].bitcast(F32), ALU.subtract).then_inc(sem("lo_ready"), 1)

            def split_h(which, k):
                buf = (hfull, hf2)[which][:, k % 2, :]
                eng.wait_ge(sem("h_full"), KD * which + k + 1)
                link(V.tensor_copy(h_hi[:, k, :], buf))
                link(V.tensor_tensor(h_lo[:, k, :], buf, h_hi[:, k, :].bitcast(F32), ALU.subtract), "h_split")

            def conv(pad, out, taps, name=None):
                link(V.tensor_scalar(out, pad[:, 1:1 + CONV], taps[1], None, ALU.mult))
                link(V.scalar_tensor_tensor(out=out, in0=pad[:, 0:CONV], scalar=taps[0], in1=out,
                                            op0=ALU.mult, op1=ALU.add))
                link(V.scalar_tensor_tensor(out=out, in0=pad[:, 2:2 + CONV], scalar=taps[2], in1=out,
                                            op0=ALU.mult, op1=ALU.add), name)

            V.memset(ones[:, :], 1.0).then_inc(sem("ones_ready"), 1)
            V.memset(eps[:, :], EPS).then_inc(sem("ones_ready"), 1)
            eng.wait_ge(sem("ld_vec"), 16)
            lb = v("lb_f", 0, 2 * NC)
            link(V.tensor_tensor(bound[:, 0, :], lb, lb, ALU.subtract), "bound_in")
            eng.wait_ge(sem("bound_exp"), 1)
            link(V.reciprocal(bound[:, 2, :], bound[:, 1, :]))
            link(V.tensor_tensor(bound[:, 2, :], bound[:, 1, :], bound[:, 2, :], ALU.mult))
            link(V.tensor_tensor(bound[:, 3, :], bound[:, 2, :], bound[:, 2, :], ALU.subtract))
            link(V.tensor_scalar(bound[:, 4, :], bound[:, 3, :], -1.0, 1.0, ALU.mult, ALU.add))

            two_pi = 2.0 * math.pi
            c1 = 6.28125
            c2 = float(np.float32(two_pi - c1))
            c3 = two_pi - c1 - c2
            a, q = arg[0:NHID, 0, :], arg[0:NHID, 1, :]
            for i in range(2):
                eng.wait_ge(sem("hid_made"), i + 1)
                if i:
                    eng.wait_ge(sem("hid_ready"), i)
                link(V.tensor_scalar(a, ap(ps, 2 * i * 512, [(1, T)])[0:NHID, :], v(f"b{i + 1}")[0:NHID, :],
                                     v(f"fr{i + 1}")[0:NHID, :], ALU.add, ALU.mult))
                link(V.tensor_scalar(q, a, 1.0 / two_pi, 12582912.0, ALU.mult, ALU.add))
                link(V.tensor_scalar(q, q, 12582912.0, None, ALU.subtract))
                for cc in (c1, c2, c3):
                    link(V.scalar_tensor_tensor(out=a, in0=q, scalar=-cc, in1=a, op0=ALU.mult, op1=ALU.add))
                link(V.tensor_scalar(a, a, -3.1415925, 3.1415925, ALU.max, ALU.min), "arg_ready")
            eng.wait_ge(sem("ld_decay"), 16)
            for i in range(NT):
                eng.wait_ge(sem("taps_made"), i + 1)
                b = 4 + 2 * (i % 2)
                link(V.tensor_tensor(filt[:, :, i, :], ps[:, b:b + 2, :],
                                     ap(decay, i * HW, [(0, 2), (1, HW)]), ALU.mult))
                if i in (0, NT - 1):
                    link(V.memset(filt[0:1, 1, i, :], 0.0))
                eng.sem_inc(sem("taps_ready"), 1)
            for i in range(NT):
                eng.wait_ge(sem("abs_ready"), i + 1)
                link(V.tensor_tensor(decay[:, i, :], filt[:, 0, i, :], filt[:, 1, i, :], ALU.subtract))
                link(V.tensor_tensor(filt[:, 0, i, :], filt[:, 0, i, :], filt[:, 1, i, :], ALU.add), "sides_ready")
            eng.wait_ge(sem("abs_used"), NT)
            link(V.tensor_reduce(knorm[:, 0, 0:NC], ap(ps, 2 * 512, [(1, NC), (NC, 8)]), mybir.AxisListType.X, ALU.add))
            link(V.tensor_reduce(knorm[:, 0, NC:2 * NC], ap(ps, 2 * 512 + 8 * NC, [(1, NC), (NC, 2)]), mybir.AxisListType.X, ALU.add))
            link(V.tensor_scalar(knorm[:, 0, :], knorm[:, 0, :], EPS, None, ALU.add))
            link(V.reciprocal(knorm[:, 1, :], knorm[:, 0, :]), "knorm_ready")
            for i in range(NT):
                eng.wait_ge(sem("norm_ready"), i + 1)
                link(V.reciprocal(stat[:, 0, 1, i:i + 1], stat[:, 0, 1, i:i + 1]))
                link(V.tensor_scalar(xin[:, i, :], xin[:, i, :], stat[:, 0, 1, i:i + 1], None, ALU.mult), "x_scaled")
            for m in range(2):
                eng.wait_ge(sem("kodd"), 2 * m + 2)
                link(V.tensor_tensor(kspec[:, m, 0, 0, :], ps[:, 4 * m, :], part[:, 0, :], ALU.add))
                link(V.tensor_tensor(kspec[:, m, 1, 0, :], ps[:, 4 * m, :], part[:, 0, :], ALU.subtract))
                link(V.tensor_tensor(kspec[:, m, 0, 1, :], ps[:, 4 * m + 2, :], part[:, 1, :], ALU.add))
                link(V.tensor_tensor(kspec[:, m, 1, 1, :], part[:, 1, :], ps[:, 4 * m + 2, :], ALU.subtract), "kspec_ready")
            eng.wait_ge(sem("kdft"), 3)
            link(V.tensor_copy(kspec_p[:, :, :], ps[:, 0:2, :]), "kspec_ready")
            eng.wait_ge(sem("ada_used"), ADA1)
            link(V.tensor_tensor(mod[:, 0:2 * KD, :], ap(ps, 7 * 512, [(2, 2 * KD), (1, 2)]),
                                 ap(vec, VEC["ada_b"], [(1, 2 * KD), (0, 2)]), ALU.add))
            link(V.scalar_tensor_tensor(out=gain[:, 0, :, :], in0=mod[:, KD:2 * KD, :], scalar=1.0,
                                        in1=ap(vec, VEC["norm1"], [(1, KD), (0, 2)]), op0=ALU.add, op1=ALU.mult), "gain_ready")
            split_lo(0)
            split_lo(1)
            for k in range(KD):
                split_h(0, k)
            for n in range(2 * IV):
                split_lo(n + 2)

            def start_head(h):
                if h:
                    eng.wait_ge(sem("head_steps"), (h - 1) * STEPS + OUT + 1)
                n = 0
                for d in range(2):
                    t0 = TT[0][:, (1 - d) * T:(2 - d) * T]
                    fb = NC * d + h
                    link(V.tensor_scalar(t0, t0, bound[:, 4, fb:fb + 1], bound[:, 3, fb:fb + 1], ALU.mult, ALU.add))
                    link(V.tensor_scalar(KK[:, d, :], KK[:, d, :], bound[:, 4, fb:fb + 1], None, ALU.mult))
                link(V.scalar_tensor_tensor(out=QQ[:, :, :], in0=ap(qs, 0, [(0, 2), (1, T)]), scalar=SCALE,
                                            in1=ap(TT[0], 0, [(T, 2), (1, T)]), op0=ALU.mult, op1=ALU.mult))
                link(V.tensor_tensor(kdiag[:, :], KK[:, 0, :], KK[:, 1, :], ALU.add), "qk_next")

            def take_level(h, j):
                eng.wait_ge(sem("head_steps"), h * STEPS + j + 1)
                if j == DIAG:
                    link(V.tensor_tensor(scores[:, :], banks(4), ap(eyes, 0, [(0, NT), (1, P)]), ALU.mult), "scores_taken")
                    return
                l = j - LEVEL0
                link(V.copy_predicated(scores[:, :], ap(masks, l * P, [(0, NT), (1, P)]), banks(4)), "scores_taken")
                s = 1 << l
                nb, n = T // (2 * s), T // s
                t, t2 = TT[l % 2], TT[(l + 1) % 2]
                both = [(2 * s, nb), (T + s, 2), (1, s)]
                link(V.tensor_tensor(ap(QQ, 0, both), ap(QQ, 0, both), ap(t, 1, [(2, nb), (n - 1, 2), (0, s)]), ALU.mult))
                link(V.tensor_tensor(ap(KK, 0, both), ap(KK, 0, both), ap(t, n + 1, [(2, nb), (-n - 1, 2), (0, s)]), ALU.mult))
                link(V.tensor_tensor(ap(t2, 0, [(nb, 2), (1, nb)]), ap(t, 0, [(n, 2), (2, nb)]),
                                     ap(t, 1, [(n, 2), (2, nb)]), ALU.mult), "qk_next")

            def make_states(h):
                eng.wait_ge(sem("head_steps"), h * STEPS + KV + 1)
                t7 = TT[LEVELS % 2]
                for d in range(2):
                    for n in range(3):
                        c = n if d == 0 else 3 - n
                        at = (0, 1, 2)[n] if d == 0 else 2 - n
                        idx = c if d == 0 else c - 1
                        prev = state0[:, d, h, :] if n == 0 else states[:, d, at - 1 if d == 0 else at + 1, :]
                        col = (NT + c) if d == 0 else c
                        link(V.scalar_tensor_tensor(out=states[:, d, at, :], in0=prev, scalar=t7[:, col:col + 1],
                                                    in1=ps[:, 4 + d, idx * P:(idx + 1) * P], op0=ALU.mult, op1=ALU.add))
                if h:
                    eng.wait_ge(sem("stored"), 16 * h)
                link(V.tensor_copy(newst[:, :, :], ap(ps, 4 * 512 + 3 * P, [(512, 2), (1, P)])), "new_states")

            def finish_head(h):
                eng.wait_ge(sem("rms_ready"), h + 1)
                link(V.reciprocal(scratch[:, :], scratch[:, :]))
                link(V.scalar_tensor_tensor(out=o_hg[:, h, :], in0=banks(6), scalar=v("hg_norm", h),
                                            in1=scratch[:, :], op0=ALU.mult, op1=ALU.mult))
                link(V.tensor_tensor(o_hg[:, h, :], o_hg[:, h, :], gs[:, h % 2, :], ALU.mult), "heads_done")

            def step(h, j):
                if j < KTURN:
                    take_level(h, j)
                elif j == KV:
                    make_states(h)
                elif j == NORM:
                    finish_head(h)

            eng.wait_ge(sem("v_bank"), NT)
            eng.wait_ge(sem("ld_hg"), 48)
            link(V.tensor_copy(masks[:, :, :], ap(QQ, 0, [(P, LEVELS), (1, P)]).bitcast(U32)))
            for i in range(2):
                link(V.memset(padm[:, i, :], 0.0), "pad_zero" if i else None)
            for n in range(NH):
                kind, i = TILES[n // 2]
                if n % 2 == 0 and n < NH - 4:
                    split_lo(UNIT_TILE + n // 2 + 2)
                if n % 2:
                    eng.wait_ge(sem("half_free"), n + 1)
                    if kind == "hy":
                        c, what = divmod(i, 3)
                        taps = [v("hy_conv", (w * 3 + what) * NC + c) for w in range(3)]
                        out = (cv[:, 0, :], cv[:, 1, :], x2[:, c, :])[what]
                        conv(padm[:, i % 2, :], out, taps, "hy_conv")
                        if what == 1:
                            link(V.tensor_tensor(rows64(u_hy[:, c, 0:TS]), grid(cv, 0), grid(cv, CONV), ALU.mult))
                            link(V.tensor_tensor(u_hy[:, c, TS:T], cv[:, 0, PADS:CONV], cv[:, 1, PADS:CONV], ALU.mult), "u_ready")
                if step_at(n):
                    step(*step_at(n))
                if kind == "fb" and n % 2:
                    start_head(i)
            for n in range(NH, FIRST_STEP + HEADS * STEPS):
                step(*step_at(n))

            eng.wait_ge(sem("half_made"), NH)
            link(V.tensor_copy(h_hi[:, 0:NC, :], o_hg[:, :, :]))
            link(V.tensor_tensor(h_lo[:, 0:NC, :], o_hg[:, :, :], h_hi[:, 0:NC, :].bitcast(F32), ALU.subtract))
            eng.wait_ge(sem("ada_used"), ADA1 + ADA2)
            link(V.tensor_tensor(mod[:, 2 * KD:6 * KD, :], ap(ps, 3 * 512 + 4 * KD, [(2, 4 * KD), (1, 2)]),
                                 ap(vec, VEC["ada_b"] + 2 * KD, [(1, 4 * KD), (0, 2)]), ALU.add))
            link(V.scalar_tensor_tensor(out=gain[:, 1, :, :], in0=mod[:, 4 * KD:5 * KD, :], scalar=1.0,
                                        in1=ap(vec, VEC["norm2"], [(1, KD), (0, 2)]), op0=ALU.add, op1=ALU.mult), "gain_ready")

            link(V.memset(zc[:, :], 0.0), "zc_zero")
            for m in range(2):
                eng.wait_ge(sem("uodd"), 2 * m + 2)
                c0, s0 = prod[:, 0, 0, :], prod[:, 1, 0, :]
                link(V.tensor_tensor(U[:, m, 0, 0, :], ps[:, 4 * m, :], c0, ALU.add))
                link(V.tensor_tensor(U[:, m, 1, 1, :], ps[:, 4 * m, :], c0, ALU.subtract))
                link(V.tensor_tensor(U[:, m, 0, 1, :], ps[:, 4 * m + 2, :], s0, ALU.add))
                link(V.tensor_tensor(U[:, m, 1, 0, :], ps[:, 4 * m + 2, :], s0, ALU.subtract), "uspec_ready")
            for m in range(2):
                C, S = U[:, m, :, 0, :], U[:, m, :, 1, :]
                Kr, Ks = kspec[:, m, :, 0, :], kspec[:, m, :, 1, :]
                r, t = prod[:, 0, :, :], prod[:, 1, :, :]
                link(V.tensor_tensor(r, C, Kr, ALU.mult))
                link(V.tensor_tensor(t, S, Ks, ALU.mult))
                link(V.tensor_tensor(r, r, t, ALU.subtract))
                link(V.tensor_tensor(t, C, Ks, ALU.mult))
                link(V.tensor_tensor(S, S, Kr, ALU.mult))
                link(V.tensor_tensor(S, S, t, ALU.add))
                link(V.tensor_tensor(U[:, m, 0, 0, :], r[:, 0, :], U[:, m, 1, 1, :], ALU.add))
                link(V.tensor_tensor(U[:, m, 1, 0, :], r[:, 1, :], U[:, m, 0, 1, :], ALU.add))
                link(V.tensor_tensor(U[:, m, 1, 1, :], r[:, 0, :], U[:, m, 1, 1, :], ALU.subtract))
                link(V.tensor_tensor(U[:, m, 0, 1, :], U[:, m, 0, 1, :], r[:, 1, :], ALU.subtract), "zspec_ready")
            eng.wait_ge(sem("up_ready"), 1)
            r, t = prod[:, 0, 0, :], prod[:, 1, 0, :]
            link(V.tensor_tensor(r, Up[:, 0, :], kspec_p[:, 0, :], ALU.mult))
            link(V.tensor_tensor(t, Up[:, 1, :], kspec_p[:, 1, :], ALU.mult))
            link(V.tensor_tensor(r, r, t, ALU.subtract))
            link(V.tensor_tensor(t, Up[:, 0, :], kspec_p[:, 1, :], ALU.mult))
            link(V.tensor_tensor(Up[:, 1, :], Up[:, 1, :], kspec_p[:, 0, :], ALU.mult))
            link(V.tensor_tensor(Up[:, 1, :], Up[:, 1, :], t, ALU.add))
            link(V.tensor_copy(Up[:, 0, :], r), "zspec_ready")
            split_lo(UNIT_WOUT)
            split_lo(UNIT_WOUT + 1)
            for c in range(NC):
                eng.wait_ge(sem("z_ready"), c + 1)
                link(V.scalar_tensor_tensor(out=grid(zc, 0), in0=rows64(u_hy[:, c, 0:TS]), scalar=v("hy_d", c),
                                            in1=grid(zc, 0), op0=ALU.mult, op1=ALU.add))
                link(V.scalar_tensor_tensor(out=zc[:, PADS:CONV], in0=u_hy[:, c, TS:T], scalar=v("hy_d", c),
                                            in1=zc[:, PADS:CONV], op0=ALU.mult, op1=ALU.add))
                link(V.tensor_tensor(x2[:, c, :], x2[:, c, :], zc[:, :], ALU.mult), "yhy_ready")
            eng.wait_ge(sem("rms_ready"), HEADS + 1)
            link(V.reciprocal(sq[:, :], sq[:, :]))
            for c in range(NC):
                link(V.scalar_tensor_tensor(out=x2[:, c, :], in0=x2[:, c, :], scalar=v("hy_norm", c),
                                            in1=sq[:, :], op0=ALU.mult, op1=ALU.mult))
            for lo in range(2):
                for dst, src in ((ap((h_hi, h_lo)[lo], NC * T, [(T, NC), (GRID, ROWS), (1, GRID)]),
                                  ap(x2, 0, [(CONV, NC), (PADROW, ROWS), (1, GRID)])),
                                 (ap((h_hi, h_lo)[lo], NC * T + TS, [(T, NC), (1, TP)]),
                                  ap(x2, PADS, [(CONV, NC), (1, TP)]))):
                    last = "merged" if lo and len(src.shape) == 3 else None
                    if not lo:
                        link(V.tensor_copy(dst, src))
                    else:
                        hi = bass.AP(tensor=h_hi[:].tensor, offset=dst.offset, ap=dst.ap).bitcast(F32)
                        link(V.tensor_tensor(dst, src, hi, ALU.subtract), last)

            def add(which, i, n, name_taken, name_done):
                s = int(i == NT - 1)
                link(V.tensor_tensor(tmpd[:, :], ps[:, i, :], grow[:, which, s, n * HW:(n + 1) * HW], ALU.mult), name_taken)
                xs = x1[:, i, n * HW:(n + 1) * HW]
                link(V.tensor_tensor(xs, xs, tmpd[:, :], ALU.add), name_done)

            split_lo(UNIT_WOUT + 2)
            for n in range(2):
                for k in range(WOUT):
                    if n or k:
                        split_lo(UNIT_WOUT + WOUT * n + k + 2)
                if n == 0:
                    eng.wait_ge(sem("ld_res"), 16 * NT)
                    eng.wait_ge(sem("row_ready"), 8)
                for i in range(NT):
                    eng.wait_ge(sem("mixed"), NT * n + i + 1)
                    add(0, i, n, "mixed_taken", "x1_ready")
            for i in range(NT):
                eng.wait_ge(sem("norm_ready"), NT + i + 1)
                link(V.reciprocal(stat[:, 1, 1, i:i + 1], stat[:, 1, 1, i:i + 1]))
                link(V.tensor_scalar(xn[:, i, :], x1[:, i, :], stat[:, 1, 1, i:i + 1], None, ALU.mult), "x_scaled")
            for k in range(KD):
                split_h(1, k)
            for i in range(2):
                for gv in range(2):
                    link(V.memset(padf[:, i, gv, :], 0.0), "padf_zero" if i and gv else None)
            unit, t = UNIT_FFN, 0
            for r, (f0, nf) in enumerate(ROUNDS):
                for f in range(nf):
                    for gv in range(2):
                        split_lo(unit + 2)
                        unit += 1
                        eng.wait_ge(sem("half_free"), NH + 4 * t + 2 * gv + 2)
                        taps = [v("ffn_conv", (w * 2 + gv) * NF + f0 + f) for w in range(3)]
                        conv(padf[:, t % 2, gv, :], cf[:, gv, :], taps, "fconv")
                    eng.wait_ge(sem("silu_done"), t + 1)
                    link(V.tensor_tensor(rows64(actf[:, 0:TS]), grid(cf, 0), grid(cf, CONV), ALU.mult))
                    link(V.tensor_tensor(actf[:, TS:T], cf[:, 0, PADS:CONV], cf[:, 1, PADS:CONV], ALU.mult), "act_ready")
                    eng.wait_ge(sem("ahi_ready"), t + 1)
                    link(V.tensor_tensor(a_lo[:, f, :], actf[:, :], a_hi[:, f, :].bitcast(F32), ALU.subtract), "a_ready")
                    t += 1
                for n in range(2):
                    for k in range(nf // 2):
                        split_lo(unit + 2)
                        unit += 1
                    for i in range(NT):
                        eng.wait_ge(sem("down_made"), (2 * r + n) * NT + i + 1)
                        add(1, i, n, "down_taken", "down_added")
            eng.wait_ge(sem("ld_fnw"), 16)
            for i in range(NT):
                eng.wait_ge(sem("norm_ready"), 2 * NT + i + 1)
                link(V.reciprocal(stat[:, 2, 1, i:i + 1], stat[:, 2, 1, i:i + 1]))
                link(V.scalar_tensor_tensor(out=x1[:, i, :], in0=x1[:, i, :], scalar=stat[:, 2, 1, i:i + 1],
                                            in1=fnw[:, :], op0=ALU.mult, op1=ALU.mult), "y_ready")

        @block.tensor
        def _(eng):
            mm = nc.tensor.matmul

            def split_product(out, lhs, rhs, first, last):
                mm(out, lhs[0], rhs[0], start=first, stop=False)
                mm(out, lhs[0], rhs[1], start=False, stop=False)
                return mm(out, lhs[1], rhs[0], start=False, stop=last)

            def unit_ready(n):
                eng.wait_ge(sem("hi_ready"), n + 1)
                eng.wait_ge(sem("lo_ready"), n + 1)
                return w_hi[:, n % SPLITS, :], w_lo[:, n % SPLITS, :]

            eng.wait_ge(sem("ld_filt"), 64)
            mm(ps[0:NHID, 0, :], w1[0:NEMB, :], feats[0:NEMB, 0:TS], start=True, stop=True)
            mm(ps[0:NHID, 1, 0:TP], w1[0:NEMB, :], feats[0:NEMB, TS:T], start=True, stop=True).then_inc(sem("hid_made"), 1)
            eng.wait_ge(sem("hid_ready"), 1)
            mm(ps[0:NHID, 2, :], w2[0:NHID, :], hid[0:NHID, 0, 0:TS], start=True, stop=True)
            mm(ps[0:NHID, 3, 0:TP], w2[0:NHID, :], hid[0:NHID, 0, TS:T], start=True, stop=True).then_inc(sem("hid_made"), 1)
            eng.wait_ge(sem("hid_ready"), 2)
            eng.wait_ge(sem("ones_ready"), 2)

            def tap_sizes(i):
                eng.wait_ge(sem("abs_ready"), i + 1)
                for d in range(2):
                    for c in range(NC):
                        last = mm(ps[:, 2, (2 * i + d) * NC + c:(2 * i + d) * NC + c + 1], absf[:, d, c * P:(c + 1) * P],
                                  ones[:, 0:1], start=True, stop=True)
                last.then_inc(sem("abs_used"), 1)

            for i in range(NT):
                if i >= 2:
                    eng.wait_ge(sem("taps_ready"), i - 1)
                for d in range(2):
                    last = mm(ps[:, 4 + 2 * (i % 2) + d, :], hid[0:NHID, 1, i * P:(i + 1) * P],
                              w3[0:NHID, d * HW:(d + 1) * HW], start=True, stop=True)
                last.then_inc(sem("taps_made"), 1)
                if i:
                    tap_sizes(i - 1)
            tap_sizes(NT - 1)

            def ada(lo, hi, bank, sync=None):
                for s in range(lo, hi):
                    arrived(eng, s)
                    j = s - (0 if s < ADA1 else SLOT_ADA2 - ADA1)
                    for f in range(2):
                        col = 2 * (2 * j + f)
                        for k in range(KD):
                            last = mm(ps[:, bank, col:col + 2], raw[:, s % RAWS, k * 256 + f * P:k * 256 + (f + 1) * P],
                                      silu_c[:, k, :], start=(k == 0), stop=(k == KD - 1))
                    last.then_inc(sem("ada_used"), 1)

            eng.wait_ge(sem("ld_ktab"), 32)
            eng.wait_ge(sem("sides_ready"), NT)
            eng.wait_ge(sem("knorm_ready"), 1)
            for m in range(2):
                for cs in range(2):
                    src = (filt[:, 0], decay)[cs]
                    for e in range(2):
                        for k in range(2):
                            i = 2 * e + k
                            rhs = filt[:, 0, i, :] if cs == 0 else decay[:, i, :]
                            last = mm(ps[:, 4 * m + 2 * cs + e, :], ktab[:, cs, e, k, m * P:(m + 1) * P], rhs,
                                      start=(k == 0), stop=(k == 1))
                last.then_inc(sem("kdft"), 1)
            eng.wait_ge(sem("kspec_ready"), 1)
            mm(ps[:, 0, :], ptab_k[:, 0, :], filt[:, 0, NT - 1, :], start=True, stop=True)
            mm(ps[:, 1, :], ptab_k[:, 1, :], decay[:, NT - 1, :], start=True, stop=True).then_inc(sem("kdft"), 1)

            eng.wait_ge(sem("silu_c"), 1)
            eng.wait_ge(sem("kspec_ready"), 3)
            ada(0, ADA1, 7)

            def turn(src, which):
                for k in range(KD):
                    if k >= 2:
                        eng.wait_ge(sem("h_full"), KD * which + k - 1)
                    b = 2 * (k % 2)
                    for i in range(NT):
                        if k == 0:
                            eng.wait_ge(sem("x_scaled"), NT * which + i + 1)
                        dst = ps[:, b, i * P:(i + 1) * P] if i < 4 else ps[:, b + 1, 0:P]
                        last = nc.tensor.transpose(dst, src[:, i, k * P:(k + 1) * P], ident[:, :])
                    last.then_inc(sem("h_turned"), 1)

            def token_major(unit0, pairs, lhs, name, taken, done=None):
                for p in range(pairs):
                    hi, lo = unit_ready(unit0 + p)
                    for i in range(NT):
                        if p == 0 and taken is not None:
                            eng.wait_ge(sem(taken[0]), taken[1] + i + 1)
                        for kk in range(2):
                            k = 2 * p + kk
                            last = split_product(ps[:, i, :], [x[:, k, i * P:(i + 1) * P] for x in lhs],
                                                 [x[:, kk * HW:(kk + 1) * HW] for x in (hi, lo)],
                                                 k == 0, k == 2 * pairs - 1)
                        if p == pairs - 1:
                            last.then_inc(sem(name), 1)
                    if p < pairs - 1:
                        last.then_inc(sem("unit_done"), 1)

            eng.wait_ge(sem("ld_ident"), 16)
            turn(xin, 0)
            eng.wait_ge(sem("h_split"), KD)
            token_major(0, 2 * IV, (h_hi, h_lo), "v_bank", None)

            def chunk(c):
                return ps[:, 4, c * P:(c + 1) * P] if c < 4 else ps[:, 5, 0:P]

            def step(h, j):
                if j == DIAG:
                    eng.wait_ge(sem("qk_next"), 8 * h + 1)
                    if h:
                        eng.wait_ge(sem("heads_done"), h)
                    for c in range(NT):
                        last = mm(chunk(c), kdiag[:, c * P:(c + 1) * P], qs[:, c * P:(c + 1) * P], start=True, stop=True)
                elif j < KTURN:
                    l = j - LEVEL0
                    s = 1 << l
                    eng.wait_ge(sem("qk_next"), 8 * h + 1 + l)
                    eng.wait_ge(sem("scores_taken"), 8 * h + j)
                    for c in range(NT):
                        b, c0 = (4, c * P) if c < 4 else (5, 0)
                        for d in range(2):
                            half = (1 - d) * s
                            dims = [(2 * s, P // (2 * s)), (1, s)]
                            last = mm(ap(ps, b * 512 + c0 + half, dims), KK[:, d, c * P:(c + 1) * P],
                                      ap(QQ, (1 - d) * T + c * P + half, dims), start=True, stop=True)
                elif j == KTURN:
                    eng.wait_ge(sem("qk_next"), 8 * h + 8)
                    for d in range(2):
                        for n, c in enumerate((0, 1, 2, 4) if d == 0 else (1, 2, 3, 4)):
                            last = nc.tensor.transpose(ps[:, 4 + d, n * P:(n + 1) * P], KK[:, d, c * P:(c + 1) * P], ident[:, :])
                elif j == KV:
                    eng.wait_ge(sem("ktok_ready"), h + 1)
                    for d in range(2):
                        for n, c in enumerate((0, 1, 2, 4) if d == 0 else (1, 2, 3, 4)):
                            last = mm(ps[:, 4 + d, n * P:(n + 1) * P], ktok[:, d, n, :], vtok[:, c, h * P:(h + 1) * P],
                                      start=True, stop=True)
                elif j == OUT:
                    eng.wait_ge(sem("new_states"), h + 1)
                    for c in range(NT):
                        out = ps[:, 6, c * P:(c + 1) * P] if c < 4 else ps[:, 7, 0:P]
                        cols = slice(c * P, (c + 1) * P)
                        last = mm(out, vtok[:, c, h * P:(h + 1) * P], scores[:, cols], start=True, stop=(c == 4))
                        if c < 4:
                            sf = state0[:, 0, h, :] if c == 0 else states[:, 0, c - 1, :]
                            sbk = state0[:, 1, h, :] if c == 3 else states[:, 1, c, :]
                            mm(out, sf, QQ[:, 1, cols], start=False, stop=False)
                            last = mm(out, sbk, QQ[:, 0, cols], start=False, stop=True)
                elif j == NORM:
                    eng.wait_ge(sem("osq_ready"), h + 1)
                    mm(ps[:, 4, :], ones[:, :], scratch[:, 0:TS], start=True, stop=True)
                    last = mm(ps[:, 5, 0:TP], ones[:, :], scratch[:, TS:T], start=True, stop=True)
                last.then_inc(sem("head_steps"), 1)

            def half_product(n, unit, half):
                bank = half_bank(n)
                hi, lo = unit_ready(unit)
                for k in range(KD):
                    cols = slice(half * HT, (half + 1) * HT)
                    last = split_product(ps[:, bank, 0:HT], [x[:, k * P:(k + 1) * P] for x in (hi, lo)],
                                         (h_hi[:, k, cols], h_lo[:, k, cols]), k == 0, k == KD - 1)
                last.then_inc(sem("half_made"), 1)

            eng.wait_ge(sem("v_ready"), NT)
            for n in range(NH):
                if n >= 4:
                    eng.wait_ge(sem("half_free"), n - 3)
                half_product(n, UNIT_TILE + n // 2, n % 2)
                if step_at(n):
                    step(*step_at(n))
            for n in range(NH, FIRST_STEP + HEADS * STEPS):
                step(*step_at(n))

            eng.wait_ge(sem("half_free"), NH)
            ada(SLOT_ADA2, SLOT_WOUT, 3)

            eng.wait_ge(sem("u_ready"), NC)
            eng.wait_ge(sem("heads_done"), HEADS)
            eng.wait_ge(sem("gain_ready"), 2)
            for i in range(NT):
                for c in range(NC):
                    if i < 4:
                        e, k = divmod(i, 2)
                        src = ap(u_hy, c * T + 2 * P * k + e, [(2, P)])
                    else:
                        src = u_hy[:, c, TS:T]
                    last = nc.tensor.transpose(ps[:, i, c * P:(c + 1) * P], src, ident[:, :])
                last.then_inc(sem("u_turned"), 1)
            eng.wait_ge(sem("ut_ready"), NT)
            eng.wait_ge(sem("ld_utab"), 48)
            for m in range(2):
                for cs in range(2):
                    for e in range(2):
                        for k in range(2):
                            last = mm(ps[:, 4 * m + 2 * cs + e, :], utab[:, cs, e, k, m * P:(m + 1) * P],
                                      ut[:, 2 * e + k, :], start=(k == 0), stop=(k == 1))
                last.then_inc(sem("udft"), 1)
            eng.wait_ge(sem("uspec_ready"), 1)
            mm(ps[:, 0, :], ptab[:, 0, 0, :], ut[:, NT - 1, :], start=True, stop=True)
            mm(ps[:, 1, :], ptab[:, 0, 1, :], ut[:, NT - 1, :], start=True, stop=True).then_inc(sem("udft"), 1)
            eng.wait_ge(sem("zspec_ready"), 3)

            def sum_channels(c):
                eng.wait_ge(sem("ysq_ready"), c + 1)
                for half in range(2):
                    last = mm(ps[:, 4 + half, 0:CONV // 2], ones[:, :], sq[:, half * (CONV // 2):(half + 1) * (CONV // 2)],
                              start=(c == 0), stop=(c == NC - 1))
                last.then_inc(sem("ysq_used"), 1)

            for c in range(NC):
                b = 2 * (c % 2)
                if c >= 2:
                    eng.wait_ge(sem("z_ready"), c - 1)
                cols = slice(c * P, (c + 1) * P)
                for e in range(2):
                    for n, (m, cs) in enumerate(((0, 0), (0, 1), (1, 0), (1, 1))):
                        lhs = U[:, m, cs, 0, cols] if e == 0 else U[:, m, 1 - cs, 1, cols]
                        mm(ps[:, b, e * 256:(e + 1) * 256], lhs, itab[:, m, cs, e, :], start=(n == 0), stop=(n == 3))
                for cs in range(2):
                    last = mm(ps[:, b + 1, 0:TP], Up[:, cs, cols], ptab[:, 1, cs, :], start=(cs == 0), stop=(cs == 1))
                last.then_inc(sem("z_made"), 1)
                if c:
                    sum_channels(c - 1)
            sum_channels(NC - 1)

            eng.wait_ge(sem("merged"), 1)
            for r in range(8):
                which, s, half = r // 4, (r // 2) % 2, r % 2
                if r >= 3:
                    eng.wait_ge(sem("row_ready"), r - 2)
                for k in range(4):
                    col = (2 + 3 * which) * KD + 4 * half + k
                    last = mm(ps[:, 5 + r % 3, k * P:(k + 1) * P], ap(mod, 2 * col + s, [(0, P)]), ident[:, :],
                              start=True, stop=True)
                last.then_inc(sem("row_made"), 1)

            for n in range(2):
                token_major(UNIT_WOUT + WOUT * n, WOUT, (h_hi, h_lo), "mixed", ("mixed_taken", 0) if n else None)
            eng.wait_ge(sem("mixed_taken"), 2 * NT)
            turn(xn, 1)
            eng.wait_ge(sem("h_split"), 2 * KD)
            eng.wait_ge(sem("row_ready"), 8)
            unit, n = UNIT_FFN, NH
            for r, (f0, nf) in enumerate(ROUNDS):
                for t in range(2 * nf):
                    for half in range(2):
                        if n >= NH + 3:
                            eng.wait_ge(sem("half_free"), n - 2)
                        half_product(n, unit, half)
                        n += 1
                    unit += 1
                eng.wait_ge(sem("a_ready"), f0 + nf)
                for half in range(2):
                    x = 2 * r + half
                    token_major(unit, nf // 2, (a_hi, a_lo), "down_made", ("down_taken", (x - 1) * NT) if x else None)
                    unit += nf // 2


def grid(t, offset):
    return ap(t, offset, [(PADROW, ROWS), (1, GRID)])


def rows64(t):
    return t.rearrange("p (r c) -> p r c", c=GRID)


def lay_out(x):
    cols = np.zeros((P, NVEC), np.float32)

    def put(name, a):
        a = np.asarray(a).reshape(-1)
        n = -(-a.size // P)
        for i in range(n):
            part = a[i * P:(i + 1) * P]
            cols[:part.size, VEC[name] + i] = part

    for name, key in (("c", "c"), ("c_ctx", "c_ctx"), ("norm1", "norm1_w"), ("norm2", "norm2_w"), ("ada_b", "ada_b"),
                      ("lb_f", "hg_lb_fwd"), ("lb_b", "hg_lb_bwd"), ("hg_norm", "hg_norm_w"), ("hy_d", "hy_d"),
                      ("hy_norm", "hy_norm_w"), ("hy_conv", "hy_conv_w"), ("ffn_conv", "ffn_conv_w"),
                      ("b1", "hy_b1"), ("fr1", "hy_freq1"), ("b2", "hy_b2"), ("fr2", "hy_freq2")):
        put(name, x[key])

    def cut(w, r0, nr, c0, ncol):
        return w[r0:r0 + nr * P, c0:c0 + ncol].reshape(nr, P, ncol).transpose(1, 0, 2).reshape(P, nr * ncol)

    ada, w_in, w_out = x["ada_w"][0], x["w_in"][0], x["w_out"][0]
    up, down = x["ffn_w_up"][0], x["ffn_w_down"][0]
    slots = np.zeros((NSLOT, P, RAW * UNIT), np.float32)
    s = 0

    def slot(*parts):
        nonlocal s
        at = 0
        for p in parts:
            slots[s, :, at:at + p.shape[1]] = p
            at += p.shape[1]
        s += 1

    for j in range(ADA1):
        slot(cut(ada, 0, KD, j * 256, 256))
    for i in range(IV):
        slot(cut(w_in, i * HW, 4, 3 * HW, HW))
    for i in range(0, len(TILES), 2):
        slot(*[cut(w_in, 0, KD, tile_column(t), P) for t in TILES[i:i + 2]])
    for j in range(ADA1, ADA1 + ADA2):
        slot(cut(ada, 0, KD, j * 256, 256))
    for n in range(2):
        for i in range(2):
            slot(cut(w_out, i * HW, 4, n * HW, HW))
    for f0, nf in ROUNDS:
        for f in range(f0, f0 + nf):
            slot(cut(up, 0, KD, f * P, P), cut(up, 0, KD, F + f * P, P))
        for n in range(2):
            for f in range(f0, f0 + nf, 4):
                slot(cut(down, f * P, min(4, f0 + nf - f), n * HW, HW))
    return cols, slots


OUTS = [("y_prompt", (1, TP, D)), ("y_sample", (1, TS, D)), ("new_state", (1, 1, 2, HEADS, P, P))]


def kernel(**inputs):
    import concourse.bacc as bacc
    from concourse.bass_utils import run_bass_kernel_spmd

    x = {k: np.ascontiguousarray(a) for k, a in inputs.items()}
    given = {k: x[k] for k in ("x_prompt", "x_sample", "state_hgrn", "hy_w1", "hy_w2", "hy_w3", "final_norm_w")}
    given["vec"], given["slots"] = lay_out(x)
    given.update(constants())
    nc = bacc.Bacc("TRN2", target_bir_lowering=False, num_devices=1)
    io, arrays = {}, {}
    for name, a in given.items():
        arrays[f"in_{name}"] = np.ascontiguousarray(a)
        io[name] = nc.dram_tensor(f"in_{name}", a.shape, mybir.dt.from_np(a.dtype), kind="ExternalInput").ap()
    for name, shape in OUTS:
        io[name] = nc.dram_tensor(f"out_{name}", shape, F32, kind="ExternalOutput").ap()
    build(nc, io)
    r = run_bass_kernel_spmd(nc, [arrays], core_ids=[0])
    return tuple(r.results[0][f"out_{name}"] for name, _ in OUTS)
```

```python
import math
from contextlib import ExitStack

import numpy as np
import concourse.bass as bass
from concourse import mybir

F32 = mybir.dt.float32
F32R = mybir.dt.float32r
U32 = mybir.dt.uint32
U8 = mybir.dt.uint8
ALU = mybir.AluOpType
ACT = mybir.ActivationFunctionType

P = 128
D = 1024
KD = D // P
TS, TP = 512, 128
T = TS + TP
NT = T // P
HT = T // 2
GRID = 64
ROWS = TS // GRID
PADROW = GRID + 1
PADS = ROWS * PADROW
CONV = PADS + TP
PAD = CONV + 2
HEADS = 4
HW = 512
NC = HW // P
F = 2816
NF = F // P
NHID = 64
NEMB = 33
LEVELS = 7
EPS = 1e-6
SCALE = P ** -0.5
UNIT = 1024
RAW = 2
RAWS = 3
SPLITS = 3
ROUNDS = [(0, 8), (8, 8), (16, 6)]

VEC = {}
_at = 0
for _name, _n in (("c", KD), ("c_ctx", KD), ("norm1", KD), ("norm2", KD), ("ada_b", 6 * KD),
                  ("lb_f", NC), ("lb_b", NC), ("hg_norm", NC), ("hy_d", NC), ("hy_norm", NC),
                  ("hy_conv", 3 * 3 * NC), ("ffn_conv", 3 * 2 * NF),
                  ("b1", 1), ("fr1", 1), ("b2", 1), ("fr2", 1)):
    VEC[_name] = _at
    _at += _n
NVEC = _at

TILES = []
_hy = 0
for _g in range(HEADS + 1):
    _n = (0, 2, 2, 2, 6)[_g]
    TILES += [("hy", _hy + i) for i in range(_n)]
    _hy += _n
    if _g < HEADS:
        TILES += [(k, _g) for k in ("q", "g", "ff", "fb")]
STEPS = 12
FIRST_STEP = 9
DIAG, LEVEL0, KTURN, KV, OUT, NORM = 0, 1, 8, 9, 10, 11


def tile_column(tile):
    kind, i = tile
    if kind == "hy":
        return 5 * HW + (i % 3) * HW + (i // 3) * P
    return {"q": 0, "ff": 1, "fb": 2, "g": 4}[kind] * HW + i * P


ADA1, IV, PROJ, ADA2, WOUT, ADA3 = 8, 2, len(TILES) // 2, 12, 4, 4
SLOT_IV = ADA1
SLOT_PROJ = SLOT_IV + IV
SLOT_ADA2 = SLOT_PROJ + PROJ
SLOT_WOUT = SLOT_ADA2 + ADA2
SLOT_ADA3 = SLOT_WOUT + WOUT
SLOT_FFN = SLOT_ADA3 + ADA3
ADA_SLOTS = [*range(ADA1), *range(SLOT_ADA2, SLOT_WOUT), *range(SLOT_ADA3, SLOT_FFN)]
SLOT_UNITS = [RAW] * SLOT_FFN
for _f0, _nf in ROUNDS:
    SLOT_UNITS += [RAW] * _nf
    for _n in range(2):
        SLOT_UNITS += [min(4, _nf - f) // 2 for f in range(0, _nf, 4)]
NSLOT = len(SLOT_UNITS)
IS_ADA = [s in ADA_SLOTS for s in range(NSLOT)]
UNITS = [(s, u) for s in range(NSLOT) if not IS_ADA[s] for u in range(SLOT_UNITS[s])]
NU = len(UNITS)
UNIT_TILE = 2 * IV
UNIT_WOUT = UNIT_TILE + len(TILES)
UNIT_FFN = UNIT_WOUT + 2 * WOUT


def unit_last():
    out, plain, down = [], 0, 0

    def token_major(pairs, name, value):
        nonlocal plain
        for _ in range(pairs - 1):
            plain += 1
            out.append(("unit_done", plain))
        out.append((name, value))

    token_major(2 * IV, "v_bank", NT)
    out.extend(("half_made", 2 * t + 2) for t in range(len(TILES)))
    token_major(WOUT, "mixed", NT)
    token_major(WOUT, "mixed", 2 * NT)
    t = len(TILES)
    for _, nf in ROUNDS:
        out.extend(("half_made", 2 * (t + i) + 2) for i in range(2 * nf))
        t += 2 * nf
        for _ in range(2):
            down += NT
            token_major(nf // 2, "down_made", down)
    return out


UNIT_LAST = unit_last()
assert len(UNIT_LAST) == NU


def constants():
    c = {}
    c["ident"] = np.eye(P, dtype=np.float32)
    c["diag"] = (np.eye(P) * SCALE).astype(np.float32)
    i, j = np.arange(P)[:, None], np.arange(P)[None, :]
    c["masks"] = np.stack([((i >> (l + 1)) == (j >> (l + 1))) & ((i >> l) != (j >> l))
                           for l in range(LEVELS)], 1).astype(np.uint32)
    order = np.concatenate([np.arange(0, TS, 2), np.arange(1, TS, 2)])

    def feats(L, pos):
        t = np.linspace(0.0, 1.0, L, dtype=np.float32)[pos]
        bands = np.linspace(1e-4, 15, 16, dtype=np.float32)
        ang = (np.float32(2.0 * math.pi) * pos[:, None].astype(np.float32) * bands[None, :] / np.float32(L)).astype(np.float32)
        return t, np.concatenate([t[:, None], np.cos(ang), np.sin(ang)], 1)

    ts, fs = feats(TS, order)
    tp, fp = feats(TP, np.arange(TP))
    c["feats"] = np.ascontiguousarray(np.concatenate([fs, fp]).T.astype(np.float32))
    deltas = np.abs(np.linspace(math.log(1e-2) / 1.5, math.log(1e-2) / 0.3, HW, dtype=np.float32))
    dec = np.exp(-np.concatenate([ts, tp])[:, None] * deltas[None, :]).astype(np.float32)
    c["decay"] = np.ascontiguousarray(dec.reshape(NT, P, HW).transpose(1, 0, 2))

    th = math.pi * (2 * np.arange(TS // 2) + 1) / (2 * TS)
    n = order.reshape(2, 2, P)

    def tab(shift):
        a = n[..., None] * th if not shift else (n[..., None] + 0.5) * th
        return np.stack([np.cos(a), np.sin(a)], 0)

    c["ktab"] = np.ascontiguousarray(tab(0).transpose(3, 0, 1, 2, 4).astype(np.float32))
    c["utab"] = np.ascontiguousarray(tab(1).transpose(3, 0, 1, 2, 4).astype(np.float32))
    inv = tab(1).reshape(2, 2, 2 * P, 2, P) / TS
    c["itab"] = np.ascontiguousarray(inv.transpose(4, 3, 0, 1, 2).astype(np.float32))
    tg = math.pi * (2 * np.arange(TP) + 1) / (2 * TP)
    m = np.arange(TP)
    k = np.stack([np.cos(m[:, None] * tg), np.sin(m[:, None] * tg)], 1)
    u = np.stack([np.cos((m[:, None] + 0.5) * tg), np.sin((m[:, None] + 0.5) * tg)], 1)
    v = (u.transpose(2, 1, 0)) / TP
    c["ptab"] = np.ascontiguousarray(np.stack([k, u, v], 1).astype(np.float32))
    return c




def ap(t, offset, dims):
    base = t[:]
    return bass.AP(tensor=base.tensor, offset=offset, ap=[base.ap[0], *[list(d) for d in dims]])


def build(nc, io):
    ctx = ExitStack()

    def sb(stack, name, shape, dt=F32):
        return stack.enter_context(nc.sbuf_tensor(name, [P, *shape], dt))

    sems = {}

    def sem(name):
        if name not in sems:
            sems[name] = ctx.enter_context(nc.semaphore(name))
        return sems[name]

    with ctx:
        raw = sb(ctx, "raw", [RAWS, RAW * UNIT])
        w_hi = sb(ctx, "w_hi", [SPLITS, UNIT], F32R)
        w_lo = sb(ctx, "w_lo", [SPLITS, UNIT], F32R)
        h_hi = sb(ctx, "h_hi", [KD, T], F32R)
        h_lo = sb(ctx, "h_lo", [KD, T], F32R)
        vec = sb(ctx, "vec", [NVEC])
        ident = sb(ctx, "ident", [P])
        ones = sb(ctx, "ones", [P])
        eps = sb(ctx, "eps", [1])
        silu_c = sb(ctx, "silu_c", [KD, 2])
        mod = sb(ctx, "mod", [6 * KD, 2])
        gain = sb(ctx, "gain", [2, KD, 2])
        bound = sb(ctx, "bound", [5, 2 * NC])
        stat = sb(ctx, "stat", [3, 2, NT])
        knorm = sb(ctx, "knorm", [2, 2 * NC])

        mid = ExitStack()
        kspec = sb(mid, "kspec", [2, 2, 2, HW])
        kspec_p = sb(mid, "kspec_p", [2, HW])

        early = ExitStack()
        xin = sb(early, "xin", [NT, D])
        hfull = sb(early, "hfull", [2, T])
        feats = sb(early, "feats", [T])
        w1 = sb(early, "w1", [NHID])
        w2 = sb(early, "w2", [NHID])
        w3 = sb(early, "w3", [2 * HW])
        hid = sb(early, "hid", [2, T])
        arg = sb(early, "arg", [2, T])
        decay = sb(early, "decay", [NT, HW])
        filt = sb(early, "filt", [2, NT, HW])
        ktab = sb(early, "ktab", [2, 2, 2, 2 * P])
        ptab_k = sb(early, "ptab_k", [2, TP])
        tapsum = sb(early, "tapsum", [2, HW])
        row_e = sb(early, "row_e", [2, HW])
        part = sb(early, "part", [2, HW])
        early.close()

        o_hg = sb(mid, "o_hg", [NC, T])
        x2 = sb(mid, "x2", [NC, CONV])
        u_hy = sb(mid, "u_hy", [NC, T])
        hg = ExitStack()
        eyes = sb(hg, "eyes", [P])
        masks = sb(hg, "masks", [LEVELS, P], U8)
        vtok = sb(hg, "vtok", [NT, HW])
        state0 = sb(hg, "state0", [2, HEADS, P])
        qs = sb(hg, "qs", [T])
        QQ = sb(hg, "QQ", [2, T])
        KK = sb(hg, "KK", [2, T])
        TT = [sb(hg, "TT", [2 * T]), sb(hg, "TU", [T])]
        kc = sb(hg, "kc", [2, T])
        kdiag = kc[:, 1, :]
        scores = sb(hg, "scores", [T])
        ktok = sb(hg, "ktok", [2, 4, P])
        states = sb(hg, "states", [2, 3, P])
        newst = sb(hg, "newst", [2, P])
        padm = sb(hg, "padm", [2, PAD])
        cv = sb(hg, "cv", [2, CONV])
        gs = sb(hg, "gs", [2, T])
        hg.close()
        hy = ExitStack()
        utab = sb(hy, "utab", [2, 2, 2, 2 * P])
        itab = sb(hy, "itab", [2, 2, 2, 2 * P])
        ptab = sb(hy, "ptab", [2, 2, TP])
        ut = sb(hy, "ut", [NT, HW])
        U = sb(hy, "U", [2, 2, 2, HW])
        Up = sb(hy, "Up", [2, HW])
        prod = sb(hy, "prod", [2, 2, HW])
        zc = sb(hy, "zc", [CONV])
        sq = sb(hy, "sq", [CONV])
        row_h = sb(hy, "row_h", [2, HW])
        hy.close()
        mid.close()

        late = ExitStack()
        x1 = sb(late, "x1", [NT, D])
        grow = sb(late, "grow", [2, 2, D])
        fnw = sb(late, "fnw", [D])
        tmpd = sb(late, "tmpd", [HW])
        norm2 = ExitStack()
        xn = sb(norm2, "xn", [NT, D])
        hf2 = sb(norm2, "hf2", [2, T])
        row_l = sb(norm2, "row_l", [2, HW])
        norm2.close()
        a_hi = sb(late, "a_hi", [8, T], F32R)
        a_lo = sb(late, "a_lo", [8, T], F32R)
        padf = sb(late, "padf", [2, 2, PAD])
        cf = sb(late, "cf", [2, CONV])
        actf = sb(late, "actf", [T])
        late.close()

        ps = ctx.enter_context(nc.psum_tensor("ps", [P, 8, 512], F32))

        def v(name, i=0, n=1):
            return vec[:, VEC[name] + i:VEC[name] + i + n]

        def banks(b, n=T, off=0):
            return ap(ps, b * 512 + off, [(1, n)])

        def linker(eng, own):
            count = {}

            def link(ins, name=None):
                name = name or own
                count[name] = count.get(name, 0) + 1
                ins.then_inc(sem(name), 1)
                eng.wait_ge(sem(name), count[name])
            return link

        def arrived(eng, s):
            eng.wait_ge(sem(f"raw_in{s % RAWS}"), 16 * (s // RAWS + 1))

        def unit_free(eng, n):
            name, value = UNIT_LAST[n]
            eng.wait_ge(sem(name), value)

        ada_before = [sum(IS_ADA[:s + 1]) for s in range(NSLOT)]
        units_before = [sum(SLOT_UNITS[i] for i in range(s + 1) if not IS_ADA[i]) for s in range(NSLOT)]
        NH = 2 * len(TILES)

        def half_bank(n):
            return n % 4 if n < NH else 5 + (n - NH) % 3

        def step_at(n):
            return divmod(n - FIRST_STEP, STEPS) if FIRST_STEP <= n < FIRST_STEP + HEADS * STEPS else None

        ADA_ROWS = [row_e] * 4 + [row_h] * 6 + [row_l] * 2
        V_BANKS = (2, 3, 0, 1, 4)

        def sizes(i):
            return ap((part, arg)[i % 2], 0, [(HW, 2), (1, HW)])

        def score_bank(j):
            return 6 if j and j % 2 else 4

        def x_rows(i):
            return io["x_sample"][0][i * P:(i + 1) * P, :] if i < TS // P else io["x_prompt"][0]

        block = ctx.enter_context(nc.Block())

        @block.sync
        def _(eng):
            def load(dst, src, name):
                eng.dma_start(dst, src).then_inc(sem(name), 16)

            def slot(s):
                if s >= RAWS:
                    o = s - RAWS
                    if IS_ADA[o]:
                        eng.wait_ge(sem("ada_used"), ada_before[o])
                    else:
                        eng.wait_ge(sem("hi_ready"), units_before[o])
                        eng.wait_ge(sem("lo_ready"), units_before[o])
                n = SLOT_UNITS[s] * UNIT
                load(raw[:, s % RAWS, 0:n], io["slots"][s, :, 0:n], f"raw_in{s % RAWS}")

            def store_state(h):
                eng.wait_ge(sem("new_states"), h + 1)
                load(io["new_state"][0, 0].rearrange("d h k w -> h k d w")[h], newst[:, :, :], "stored")

            load(vec[:, :], io["vec"], "ld_vec")
            load(feats[0:NEMB, :], io["feats"], "ld_filt")
            load(w1[0:NEMB, :], io["hy_w1"][0], "ld_filt")
            load(w2[0:NHID, :], io["hy_w2"][0], "ld_filt")
            load(w3[0:NHID, :], io["hy_w3"][0], "ld_filt")
            load(ident[:, :], io["ident"], "ld_ident")
            for s in range(RAWS):
                slot(s)
            load(decay[:, :, :], io["decay"], "ld_decay")
            for s in range(RAWS, 2 * RAWS):
                slot(s)
            for i in range(NT):
                load(xin[:, i, :], x_rows(i), f"ld_x{i}")
            for s in range(2 * RAWS, ADA1):
                slot(s)
            load(ktab[:, :, :, :, :], io["ktab"], "ld_ktab")
            load(ptab_k[:, :, :], io["ptab"][:, 0], "ld_ktab")
            slot(ADA1)
            eng.wait_ge(sem("h_split"), KD)
            eng.wait_ge(sem("kspec_ready"), 5)
            load(ap(QQ, 0, [(P, LEVELS), (1, P)]).bitcast(U32), io["masks"], "ld_hg")
            load(eyes[:, :], io["diag"], "ld_hg")
            load(state0[:, :, :, :], io["state_hgrn"][0, 0].rearrange("d h k w -> k d h w"), "ld_hg")
            for s in range(ADA1 + 1, SLOT_ADA2 + 2):
                slot(s)
                if s - SLOT_PROJ in (8, 11, 14):
                    store_state((s - SLOT_PROJ - 8) // 3)
            store_state(HEADS - 1)
            eng.wait_ge(sem("head_steps"), (HEADS - 1) * STEPS + OUT + 1)
            load(utab[:, :, :, :, :], io["utab"], "ld_utab")
            load(itab[:, :, :, :, :], io["itab"], "ld_utab")
            load(ptab[:, :, :, :], io["ptab"][:, 1:3], "ld_utab")
            for s in range(SLOT_ADA2 + 2, SLOT_WOUT + 2):
                slot(s)
            eng.wait_ge(sem("merged"), 1)
            eng.wait_ge(sem("ada_cols"), 10)
            for i in range(NT):
                load(x1[:, i, :], x_rows(i), "ld_res")
            load(fnw[:, :], io["final_norm_w"].partition_broadcast(P), "ld_fnw")
            for s in range(SLOT_WOUT + 2, NSLOT):
                slot(s)
            for i in range(NT):
                eng.wait_ge(sem("y_ready"), i + 1)
                dst = io["y_sample"][0][i * P:(i + 1) * P, :] if i < TS // P else io["y_prompt"][0]
                load(dst, x1[:, i, :], "stored")
            eng.wait_ge(sem("stored"), 16 * (NT + HEADS))

        @block.scalar
        def _(eng):
            link = linker(eng, "act_own")
            A = nc.scalar.activation

            def split_hi(n):
                if n >= NU:
                    return
                s, u = UNITS[n]
                arrived(eng, s)
                if n >= SPLITS:
                    unit_free(eng, n - SPLITS)
                A(w_hi[:, n % SPLITS, :], raw[:, s % RAWS, u * UNIT:(u + 1) * UNIT],
                  ACT.Copy).then_inc(sem("hi_ready"), 1)

            def spread(src, pad, half, name):
                if half == 0:
                    A(pad[:, 1:1 + 5 * PADROW].rearrange("p (r c) -> p r c", c=PADROW)[:, :, 0:GRID],
                      src.rearrange("p (r c) -> p r c", c=GRID), ACT.Copy).then_inc(sem(name), 1)
                else:
                    A(pad[:, 1 + 5 * PADROW:1 + PADS].rearrange("p (r c) -> p r c", c=PADROW)[:, :, 0:GRID],
                      src[:, 0:3 * GRID].rearrange("p (r c) -> p r c", c=GRID), ACT.Copy)
                    A(pad[:, 1 + PADS:1 + CONV], src[:, 3 * GRID:HT], ACT.Copy).then_inc(sem(name), 1)

            def ada_row(b, bank):
                eng.wait_ge(sem("ada_used"), 2 * b + 2)
                if b >= 2:
                    eng.wait_ge(sem("ada_cols"), b - 1)
                A(ADA_ROWS[b][0:2, b % 2, :], ps[0:2, bank, :], ACT.Copy).then_inc(sem("ada_row"), 1)

            def row_norm(which, i, x, junk):
                link(A(ap(junk, 0, [(1, D)]), x[:, i, :], ACT.Square, accum_out=stat[:, which, 0, i:i + 1]))
                A(stat[:, which, 1, i:i + 1], stat[:, which, 0, i:i + 1], ACT.Sqrt, scale=1.0 / D,
                  bias=eps[:, :]).then_inc(sem("norm_ready"), 1)

            def modulate(which, k):
                buf, sh, b = (hfull, hf2)[which], 3 * KD * which + k, 2 * (k % 2)
                eng.wait_ge(sem("h_turned"), KD * which + k + 1)
                if k >= 2:
                    eng.wait_ge(sem("h_split"), KD * which + k - 1)
                A(buf[:, k % 2, 0:TS], ps[:, b, :], ACT.Identity,
                  scale=gain[:, which, k, 0:1], bias=mod[:, sh, 0:1])
                A(buf[:, k % 2, TS:T], ps[:, b + 1, 0:TP], ACT.Identity,
                  scale=gain[:, which, k, 1:2], bias=mod[:, sh, 1:2]).then_inc(sem("h_full"), 1)

            eng.wait_ge(sem("ones_ready"), 2)
            eng.wait_ge(sem("ld_vec"), 16)
            A(silu_c[:, :, 0], v("c", 0, KD), ACT.Silu)
            A(silu_c[:, :, 1], v("c_ctx", 0, KD), ACT.Silu).then_inc(sem("silu_c"), 1)
            eng.wait_ge(sem("bound_in"), 1)
            A(bound[:, 1, :], bound[:, 0, :], ACT.Exp).then_inc(sem("bound_exp"), 1)
            for i in range(2):
                eng.wait_ge(sem("arg_ready"), i + 1)
                A(hid[0:NHID, i, :], arg[0:NHID, 0, :], ACT.Sin).then_inc(sem("hid_ready"), 1)
                ada_row(i, 2)

            def tap_sizes(i):
                eng.wait_ge(sem("taps_ready"), i + 1)
                if i >= 2:
                    eng.wait_ge(sem("sides_ready"), i - 1)
                A(sizes(i), filt[:, :, i, :], ACT.Abs).then_inc(sem("abs_ready"), 1)

            def norm1(i):
                eng.wait_ge(sem(f"ld_x{i}"), 16)
                row_norm(0, i, xin, hfull)

            tap_sizes(0)
            tap_sizes(1)
            ada_row(2, 2)
            tap_sizes(2)
            tap_sizes(3)
            norm1(0)
            norm1(1)
            tap_sizes(4)
            for i in range(2, NT):
                norm1(i)
            ada_row(3, 2)
            split_hi(0)
            split_hi(1)
            eng.wait_ge(sem("gain_ready"), 1)
            def take_odd(n):
                cs = n % 2
                eng.wait_ge(sem("kdft"), n + 1)
                if n >= 2:
                    eng.wait_ge(sem("kspec_ready"), n - 1)
                A(part[:, cs, :], ps[:, 4 + 2 * cs + 1, :], ACT.Copy).then_inc(sem("kodd"), 1)

            for k in range(KD):
                modulate(0, k)
                if k == 5:
                    take_odd(0)
            for n in range(1, 4):
                take_odd(n)
            for n in range(2 * IV):
                split_hi(n + 2)
            eng.wait_ge(sem("v_bank"), NT)
            eng.wait_ge(sem("kspec_ready"), 5)
            for i in range(NT):
                A(vtok[:, i, :], ps[:, V_BANKS[i], :], ACT.Copy).then_inc(sem("v_ready"), 1)

            def step(h, j):
                if j < KTURN - 1:
                    eng.wait_ge(sem("k_next"), 8 * h + j + 1)
                    if j:
                        eng.wait_ge(sem("head_steps"), h * STEPS + j)
                    A(kc[:, j % 2, :], ap(KK, 0, [(2 << j, T >> (j + 1)), (T + (1 << j), 2), (1, 1 << j)]),
                      ACT.Copy).then_inc(sem("kc_ready"), 1)
                if j == KTURN:
                    eng.wait_ge(sem("head_steps"), h * STEPS + KTURN + 1)
                    A(ktok[:, :, :, :], banks(4, 2 * 512), ACT.Copy).then_inc(sem("ktok_ready"), 1)
                if j == OUT:
                    eng.wait_ge(sem("head_steps"), h * STEPS + OUT + 1)
                    A(o_hg[:, h, :], banks(6), ACT.Square).then_inc(sem("osq_ready"), 1)
                if j == NORM:
                    eng.wait_ge(sem("head_steps"), h * STEPS + NORM + 1)
                    A(o_hg[:, h, :], banks(4), ACT.Sqrt, scale=1.0 / P, bias=eps[:, :]).then_inc(sem("rms_ready"), 1)

            for n in range(NH):
                kind, i = TILES[n // 2]
                half = n % 2
                c0 = half * HT
                src = ps[:, half_bank(n), 0:HT]
                if half == 0 and n < NH - 4:
                    split_hi(UNIT_TILE + n // 2 + 2)
                eng.wait_ge(sem("half_made"), n + 1)
                if kind == "q":
                    if i:
                        eng.wait_ge(sem("head_steps"), (i - 1) * STEPS + DIAG + 1)
                    A(qs[:, c0:c0 + HT], src, ACT.Silu).then_inc(sem("half_free"), 1)
                elif kind == "g":
                    if i >= 2:
                        eng.wait_ge(sem("heads_done"), i - 1)
                    A(gs[:, i % 2, c0:c0 + HT], src, ACT.Silu).then_inc(sem("half_free"), 1)
                elif kind in ("ff", "fb"):
                    d = int(kind == "ff")
                    if i:
                        eng.wait_ge(sem("scores_taken"), (i - 1) * 8 + 8)
                        eng.wait_ge(sem("head_steps"), (i - 1) * STEPS + KTURN + 1)
                    A(TT[0][:, d * T + c0:d * T + c0 + HT], src, ACT.Sigmoid)
                    A(KK[:, 1 - d, c0:c0 + HT], src, ACT.Sigmoid, scale=-1.0).then_inc(sem("half_free"), 1)
                else:
                    if i < 2:
                        eng.wait_ge(sem("pad_zero"), 1)
                    else:
                        eng.wait_ge(sem("hy_conv"), i - 1)
                    spread(src, padm[:, i % 2, :], half, "half_free")
                if step_at(n):
                    step(*step_at(n))
            def take_u(i):
                eng.wait_ge(sem("u_turned"), i + 1)
                A(ut[:, i, :], ps[:, i % 4, :], ACT.Copy).then_inc(sem("ut_ready"), 1)

            for n in range(NH, FIRST_STEP + HEADS * STEPS):
                if step_at(n)[1] == NORM:
                    for i in range(4):
                        take_u(i)
                step(*step_at(n))
            take_u(4)
            eng.wait_ge(sem("heads_done"), HEADS)
            eng.wait_ge(sem("hy_conv"), 3 * NC)
            eng.wait_ge(sem("stored"), 16 * HEADS)
            for m in range(2):
                for cs in range(2):
                    n = 2 * m + cs
                    eng.wait_ge(sem("udft"), n + 1)
                    if m:
                        eng.wait_ge(sem("uspec_ready"), n - 1)
                    A(prod[:, cs, 0, :], ps[:, 4 * m + 2 * cs + 1, :], ACT.Copy).then_inc(sem("uodd"), 1)
            eng.wait_ge(sem("udft"), 5)
            A(Up[:, :, :], banks(0, 2 * 512), ACT.Copy).then_inc(sem("up_ready"), 1)
            for b in range(4, 8):
                ada_row(b, 6)
            for c in range(NC):
                b = 2 * (c % 2)
                eng.wait_ge(sem("z_made"), c + 1)
                if c:
                    eng.wait_ge(sem("yhy_ready"), c)
                else:
                    eng.wait_ge(sem("zc_zero"), 1)
                A(ap(zc, 0, [(1, 2), (PADROW, ROWS), (2, GRID // 2)]),
                  ps[:, b, :].rearrange("p (e r c) -> p e r c", e=2, r=ROWS), ACT.Copy, scale=knorm[:, 1, c:c + 1])
                A(zc[:, PADS:CONV], ps[:, b + 1, 0:TP], ACT.Copy,
                  scale=knorm[:, 1, NC + c:NC + c + 1]).then_inc(sem("z_ready"), 1)
                eng.wait_ge(sem("yhy_ready"), c + 1)
                if c:
                    eng.wait_ge(sem("ysq_used"), c)
                A(sq[:, :], x2[:, c, :], ACT.Square).then_inc(sem("ysq_ready"), 1)
            eng.wait_ge(sem("ysq_used"), NC)
            A(ap(sq, 0, [(CONV // 2, 2), (1, CONV // 2)]), ap(ps, 4 * 512, [(512, 2), (1, CONV // 2)]), ACT.Sqrt,
              scale=1.0 / HW, bias=eps[:, :]).then_inc(sem("rms_ready"), 1)
            ada_row(8, 6)
            split_hi(UNIT_WOUT)
            split_hi(UNIT_WOUT + 1)
            ada_row(9, 6)

            def gate_row(r):
                eng.wait_ge(sem("row_made"), r + 1)
                A(grow[:, r // 4, (r // 2) % 2, (r % 2) * 512:(r % 2 + 1) * 512], ps[:, 5 + r % 3, :],
                  ACT.Copy).then_inc(sem("row_ready"), 1)

            split_hi(UNIT_WOUT + 2)
            split_hi(UNIT_WOUT + 3)
            eng.wait_ge(sem("merged"), 1)
            for r in range(4):
                gate_row(r)
            for n in range(4, 2 * WOUT):
                split_hi(UNIT_WOUT + n)
            for i in range(NT):
                eng.wait_ge(sem("x1_ready"), NT + i + 1)
                row_norm(1, i, x1, hf2)
                if i == 2:
                    ada_row(10, 6)
            ada_row(11, 6)
            split_hi(UNIT_FFN)
            split_hi(UNIT_FFN + 1)
            eng.wait_ge(sem("gain_ready"), 2)
            for k in range(KD):
                modulate(1, k)
                if k % 2:
                    gate_row(4 + k // 2)
            eng.wait_ge(sem("padf_zero"), 1)
            unit, t = UNIT_FFN, 0
            for r, (f0, nf) in enumerate(ROUNDS):
                for f in range(nf):
                    for gv in range(2):
                        split_hi(unit + 2)
                        unit += 1
                        for half in range(2):
                            n = NH + 4 * t + 2 * gv + half
                            eng.wait_ge(sem("half_made"), n + 1)
                            if t >= 2 and half == 0:
                                eng.wait_ge(sem("fconv"), 2 * (t - 2) + gv + 1)
                            spread(ps[:, half_bank(n), 0:HT], padf[:, t % 2, gv, :], half, "half_free")
                        if gv == 0:
                            eng.wait_ge(sem("fconv"), 2 * t + 1)
                            A(cf[:, 0, :], cf[:, 0, :], ACT.Silu).then_inc(sem("silu_done"), 1)
                    eng.wait_ge(sem("act_ready"), t + 1)
                    if r and f == 0:
                        eng.wait_ge(sem("down_made"), 2 * r * NT)
                    A(a_hi[:, f, :], actf[:, :], ACT.Copy).then_inc(sem("ahi_ready"), 1)
                    t += 1
                for k in range(nf):
                    split_hi(unit + 2)
                    unit += 1
            for i in range(NT):
                eng.wait_ge(sem("down_added"), 4 * NT + i + 1)
                link(A(ap(cf, 0, [(1, HW)]), x1[:, i, 0:HW], ACT.Square, accum_out=stat[:, 2, 0, i:i + 1]))
                link(A(stat[:, 0, 0, i:i + 1], stat[:, 2, 0, i:i + 1], ACT.Identity, scale=1.0 / D, bias=eps[:, :]))
            for i in range(NT):
                eng.wait_ge(sem("down_added"), 5 * NT + i + 1)
                link(A(ap(cf, 0, [(1, HW)]), x1[:, i, HW:D], ACT.Square, accum_out=stat[:, 0, 1, i:i + 1]))
                A(stat[:, 2, 1, i:i + 1], stat[:, 0, 1, i:i + 1], ACT.Sqrt, scale=1.0 / D,
                  bias=stat[:, 0, 0, i:i + 1]).then_inc(sem("norm_ready"), 1)

        @block.vector
        def _(eng):
            link = linker(eng, "dve_own")
            V = nc.vector

            def split_lo(n):
                if n >= NU:
                    return
                s, u = UNITS[n]
                eng.wait_ge(sem("hi_ready"), n + 1)
                if n >= SPLITS:
                    unit_free(eng, n - SPLITS)
                V.tensor_tensor(w_lo[:, n % SPLITS, :], raw[:, s % RAWS, u * UNIT:(u + 1) * UNIT],
                                w_hi[:, n % SPLITS, :].bitcast(F32), ALU.subtract).then_inc(sem("lo_ready"), 1)

            def split_h(which, k):
                buf = (hfull, hf2)[which][:, k % 2, :]
                eng.wait_ge(sem("h_full"), KD * which + k + 1)
                link(V.tensor_copy(h_hi[:, k, :], buf))
                link(V.tensor_tensor(h_lo[:, k, :], buf, h_hi[:, k, :].bitcast(F32), ALU.subtract), "h_split")

            def conv(pad, out, taps, name=None):
                link(V.tensor_scalar(out, pad[:, 1:1 + CONV], taps[1], None, ALU.mult))
                link(V.scalar_tensor_tensor(out=out, in0=pad[:, 0:CONV], scalar=taps[0], in1=out,
                                            op0=ALU.mult, op1=ALU.add))
                link(V.scalar_tensor_tensor(out=out, in0=pad[:, 2:2 + CONV], scalar=taps[2], in1=out,
                                            op0=ALU.mult, op1=ALU.add), name)

            V.memset(ones[:, :], 1.0).then_inc(sem("ones_ready"), 1)
            V.memset(eps[:, :], EPS).then_inc(sem("ones_ready"), 1)
            eng.wait_ge(sem("ld_vec"), 16)
            lb = v("lb_f", 0, 2 * NC)
            link(V.tensor_tensor(bound[:, 0, :], lb, lb, ALU.subtract), "bound_in")
            eng.wait_ge(sem("bound_exp"), 1)
            link(V.reciprocal(bound[:, 2, :], bound[:, 1, :]))
            link(V.tensor_tensor(bound[:, 2, :], bound[:, 1, :], bound[:, 2, :], ALU.mult))
            link(V.tensor_tensor(bound[:, 3, :], bound[:, 2, :], bound[:, 2, :], ALU.subtract))
            link(V.tensor_scalar(bound[:, 4, :], bound[:, 3, :], -1.0, 1.0, ALU.mult, ALU.add))

            two_pi = 2.0 * math.pi
            c1 = 6.28125
            c2 = float(np.float32(two_pi - c1))
            c3 = two_pi - c1 - c2
            a, q = arg[0:NHID, 0, :], arg[0:NHID, 1, :]
            for i in range(2):
                eng.wait_ge(sem("hid_made"), i + 1)
                if i:
                    eng.wait_ge(sem("hid_ready"), i)
                link(V.tensor_scalar(a, banks(0)[0:NHID, :], v(f"b{i + 1}")[0:NHID, :],
                                     v(f"fr{i + 1}")[0:NHID, :], ALU.add, ALU.mult))
                link(V.tensor_scalar(q, a, 1.0 / two_pi, 12582912.0, ALU.mult, ALU.add))
                link(V.tensor_scalar(q, q, 12582912.0, None, ALU.subtract))
                for cc in (c1, c2, c3):
                    link(V.scalar_tensor_tensor(out=a, in0=q, scalar=-cc, in1=a, op0=ALU.mult, op1=ALU.add))
                link(V.tensor_scalar(a, a, -3.1415925, 3.1415925, ALU.max, ALU.min), "arg_ready")
            eng.wait_ge(sem("ld_decay"), 16)
            def damp(i):
                eng.wait_ge(sem("taps_made"), i + 1)
                b, first = 4 + 2 * (i % 2), i in (0, NT - 1)
                link(V.tensor_tensor(filt[:, :, i, :], ps[:, b:b + 2, :],
                                     ap(decay, i * HW, [(0, 2), (1, HW)]), ALU.mult), None if first else "taps_ready")
                if first:
                    link(V.memset(filt[0:1, 1, i, :], 0.0), "taps_ready")

            def sides(i):
                link(V.tensor_tensor(decay[:, i, :], filt[:, 0, i, :], filt[:, 1, i, :], ALU.subtract))
                eng.wait_ge(sem("abs_ready"), i + 1)
                link(V.tensor_tensor(filt[:, 0, i, :], filt[:, 0, i, :], filt[:, 1, i, :], ALU.add))
                total, size = tapsum[:, i // (NT - 1), :], (part, arg)[i % 2]
                forth, back = ap(size, 0, [(1, HW)]), ap(size, HW, [(1, HW)])
                if i not in (0, NT - 1):
                    link(V.tensor_tensor(total, forth, total, ALU.add))
                    forth = total
                link(V.tensor_tensor(total, forth, back, ALU.add), "sides_ready")

            damp(0)
            for i in range(NT):
                if i + 1 < NT:
                    damp(i + 1)
                sides(i)
            eng.wait_ge(sem("tapsums"), 1)
            link(V.tensor_scalar(knorm[:, 0, :], ps[:, 1, 0:2 * NC], EPS, None, ALU.add))
            link(V.reciprocal(knorm[:, 1, :], knorm[:, 0, :]), "knorm_ready")
            for i in range(NT):
                eng.wait_ge(sem("norm_ready"), i + 1)
                link(V.reciprocal(stat[:, 0, 1, i:i + 1], stat[:, 0, 1, i:i + 1]))
                link(V.tensor_scalar(xin[:, i, :], xin[:, i, :], stat[:, 0, 1, i:i + 1], None, ALU.mult), "x_scaled")
            eng.wait_ge(sem("ada_cols"), 4)
            link(V.tensor_tensor(mod[:, 0:2 * KD, :], ap(ps, 3 * 512, [(2, 2 * KD), (1, 2)]),
                                 ap(vec, VEC["ada_b"], [(1, 2 * KD), (0, 2)]), ALU.add))
            link(V.scalar_tensor_tensor(out=gain[:, 0, :, :], in0=mod[:, KD:2 * KD, :], scalar=1.0,
                                        in1=ap(vec, VEC["norm1"], [(1, KD), (0, 2)]), op0=ALU.add, op1=ALU.mult), "gain_ready")
            split_lo(0)
            split_lo(1)
            def join(n):
                m, cs = 1 - n // 2, n % 2
                eng.wait_ge(sem("kodd"), n + 1)
                even = ps[:, 4 + 2 * cs, :]
                link(V.tensor_tensor(kspec[:, m, 0, cs, :], even, part[:, cs, :], ALU.add))
                first, second = (even, part[:, 0, :]) if cs == 0 else (part[:, 1, :], even)
                link(V.tensor_tensor(kspec[:, m, 1, cs, :], first, second, ALU.subtract), "kspec_ready")

            for k in range(KD):
                split_h(0, k)
                if k == 5:
                    join(0)
            for n in range(1, 4):
                join(n)
            eng.wait_ge(sem("kdft"), 5)
            link(V.tensor_copy(kspec_p[:, :, :], ps[:, 0:2, :]), "kspec_ready")
            for n in range(2 * IV):
                split_lo(n + 2)

            def bound_gates(h, d):
                t0 = TT[0][:, (1 - d) * T:(2 - d) * T]
                fb = NC * d + h
                link(V.tensor_scalar(t0, t0, bound[:, 4, fb:fb + 1], bound[:, 3, fb:fb + 1], ALU.mult, ALU.add))
                link(V.tensor_scalar(KK[:, d, :], KK[:, d, :], bound[:, 4, fb:fb + 1], None, ALU.mult),
                     "k_next" if d else None)

            def start_head(h):
                link(V.tensor_tensor(kdiag, KK[:, 0, :], KK[:, 1, :], ALU.add))
                if h:
                    eng.wait_ge(sem("head_steps"), (h - 1) * STEPS + OUT + 1)
                link(V.scalar_tensor_tensor(out=QQ[:, :, :], in0=ap(qs, 0, [(0, 2), (1, T)]), scalar=SCALE,
                                            in1=ap(TT[0], 0, [(T, 2), (1, T)]), op0=ALU.mult, op1=ALU.mult), "qk_next")

            def take_level(h, j):
                if j == DIAG:
                    eng.wait_ge(sem("head_steps"), h * STEPS + j + 1)
                    link(V.tensor_tensor(scores[:, :], banks(score_bank(j)), ap(eyes, 0, [(0, NT), (1, P)]), ALU.mult), "scores_taken")
                    return
                l = j - LEVEL0
                s = 1 << l
                nb, n = T // (2 * s), T // s
                t, t2 = TT[l % 2], TT[(l + 1) % 2]
                both = [(2 * s, nb), (T + s, 2), (1, s)]
                eng.wait_ge(sem("kc_ready"), LEVELS * h + l + 1)
                link(V.tensor_tensor(ap(KK, 0, both), ap(KK, 0, both), ap(t, n + 1, [(2, nb), (-n - 1, 2), (0, s)]), ALU.mult), "k_next")
                eng.wait_ge(sem("head_steps"), h * STEPS + j + 1)
                link(V.tensor_tensor(ap(QQ, 0, both), ap(QQ, 0, both), ap(t, 1, [(2, nb), (n - 1, 2), (0, s)]), ALU.mult), "qk_next")
                link(V.tensor_tensor(ap(t2, 0, [(nb, 2), (1, nb)]), ap(t, 0, [(n, 2), (2, nb)]),
                                     ap(t, 1, [(n, 2), (2, nb)]), ALU.mult))
                link(V.copy_predicated(scores[:, :], ap(masks, l * P, [(0, NT), (1, P)]), banks(score_bank(j))), "scores_taken")

            def make_states(h):
                eng.wait_ge(sem("head_steps"), h * STEPS + KV + 1)
                t7 = TT[LEVELS % 2]
                for d in range(2):
                    for n in range(3):
                        c = n if d == 0 else 3 - n
                        at = (0, 1, 2)[n] if d == 0 else 2 - n
                        idx = c if d == 0 else c - 1
                        prev = state0[:, d, h, :] if n == 0 else states[:, d, at - 1 if d == 0 else at + 1, :]
                        col = (NT + c) if d == 0 else c
                        link(V.scalar_tensor_tensor(out=states[:, d, at, :], in0=prev, scalar=t7[:, col:col + 1],
                                                    in1=ps[:, 4 + d, idx * P:(idx + 1) * P], op0=ALU.mult, op1=ALU.add))
                if h:
                    eng.wait_ge(sem("stored"), 16 * h)
                link(V.tensor_copy(newst[:, :, :], ap(ps, 4 * 512 + 3 * P, [(512, 2), (1, P)])), "new_states")

            def finish_head(h):
                eng.wait_ge(sem("rms_ready"), h + 1)
                link(V.reciprocal(o_hg[:, h, :], o_hg[:, h, :]))
                link(V.scalar_tensor_tensor(out=o_hg[:, h, :], in0=banks(6), scalar=v("hg_norm", h),
                                            in1=o_hg[:, h, :], op0=ALU.mult, op1=ALU.mult))
                link(V.tensor_tensor(o_hg[:, h, :], o_hg[:, h, :], gs[:, h % 2, :], ALU.mult), "heads_done")

            def step(h, j):
                if j < KTURN:
                    take_level(h, j)
                elif j == KV:
                    make_states(h)
                elif j == NORM:
                    finish_head(h)

            eng.wait_ge(sem("v_bank"), NT)
            eng.wait_ge(sem("ld_hg"), 48)
            link(V.tensor_copy(masks[:, :, :], ap(QQ, 0, [(P, LEVELS), (1, P)]).bitcast(U32)))
            for i in range(2):
                link(V.memset(padm[:, i, :], 0.0), "pad_zero" if i else None)
            for n in range(NH):
                kind, i = TILES[n // 2]
                if n % 2 == 0 and n < NH - 4:
                    split_lo(UNIT_TILE + n // 2 + 2)
                if n % 2:
                    eng.wait_ge(sem("half_free"), n + 1)
                    if kind == "hy":
                        c, what = divmod(i, 3)
                        taps = [v("hy_conv", (w * 3 + what) * NC + c) for w in range(3)]
                        out = (cv[:, 0, :], cv[:, 1, :], x2[:, c, :])[what]
                        conv(padm[:, i % 2, :], out, taps, "hy_conv")
                        if what == 1:
                            link(V.tensor_tensor(rows64(u_hy[:, c, 0:TS]), grid(cv, 0), grid(cv, CONV), ALU.mult))
                            link(V.tensor_tensor(u_hy[:, c, TS:T], cv[:, 0, PADS:CONV], cv[:, 1, PADS:CONV], ALU.mult), "u_ready")
                    elif kind in ("ff", "fb"):
                        bound_gates(i, int(kind == "fb"))
                if step_at(n):
                    step(*step_at(n))
                if kind == "fb" and n % 2:
                    start_head(i)
            for n in range(NH, FIRST_STEP + HEADS * STEPS):
                step(*step_at(n))

            def ada_columns(b0, b1, bank):
                eng.wait_ge(sem("ada_cols"), b1)
                link(V.tensor_tensor(mod[:, 4 * b0:4 * b1, :], ap(ps, bank * 512 + 8 * b0, [(2, 4 * (b1 - b0)), (1, 2)]),
                                     ap(vec, VEC["ada_b"] + 4 * b0, [(1, 4 * (b1 - b0)), (0, 2)]), ALU.add), "mod_ready")

            eng.wait_ge(sem("stored"), 16 * HEADS)
            for m in range(2):
                for cs in range(2):
                    eng.wait_ge(sem("uodd"), 2 * m + cs + 1)
                    even, odd = ps[:, 4 * m + 2 * cs, :], prod[:, cs, 0, :]
                    link(V.tensor_tensor(U[:, m, 0, cs, :], even, odd, ALU.add))
                    link(V.tensor_tensor(U[:, m, 1, 1 - cs, :], even, odd, ALU.subtract), "uspec_ready")
            for m in range(2):
                C, S = U[:, m, :, 0, :], U[:, m, :, 1, :]
                Kr, Ks = kspec[:, m, :, 0, :], kspec[:, m, :, 1, :]
                r, t = prod[:, 0, :, :], prod[:, 1, :, :]
                link(V.tensor_tensor(r, C, Kr, ALU.mult))
                link(V.tensor_tensor(t, S, Ks, ALU.mult))
                link(V.tensor_tensor(r, r, t, ALU.subtract))
                link(V.tensor_tensor(t, C, Ks, ALU.mult))
                link(V.tensor_tensor(S, S, Kr, ALU.mult))
                link(V.tensor_tensor(S, S, t, ALU.add))
                link(V.tensor_tensor(U[:, m, 0, 0, :], r[:, 0, :], U[:, m, 1, 1, :], ALU.add))
                link(V.tensor_tensor(U[:, m, 1, 0, :], r[:, 1, :], U[:, m, 0, 1, :], ALU.add))
                link(V.tensor_tensor(U[:, m, 1, 1, :], r[:, 0, :], U[:, m, 1, 1, :], ALU.subtract))
                link(V.tensor_tensor(U[:, m, 0, 1, :], U[:, m, 0, 1, :], r[:, 1, :], ALU.subtract), "zspec_ready")
            eng.wait_ge(sem("up_ready"), 1)
            r, t = prod[:, 0, 0, :], prod[:, 1, 0, :]
            link(V.tensor_tensor(r, Up[:, 0, :], kspec_p[:, 0, :], ALU.mult))
            link(V.tensor_tensor(t, Up[:, 1, :], kspec_p[:, 1, :], ALU.mult))
            link(V.tensor_tensor(r, r, t, ALU.subtract))
            link(V.tensor_tensor(t, Up[:, 0, :], kspec_p[:, 1, :], ALU.mult))
            link(V.tensor_tensor(Up[:, 1, :], Up[:, 1, :], kspec_p[:, 0, :], ALU.mult))
            link(V.tensor_tensor(Up[:, 1, :], Up[:, 1, :], t, ALU.add))
            link(V.tensor_copy(Up[:, 0, :], r), "zspec_ready")
            link(V.memset(zc[:, :], 0.0), "zc_zero")
            eng.wait_ge(sem("half_made"), NH)
            link(V.tensor_copy(h_hi[:, 0:NC, :], o_hg[:, :, :]))
            link(V.tensor_tensor(h_lo[:, 0:NC, :], o_hg[:, :, :], h_hi[:, 0:NC, :].bitcast(F32), ALU.subtract), "heads_split")
            ada_columns(4, 8, 7)
            for c in range(NC):
                eng.wait_ge(sem("z_ready"), c + 1)
                link(V.scalar_tensor_tensor(out=grid(zc, 0), in0=rows64(u_hy[:, c, 0:TS]), scalar=v("hy_d", c),
                                            in1=grid(zc, 0), op0=ALU.mult, op1=ALU.add))
                link(V.scalar_tensor_tensor(out=zc[:, PADS:CONV], in0=u_hy[:, c, TS:T], scalar=v("hy_d", c),
                                            in1=zc[:, PADS:CONV], op0=ALU.mult, op1=ALU.add))
                link(V.tensor_tensor(x2[:, c, :], x2[:, c, :], zc[:, :], ALU.mult), "yhy_ready")
            eng.wait_ge(sem("rms_ready"), HEADS + 1)
            link(V.reciprocal(sq[:, :], sq[:, :]))
            for c in range(NC):
                link(V.scalar_tensor_tensor(out=x2[:, c, :], in0=x2[:, c, :], scalar=v("hy_norm", c),
                                            in1=sq[:, :], op0=ALU.mult, op1=ALU.mult))
            split_lo(UNIT_WOUT)
            split_lo(UNIT_WOUT + 1)
            for lo in range(2):
                for dst, src in ((ap((h_hi, h_lo)[lo], NC * T, [(T, NC), (GRID, ROWS), (1, GRID)]),
                                  ap(x2, 0, [(CONV, NC), (PADROW, ROWS), (1, GRID)])),
                                 (ap((h_hi, h_lo)[lo], NC * T + TS, [(T, NC), (1, TP)]),
                                  ap(x2, PADS, [(CONV, NC), (1, TP)]))):
                    last = "merged" if lo and len(src.shape) == 3 else None
                    if not lo:
                        link(V.tensor_copy(dst, src))
                    else:
                        hi = bass.AP(tensor=h_hi[:].tensor, offset=dst.offset, ap=dst.ap).bitcast(F32)
                        link(V.tensor_tensor(dst, src, hi, ALU.subtract), last)

            ada_columns(8, 10, 7)
            link(V.scalar_tensor_tensor(out=gain[:, 1, :, :], in0=mod[:, 4 * KD:5 * KD, :], scalar=1.0,
                                        in1=ap(vec, VEC["norm2"], [(1, KD), (0, 2)]), op0=ALU.add, op1=ALU.mult), "gain_ready")

            def add(which, i, n, name_taken, name_done):
                s = int(i == NT - 1)
                link(V.tensor_tensor(tmpd[:, :], ps[:, i, :], grow[:, which, s, n * HW:(n + 1) * HW], ALU.mult), name_taken)
                xs = x1[:, i, n * HW:(n + 1) * HW]
                link(V.tensor_tensor(xs, xs, tmpd[:, :], ALU.add), name_done)

            def norm_rows(i):
                eng.wait_ge(sem("norm_ready"), NT + i + 1)
                link(V.reciprocal(stat[:, 1, 1, i:i + 1], stat[:, 1, 1, i:i + 1]))
                link(V.tensor_scalar(xn[:, i, :], x1[:, i, :], stat[:, 1, 1, i:i + 1], None, ALU.mult), "x_scaled")

            for n in range(2):
                for k in range(2, WOUT + 2 * (1 - n)):
                    split_lo(UNIT_WOUT + WOUT * n + k)
                if n == 0:
                    eng.wait_ge(sem("ld_res"), 16 * NT)
                    eng.wait_ge(sem("row_ready"), 4)
                for i in range(NT):
                    eng.wait_ge(sem("mixed"), NT * n + i + 1)
                    add(0, i, n, "mixed_taken", "x1_ready")
                    if n and i:
                        norm_rows(i - 1)
            norm_rows(NT - 1)
            ada_columns(10, 12, 7)
            split_lo(UNIT_FFN)
            split_lo(UNIT_FFN + 1)
            for k in range(KD):
                split_h(1, k)
            for i in range(2):
                for gv in range(2):
                    link(V.memset(padf[:, i, gv, :], 0.0), "padf_zero" if i and gv else None)
            def final_norm(i):
                if i == 0:
                    eng.wait_ge(sem("ld_fnw"), 16)
                eng.wait_ge(sem("norm_ready"), 2 * NT + i + 1)
                link(V.reciprocal(stat[:, 2, 1, i:i + 1], stat[:, 2, 1, i:i + 1]))
                link(V.scalar_tensor_tensor(out=x1[:, i, :], in0=x1[:, i, :], scalar=stat[:, 2, 1, i:i + 1],
                                            in1=fnw[:, :], op0=ALU.mult, op1=ALU.mult), "y_ready")

            unit, t = UNIT_FFN, 0
            for r, (f0, nf) in enumerate(ROUNDS):
                for f in range(nf):
                    for gv in range(2):
                        split_lo(unit + 2)
                        unit += 1
                        eng.wait_ge(sem("half_free"), NH + 4 * t + 2 * gv + 2)
                        taps = [v("ffn_conv", (w * 2 + gv) * NF + f0 + f) for w in range(3)]
                        conv(padf[:, t % 2, gv, :], cf[:, gv, :], taps, "fconv")
                    eng.wait_ge(sem("silu_done"), t + 1)
                    link(V.tensor_tensor(rows64(actf[:, 0:TS]), grid(cf, 0), grid(cf, CONV), ALU.mult))
                    link(V.tensor_tensor(actf[:, TS:T], cf[:, 0, PADS:CONV], cf[:, 1, PADS:CONV], ALU.mult), "act_ready")
                    eng.wait_ge(sem("ahi_ready"), t + 1)
                    link(V.tensor_tensor(a_lo[:, f, :], actf[:, :], a_hi[:, f, :].bitcast(F32), ALU.subtract), "a_ready")
                    t += 1
                for n in range(2):
                    for k in range(nf // 2):
                        split_lo(unit + 2)
                        unit += 1
                    for i in range(NT):
                        eng.wait_ge(sem("down_made"), (2 * r + n) * NT + i + 1)
                        add(1, i, n, "down_taken", "down_added")
                        if r == len(ROUNDS) - 1 and n and i:
                            final_norm(i - 1)
            final_norm(NT - 1)

        @block.tensor
        def _(eng):
            mm = nc.tensor.matmul

            def split_product(out, lhs, rhs, first, last):
                mm(out, lhs[0], rhs[0], start=first, stop=False)
                mm(out, lhs[0], rhs[1], start=False, stop=False)
                return mm(out, lhs[1], rhs[0], start=False, stop=last)

            def unit_ready(n):
                eng.wait_ge(sem("hi_ready"), n + 1)
                eng.wait_ge(sem("lo_ready"), n + 1)
                return w_hi[:, n % SPLITS, :], w_lo[:, n % SPLITS, :]

            def ada_block(b, bank, parts=(0, 1)):
                if b and 0 in parts:
                    eng.wait_ge(sem("ada_row"), b)
                for i in parts:
                    slot = ADA_SLOTS[2 * b + i]
                    arrived(eng, slot)
                    for kk in range(4):
                        k = 4 * i + kk
                        last = mm(ps[0:2, bank, :], silu_c[:, k, :], raw[:, slot % RAWS, kk * HW:(kk + 1) * HW],
                                  start=(k == 0), stop=(k == KD - 1))
                    last.then_inc(sem("ada_used"), 1)

            def ada_turn(b, bank):
                eng.wait_ge(sem("ada_row"), b + 1)
                for k in range(4):
                    col = 8 * b + 2 * k
                    last = nc.tensor.transpose(ps[:, bank, col:col + 2], ADA_ROWS[b][0:2, b % 2, k * P:(k + 1) * P],
                                               ident[0:2, 0:2])
                last.then_inc(sem("ada_cols"), 1)

            def ada_blocks(b0, b1):
                for b in range(b0, b1):
                    ada_block(b, 6)
                    if b > b0:
                        ada_turn(b - 1, 7)
                ada_turn(b1 - 1, 7)

            def taps(i):
                if i >= 2:
                    eng.wait_ge(sem("taps_ready"), i - 1)
                for d in range(2):
                    last = mm(ps[:, 4 + 2 * (i % 2) + d, :], hid[0:NHID, 1, i * P:(i + 1) * P],
                              w3[0:NHID, d * HW:(d + 1) * HW], start=True, stop=True)
                last.then_inc(sem("taps_made"), 1)

            eng.wait_ge(sem("ld_filt"), 64)
            mm(ps[0:NHID, 0, :], w1[0:NEMB, :], feats[0:NEMB, 0:TS], start=True, stop=True)
            mm(ps[0:NHID, 1, 0:TP], w1[0:NEMB, :], feats[0:NEMB, TS:T], start=True, stop=True).then_inc(sem("hid_made"), 1)
            eng.wait_ge(sem("silu_c"), 1)
            ada_block(0, 2)
            eng.wait_ge(sem("hid_ready"), 1)
            mm(ps[0:NHID, 0, :], w2[0:NHID, :], hid[0:NHID, 0, 0:TS], start=True, stop=True)
            mm(ps[0:NHID, 1, 0:TP], w2[0:NHID, :], hid[0:NHID, 0, TS:T], start=True, stop=True).then_inc(sem("hid_made"), 1)
            ada_block(1, 2, (0,))
            eng.wait_ge(sem("hid_ready"), 2)
            taps(0)
            taps(1)
            ada_block(1, 2, (1,))
            eng.wait_ge(sem("ld_ident"), 16)
            ada_turn(0, 3)
            taps(2)
            ada_block(2, 2, (0,))
            taps(3)
            ada_block(2, 2, (1,))
            taps(4)
            ada_turn(1, 3)
            ada_block(3, 2)
            ada_turn(2, 3)
            eng.wait_ge(sem("ones_ready"), 2)
            eng.wait_ge(sem("sides_ready"), NT)
            for s in range(2):
                for c in range(NC):
                    last = mm(ps[:, 1, s * NC + c:s * NC + c + 1], tapsum[:, s, c * P:(c + 1) * P], ones[:, 0:1],
                              start=True, stop=True)
            last.then_inc(sem("tapsums"), 1)
            ada_turn(3, 3)

            def turn(src, which, before, between):
                for k in range(KD):
                    if k >= 2:
                        eng.wait_ge(sem("h_full"), KD * which + k - 1)
                    if k == 1 and before:
                        for name, value in before:
                            eng.wait_ge(sem(name), value)
                    b = 2 * (k % 2)
                    for i in range(NT):
                        if k == 0:
                            eng.wait_ge(sem("x_scaled"), NT * which + i + 1)
                        dst = ps[:, b, i * P:(i + 1) * P] if i < 4 else ps[:, b + 1, 0:P]
                        last = nc.tensor.transpose(dst, src[:, i, k * P:(k + 1) * P], ident[:, :])
                    last.then_inc(sem("h_turned"), 1)
                    between(k)

            def filter_dft(n, cs, e, k):
                rhs = filt[:, 0, 2 * e + k, :] if cs == 0 else decay[:, 2 * e + k, :]
                m = 1 - n // 2
                last = mm(ps[:, 4 + 2 * cs + e, :], ktab[:, cs, e, k, m * P:(m + 1) * P], rhs, start=(k == 0), stop=(k == 1))
                if e and k:
                    last.then_inc(sem("kdft"), 1)

            eng.wait_ge(sem("ld_ktab"), 32)
            eng.wait_ge(sem("hid_ready"), 2)
            eng.wait_ge(sem("knorm_ready"), 1)
            turn(xin, 0, (("gain_ready", 1),),
                 lambda k: filter_dft(k // 4, k // 4, (k // 2) % 2, k % 2))
            for n in range(2, 4):
                eng.wait_ge(sem("kspec_ready"), n - 1)
                for e in range(2):
                    for k in range(2):
                        filter_dft(n, n % 2, e, k)
            eng.wait_ge(sem("h_full"), KD)
            mm(ps[:, 0, :], ptab_k[:, 0, :], filt[:, 0, NT - 1, :], start=True, stop=True)
            mm(ps[:, 1, :], ptab_k[:, 1, :], decay[:, NT - 1, :], start=True, stop=True).then_inc(sem("kdft"), 1)

            def token_major(unit0, pairs, lhs, name, before, bank=range(NT), part=None, tiles_first=False):
                steps = [(p, i) for p in part or range(pairs) for i in range(NT)]
                if tiles_first:
                    steps.sort(key=lambda step: step[1])
                for p, i in steps:
                    if i == 0:
                        unit_ready(unit0 + p)
                    hi, lo = (w[:, (unit0 + p) % SPLITS, :] for w in (w_hi, w_lo))
                    for kk in range(2):
                        k = 2 * p + kk
                        before(p, i, k)
                        last = split_product(ps[:, bank[i], :], [x[:, k, i * P:(i + 1) * P] for x in lhs],
                                             [x[:, kk * HW:(kk + 1) * HW] for x in (hi, lo)],
                                             k == 0, k == 2 * pairs - 1)
                    if p == pairs - 1:
                        last.then_inc(sem(name), 1)
                    elif i == NT - 1:
                        last.then_inc(sem("unit_done"), 1)

            def before_v(p, i, k):
                if i == 0:
                    eng.wait_ge(sem("h_split"), k + 1)
                if p == 0 and i == 2 and k == 0:
                    eng.wait_ge(sem("kspec_ready"), 5)

            token_major(0, 2 * IV, (h_hi, h_lo), "v_bank", before_v, V_BANKS)

            def chunk(j, c):
                b = score_bank(j)
                return ps[:, b, c * P:(c + 1) * P] if c < 4 else ps[:, b + 1, 0:P]

            def step(h, j):
                if j == DIAG:
                    eng.wait_ge(sem("qk_next"), 8 * h + 1)
                    if h:
                        eng.wait_ge(sem("rms_ready"), h)
                    for c in range(NT):
                        last = mm(chunk(j, c), kdiag[:, c * P:(c + 1) * P], qs[:, c * P:(c + 1) * P], start=True, stop=True)
                elif j < KTURN:
                    l = j - LEVEL0
                    s = 1 << l
                    eng.wait_ge(sem("kc_ready"), LEVELS * h + l + 1)
                    eng.wait_ge(sem("qk_next"), 8 * h + 1 + l)
                    if j == 1 and h:
                        eng.wait_ge(sem("heads_done"), h)
                    if j >= 2:
                        eng.wait_ge(sem("scores_taken"), 8 * h + j - 1)
                    for c in range(NT):
                        last = mm(chunk(j, c), kc[:, l % 2, c * P:(c + 1) * P],
                                  ap(QQ, c * P, [(2 * s, P // (2 * s)), (T + s, 2), (1, s)]), start=True, stop=True)
                elif j == KTURN:
                    eng.wait_ge(sem("k_next"), 8 * h + 8)
                    eng.wait_ge(sem("scores_taken"), 8 * h + 7)
                    for d in range(2):
                        for n, c in enumerate((0, 1, 2, 4) if d == 0 else (1, 2, 3, 4)):
                            last = nc.tensor.transpose(ps[:, 4 + d, n * P:(n + 1) * P], KK[:, d, c * P:(c + 1) * P], ident[:, :])
                elif j == KV:
                    eng.wait_ge(sem("ktok_ready"), h + 1)
                    for d in range(2):
                        for n, c in enumerate((0, 1, 2, 4) if d == 0 else (1, 2, 3, 4)):
                            last = mm(ps[:, 4 + d, n * P:(n + 1) * P], ktok[:, d, n, :], vtok[:, c, h * P:(h + 1) * P],
                                      start=True, stop=True)
                elif j == OUT:
                    eng.wait_ge(sem("new_states"), h + 1)
                    eng.wait_ge(sem("scores_taken"), 8 * h + 8)
                    for c in range(NT):
                        out = ps[:, 6, c * P:(c + 1) * P] if c < 4 else ps[:, 7, 0:P]
                        cols = slice(c * P, (c + 1) * P)
                        last = mm(out, vtok[:, c, h * P:(h + 1) * P], scores[:, cols], start=True, stop=(c == 4))
                        if c < 4:
                            sf = state0[:, 0, h, :] if c == 0 else states[:, 0, c - 1, :]
                            sbk = state0[:, 1, h, :] if c == 3 else states[:, 1, c, :]
                            mm(out, sf, QQ[:, 1, cols], start=False, stop=False)
                            last = mm(out, sbk, QQ[:, 0, cols], start=False, stop=True)
                elif j == NORM:
                    eng.wait_ge(sem("osq_ready"), h + 1)
                    mm(ps[:, 4, :], ones[:, :], o_hg[:, h, 0:TS], start=True, stop=True)
                    last = mm(ps[:, 5, 0:TP], ones[:, :], o_hg[:, h, TS:T], start=True, stop=True)
                last.then_inc(sem("head_steps"), 1)

            def half_product(n, unit, half):
                bank = half_bank(n)
                hi, lo = unit_ready(unit)
                for k in range(KD):
                    if n == NH:
                        eng.wait_ge(sem("h_split"), KD + k + 1)
                    cols = slice(half * HT, (half + 1) * HT)
                    last = split_product(ps[:, bank, 0:HT], [x[:, k * P:(k + 1) * P] for x in (hi, lo)],
                                         (h_hi[:, k, cols], h_lo[:, k, cols]), k == 0, k == KD - 1)
                last.then_inc(sem("half_made"), 1)

            eng.wait_ge(sem("v_ready"), NT)
            for n in range(NH):
                if n >= 4:
                    eng.wait_ge(sem("half_free"), n - 3)
                half_product(n, UNIT_TILE + n // 2, n % 2)
                if step_at(n):
                    step(*step_at(n))
            def turn_u(i):
                for c in range(NC):
                    if i < 4:
                        e, k = divmod(i, 2)
                        src = ap(u_hy, c * T + 2 * P * k + e, [(2, P)])
                    else:
                        src = u_hy[:, c, TS:T]
                    last = nc.tensor.transpose(ps[:, i % 4, c * P:(c + 1) * P], src, ident[:, :])
                last.then_inc(sem("u_turned"), 1)

            for n in range(NH, FIRST_STEP + HEADS * STEPS):
                if step_at(n)[1] == NORM:
                    eng.wait_ge(sem("half_free"), NH)
                    eng.wait_ge(sem("u_ready"), NC)
                    for i in range(4):
                        turn_u(i)
                step(*step_at(n))
            eng.wait_ge(sem("ut_ready"), 1)
            turn_u(4)
            eng.wait_ge(sem("ut_ready"), NT)
            eng.wait_ge(sem("ld_utab"), 48)
            for m in range(2):
                if m:
                    eng.wait_ge(sem("heads_done"), HEADS)
                for cs in range(2):
                    for e in range(2):
                        for k in range(2):
                            last = mm(ps[:, 4 * m + 2 * cs + e, :], utab[:, cs, e, k, m * P:(m + 1) * P],
                                      ut[:, 2 * e + k, :], start=(k == 0), stop=(k == 1))
                    last.then_inc(sem("udft"), 1)
            eng.wait_ge(sem("uspec_ready"), 1)
            mm(ps[:, 0, :], ptab[:, 0, 0, :], ut[:, NT - 1, :], start=True, stop=True)
            mm(ps[:, 1, :], ptab[:, 0, 1, :], ut[:, NT - 1, :], start=True, stop=True).then_inc(sem("udft"), 1)
            eng.wait_ge(sem("uspec_ready"), 4)
            ada_blocks(4, 8)
            eng.wait_ge(sem("zspec_ready"), 3)

            def sum_channels(c):
                eng.wait_ge(sem("ysq_ready"), c + 1)
                for half in range(2):
                    last = mm(ps[:, 4 + half, 0:CONV // 2], ones[:, :], sq[:, half * (CONV // 2):(half + 1) * (CONV // 2)],
                              start=(c == 0), stop=(c == NC - 1))
                last.then_inc(sem("ysq_used"), 1)

            for c in range(NC):
                b = 2 * (c % 2)
                if c >= 2:
                    eng.wait_ge(sem("z_ready"), c - 1)
                cols = slice(c * P, (c + 1) * P)
                for e in range(2):
                    for n, (m, cs) in enumerate(((0, 0), (0, 1), (1, 0), (1, 1))):
                        lhs = U[:, m, cs, 0, cols] if e == 0 else U[:, m, 1 - cs, 1, cols]
                        mm(ps[:, b, e * 256:(e + 1) * 256], lhs, itab[:, m, cs, e, :], start=(n == 0), stop=(n == 3))
                for cs in range(2):
                    last = mm(ps[:, b + 1, 0:TP], Up[:, cs, cols], ptab[:, 1, cs, :], start=(cs == 0), stop=(cs == 1))
                last.then_inc(sem("z_made"), 1)
                if c:
                    sum_channels(c - 1)
            eng.wait_ge(sem("mod_ready"), 1)
            ada_block(8, 6)
            sum_channels(NC - 1)
            ada_block(9, 6)
            ada_turn(8, 7)
            ada_turn(9, 7)

            def gate_part(r, k):
                which, s, half = r // 4, (r // 2) % 2, r % 2
                if r >= 3 and k == 0:
                    eng.wait_ge(sem("row_ready"), r - 2)
                col = (2 + 3 * which) * KD + 4 * half + k
                last = mm(ps[:, 5 + r % 3, k * P:(k + 1) * P], ap(mod, 2 * col + s, [(0, P)]), ident[:, :],
                          start=True, stop=True)
                if k == 3:
                    last.then_inc(sem("row_made"), 1)

            def before_mixed(p, i, k):
                pass

            def before_mixed2(p, i, k):
                if k == 0:
                    eng.wait_ge(sem("mixed_taken"), i + 1)

            eng.wait_ge(sem("heads_split"), 1)
            eng.wait_ge(sem("rms_ready"), HEADS + 1)
            token_major(UNIT_WOUT, WOUT, (h_hi, h_lo), "mixed", before_mixed, part=range(2))
            eng.wait_ge(sem("merged"), 1)
            token_major(UNIT_WOUT, WOUT, (h_hi, h_lo), "mixed", before_mixed, part=range(2, 3))
            eng.wait_ge(sem("mod_ready"), 2)
            for r in range(4):
                for k in range(4):
                    gate_part(r, k)
            token_major(UNIT_WOUT, WOUT, (h_hi, h_lo), "mixed", before_mixed, part=range(3, 4))
            token_major(UNIT_WOUT + WOUT, WOUT, (h_hi, h_lo), "mixed", before_mixed2)
            eng.wait_ge(sem("row_ready"), 4)
            ada_blocks(10, 12)

            def gate_between(k):
                if k == 0:
                    eng.wait_ge(sem("mod_ready"), 3)
                for kk in range(2):
                    gate_part(4 + k // 2, 2 * (k % 2) + kk)

            eng.wait_ge(sem("mixed_taken"), 2 * NT)
            turn(xn, 1, (), gate_between)
            eng.wait_ge(sem("row_ready"), 8)
            unit, n = UNIT_FFN, NH
            for r, (f0, nf) in enumerate(ROUNDS):
                for t in range(2 * nf):
                    for half in range(2):
                        if n >= NH + 3:
                            eng.wait_ge(sem("half_free"), n - 2)
                        half_product(n, unit, half)
                        n += 1
                    unit += 1
                for half in range(2):
                    x = 2 * r + half

                    def before_down(p, i, k, f0=f0, half=half, x=x):
                        if half == 0 and i == 0:
                            eng.wait_ge(sem("a_ready"), f0 + k + 1)
                        if x and k == 0:
                            eng.wait_ge(sem("down_taken"), (x - 1) * NT + i + 1)

                    token_major(unit, nf // 2, (a_hi, a_lo), "down_made", before_down,
                                tiles_first=x == 2 * len(ROUNDS) - 1)
                    unit += nf // 2


def grid(t, offset):
    return ap(t, offset, [(PADROW, ROWS), (1, GRID)])


def rows64(t):
    return t.rearrange("p (r c) -> p r c", c=GRID)


def lay_out(x):
    cols = np.zeros((P, NVEC), np.float32)

    def put(name, a):
        a = np.asarray(a).reshape(-1)
        n = -(-a.size // P)
        for i in range(n):
            part = a[i * P:(i + 1) * P]
            cols[:part.size, VEC[name] + i] = part

    for name, key in (("c", "c"), ("c_ctx", "c_ctx"), ("norm1", "norm1_w"), ("norm2", "norm2_w"), ("ada_b", "ada_b"),
                      ("lb_f", "hg_lb_fwd"), ("lb_b", "hg_lb_bwd"), ("hg_norm", "hg_norm_w"), ("hy_d", "hy_d"),
                      ("hy_norm", "hy_norm_w"), ("hy_conv", "hy_conv_w"), ("ffn_conv", "ffn_conv_w"),
                      ("b1", "hy_b1"), ("fr1", "hy_freq1"), ("b2", "hy_b2"), ("fr2", "hy_freq2")):
        put(name, x[key])

    def cut(w, r0, nr, c0, ncol):
        return w[r0:r0 + nr * P, c0:c0 + ncol].reshape(nr, P, ncol).transpose(1, 0, 2).reshape(P, nr * ncol)

    ada, w_in, w_out = x["ada_w"][0], x["w_in"][0], x["w_out"][0]
    up, down = x["ffn_w_up"][0], x["ffn_w_down"][0]
    slots = np.zeros((NSLOT, P, RAW * UNIT), np.float32)
    s = 0

    def slot(*parts):
        nonlocal s
        at = 0
        for p in parts:
            slots[s, :, at:at + p.shape[1]] = p
            at += p.shape[1]
        s += 1

    def ada_block(b):
        for i in range(2):
            slot(cut(ada, i * HW, 4, b * HW, HW))

    for b in range(ADA1 // 2):
        ada_block(b)
    for i in range(IV):
        slot(cut(w_in, i * HW, 4, 3 * HW, HW))
    for i in range(0, len(TILES), 2):
        slot(*[cut(w_in, 0, KD, tile_column(t), P) for t in TILES[i:i + 2]])
    for b in range(ADA1 // 2, (ADA1 + ADA2) // 2):
        ada_block(b)
    for n in range(2):
        for i in range(2):
            slot(cut(w_out, i * HW, 4, n * HW, HW))
    for b in range((ADA1 + ADA2) // 2, (ADA1 + ADA2 + ADA3) // 2):
        ada_block(b)
    for f0, nf in ROUNDS:
        for f in range(f0, f0 + nf):
            slot(cut(up, 0, KD, f * P, P), cut(up, 0, KD, F + f * P, P))
        for n in range(2):
            for f in range(f0, f0 + nf, 4):
                slot(cut(down, f * P, min(4, f0 + nf - f), n * HW, HW))
    return cols, slots


OUTS = [("y_prompt", (1, TP, D)), ("y_sample", (1, TS, D)), ("new_state", (1, 1, 2, HEADS, P, P))]


def kernel(**inputs):
    import concourse.bacc as bacc
    from concourse.bass_utils import run_bass_kernel_spmd

    x = {k: np.ascontiguousarray(a) for k, a in inputs.items()}
    given = {k: x[k] for k in ("x_prompt", "x_sample", "state_hgrn", "hy_w1", "hy_w2", "hy_w3", "final_norm_w")}
    given["vec"], given["slots"] = lay_out(x)
    given.update(constants())
    nc = bacc.Bacc("TRN2", target_bir_lowering=False, num_devices=1)
    io, arrays = {}, {}
    for name, a in given.items():
        arrays[f"in_{name}"] = np.ascontiguousarray(a)
        io[name] = nc.dram_tensor(f"in_{name}", a.shape, mybir.dt.from_np(a.dtype), kind="ExternalInput").ap()
    for name, shape in OUTS:
        io[name] = nc.dram_tensor(f"out_{name}", shape, F32, kind="ExternalOutput").ap()
    build(nc, io)
    r = run_bass_kernel_spmd(nc, [arrays], core_ids=[0])
    return tuple(r.results[0][f"out_{name}"] for name, _ in OUTS)
```

```python
import math
from contextlib import ExitStack

import numpy as np
import concourse.bass as bass
from concourse import mybir

F32 = mybir.dt.float32
F32R = mybir.dt.float32r
U32 = mybir.dt.uint32
U8 = mybir.dt.uint8
ALU = mybir.AluOpType
ACT = mybir.ActivationFunctionType

P = 128
D = 1024
KD = D // P
TS, TP = 512, 128
T = TS + TP
NT = T // P
HT = T // 2
GRID = 64
ROWS = TS // GRID
PADROW = GRID + 1
PADS = ROWS * PADROW
CONV = PADS + TP
PAD = CONV + 2
HEADS = 4
HW = 512
NC = HW // P
F = 2816
NF = F // P
NHID = 64
NEMB = 33
LEVELS = 7
EPS = 1e-6
SCALE = P ** -0.5
UNIT = 1024
RAW = 2
RAWS = 3
SPLITS = 3
ROUNDS = [(0, 8), (8, 8), (16, 6)]

VEC = {}
_at = 0
for _name, _n in (("c", KD), ("c_ctx", KD), ("norm1", KD), ("norm2", KD), ("ada_b", 6 * KD),
                  ("lb_f", NC), ("lb_b", NC), ("hg_norm", NC), ("hy_d", NC), ("hy_norm", NC),
                  ("hy_conv", 3 * 3 * NC), ("ffn_conv", 3 * 2 * NF),
                  ("b1", 1), ("fr1", 1), ("b2", 1), ("fr2", 1)):
    VEC[_name] = _at
    _at += _n
NVEC = _at

TILES, _hy = [], 0
for _g in range(HEADS):
    for _kind in ("q", "hy", "ff", "fb", "g", "hy"):
        TILES.append((_kind, _hy if _kind == "hy" else _g))
        _hy += _kind == "hy"
TILES += [("hy", _i) for _i in range(_hy, 3 * NC)]
STEPS = 12
FIRST_STEP = 9
DIAG, LEVEL0, KTURN, KV, OUT, NORM = 0, 1, 8, 9, 10, 11


def tile_column(tile):
    kind, i = tile
    if kind == "hy":
        return 5 * HW + (i % 3) * HW + (i // 3) * P
    return {"q": 0, "ff": 1, "fb": 2, "g": 4}[kind] * HW + i * P


FINE = (8, 9)
ADA_BLOCKS = (0, 1, 2, 3, 4, 5, 6, 7, 10, 11)
MIXED = 4 * len(FINE)
ADA1, IV, PROJ, ADA2, WOUT, ADA3 = 8, 4, MIXED - 4 + (len(TILES) - MIXED + 4) // 2, 8, 4, 4
SLOT_IV = ADA1
SLOT_PROJ = SLOT_IV + IV
SLOT_ADA2 = SLOT_PROJ + PROJ
SLOT_WOUT = SLOT_ADA2 + ADA2
SLOT_ADA3 = SLOT_WOUT + WOUT
SLOT_FFN = SLOT_ADA3 + ADA3
ADA_SLOTS = [*range(ADA1), *range(SLOT_ADA2, SLOT_WOUT), *range(SLOT_ADA3, SLOT_FFN)]
SLOT_UNITS = [RAW] * SLOT_FFN
for _f0, _nf in ROUNDS:
    SLOT_UNITS += [RAW] * _nf
    for _n in range(2):
        SLOT_UNITS += [min(4, _nf - f) // 2 for f in range(0, _nf, 4)]
NSLOT = len(SLOT_UNITS)
IS_ADA = [s in ADA_SLOTS for s in range(NSLOT)]
UNITS = [(s, u) for s in range(NSLOT) if not IS_ADA[s] for u in range(SLOT_UNITS[s])]
NU = len(UNITS)


def tile_unit(t):
    return 2 * (IV + t) if t < MIXED - IV else MIXED + IV + t


UNIT_WOUT = MIXED + IV + len(TILES)
UNIT_FFN = UNIT_WOUT + 2 * WOUT


def unit_last():
    out, plain, down = [], 0, 0

    def token_major(pairs, name, value):
        nonlocal plain
        for _ in range(pairs - 1):
            plain += 1
            out.append(("unit_done", plain))
        out.append((name, value))

    token_major(IV, "v_bank", NT)
    out.extend(("half_made", 2 * t + 2) for t in range(len(TILES)))
    for j in range(MIXED):
        out.insert(2 * j + 1, ("fine_used", j + 1))
    token_major(WOUT, "mixed", NT)
    token_major(WOUT, "mixed", 2 * NT)
    t = len(TILES)
    for _, nf in ROUNDS:
        out.extend(("half_made", 2 * (t + i) + 2) for i in range(2 * nf))
        t += 2 * nf
        for _ in range(2):
            down += NT
            token_major(nf // 2, "down_made", down)
    return out


UNIT_LAST = unit_last()
assert len(UNIT_LAST) == NU


def constants():
    c = {}
    c["ident"] = np.eye(P, dtype=np.float32)
    c["diag"] = (np.eye(P) * SCALE).astype(np.float32)
    i, j = np.arange(P)[:, None], np.arange(P)[None, :]
    c["masks"] = np.stack([((i >> (l + 1)) == (j >> (l + 1))) & ((i >> l) != (j >> l))
                           for l in range(LEVELS)], 1).astype(np.uint32)
    order = np.concatenate([np.arange(0, TS, 2), np.arange(1, TS, 2)])

    def feats(L, pos):
        t = np.linspace(0.0, 1.0, L, dtype=np.float32)[pos]
        bands = np.linspace(1e-4, 15, 16, dtype=np.float32)
        ang = (np.float32(2.0 * math.pi) * pos[:, None].astype(np.float32) * bands[None, :] / np.float32(L)).astype(np.float32)
        return t, np.concatenate([t[:, None], np.cos(ang), np.sin(ang)], 1)

    ts, fs = feats(TS, order)
    tp, fp = feats(TP, np.arange(TP))
    c["feats"] = np.ascontiguousarray(np.concatenate([fs, fp]).T.astype(np.float32))
    deltas = np.abs(np.linspace(math.log(1e-2) / 1.5, math.log(1e-2) / 0.3, HW, dtype=np.float32))
    dec = np.exp(-np.concatenate([ts, tp])[:, None] * deltas[None, :]).astype(np.float32)
    c["decay"] = np.ascontiguousarray(dec.reshape(NT, P, HW).transpose(1, 0, 2))

    th = math.pi * (2 * np.arange(TS // 2) + 1) / (2 * TS)
    n = order.reshape(2, 2, P)

    def tab(shift):
        a = n[..., None] * th if not shift else (n[..., None] + 0.5) * th
        return np.stack([np.cos(a), np.sin(a)], 0)

    c["ktab"] = np.ascontiguousarray(tab(0).transpose(3, 0, 1, 2, 4).astype(np.float32))
    c["utab"] = np.ascontiguousarray(tab(1).transpose(3, 0, 1, 2, 4).astype(np.float32))
    inv = tab(1).reshape(2, 2, 2 * P, 2, P) / TS
    c["itab"] = np.ascontiguousarray(inv.transpose(4, 3, 0, 1, 2).astype(np.float32))
    tg = math.pi * (2 * np.arange(TP) + 1) / (2 * TP)
    m = np.arange(TP)
    k = np.stack([np.cos(m[:, None] * tg), np.sin(m[:, None] * tg)], 1)
    u = np.stack([np.cos((m[:, None] + 0.5) * tg), np.sin((m[:, None] + 0.5) * tg)], 1)
    v = (u.transpose(2, 1, 0)) / TP
    c["ptab"] = np.ascontiguousarray(np.stack([k, u, v], 1).astype(np.float32))
    return c




def ap(t, offset, dims):
    base = t[:]
    return bass.AP(tensor=base.tensor, offset=offset, ap=[base.ap[0], *[list(d) for d in dims]])


def build(nc, io):
    ctx = ExitStack()

    def sb(stack, name, shape, dt=F32):
        return stack.enter_context(nc.sbuf_tensor(name, [P, *shape], dt))

    sems = {}

    def sem(name):
        if name not in sems:
            sems[name] = ctx.enter_context(nc.semaphore(name))
        return sems[name]

    with ctx:
        raw = sb(ctx, "raw", [RAWS, RAW * UNIT])
        w_hi = sb(ctx, "w_hi", [SPLITS, UNIT], F32R)
        w_lo = sb(ctx, "w_lo", [SPLITS, UNIT], F32R)
        h_hi = sb(ctx, "h_hi", [KD, T], F32R)
        h_lo = sb(ctx, "h_lo", [KD, T], F32R)
        vec = sb(ctx, "vec", [NVEC])
        ident = sb(ctx, "ident", [P])
        ones = sb(ctx, "ones", [P])
        eps = sb(ctx, "eps", [1])
        silu_c = sb(ctx, "silu_c", [KD, 2])
        silu_parts = sb(ctx, "silu_parts", [KD, 4], F32R)
        mod = sb(ctx, "mod", [6 * KD, 2])
        gain = sb(ctx, "gain", [2, KD, 2])
        bound = sb(ctx, "bound", [5, 2 * NC])
        stat = sb(ctx, "stat", [3, 2, NT])
        knorm = sb(ctx, "knorm", [2, 2 * NC])

        mid = ExitStack()
        kspec = sb(mid, "kspec", [2, 2, 2, HW])
        kspec_p = sb(mid, "kspec_p", [2, HW])

        early = ExitStack()
        xin = sb(early, "xin", [NT, D])
        hfull = sb(early, "hfull", [2, T])
        feats = sb(early, "feats", [T])
        w1 = sb(early, "w1", [NHID])
        w2 = sb(early, "w2", [NHID])
        w3 = sb(early, "w3", [2 * HW])
        hid = sb(early, "hid", [2, T])
        arg = sb(early, "arg", [2, T])
        decay = sb(early, "decay", [NT, HW])
        filt = sb(early, "filt", [2, NT, HW])
        ktab = sb(early, "ktab", [2, 2, 2, 2 * P])
        ptab_k = sb(early, "ptab_k", [2, TP])
        tapsum = sb(early, "tapsum", [2, HW])
        row_e = sb(early, "row_e", [2, HW])
        part = sb(early, "part", [2, HW])
        early.close()

        o_hg = sb(mid, "o_hg", [NC, T])
        x2 = sb(mid, "x2", [NC, CONV])
        u_hy = sb(mid, "u_hy", [NC, T])
        hg = ExitStack()
        eyes = sb(hg, "eyes", [P])
        masks = sb(hg, "masks", [LEVELS, P], U8)
        qs = sb(hg, "qs", [T])
        KK = sb(hg, "KK", [2, T])
        kc = sb(hg, "kc", [2, T])
        vtok = sb(hg, "vtok", [NT, HW])
        state0 = sb(hg, "state0", [2, HEADS, P])
        QQ = sb(hg, "QQ", [2, T])
        TT = [sb(hg, "TT", [2 * T]), sb(hg, "TU", [T])]
        kdiag = kc[:, 1, :]
        scores = sb(hg, "scores", [T])
        ktok = sb(hg, "ktok", [2, 4, P])
        states = sb(hg, "states", [2, 3, P])
        newst = sb(hg, "newst", [2, P])
        padm = sb(hg, "padm", [2, PAD])
        cv = sb(hg, "cv", [2, CONV])
        gs = sb(hg, "gs", [2, T])
        hg.close()
        hy = ExitStack()
        utab = sb(hy, "utab", [2, 2, 2, 2 * P])
        itab = sb(hy, "itab", [2, 2, 2, 2 * P])
        ptab = sb(hy, "ptab", [2, 2, TP])
        ut = sb(hy, "ut", [NT, HW])
        U = sb(hy, "U", [2, 2, 2, HW])
        Up = sb(hy, "Up", [2, HW])
        prod = sb(hy, "prod", [2, 2, HW])
        zc = sb(hy, "zc", [CONV])
        sq = sb(hy, "sq", [CONV])
        row_h = sb(hy, "row_h", [2, HW])
        hy.close()
        mid.close()

        late = ExitStack()
        x1 = sb(late, "x1", [NT, D])
        grow = sb(late, "grow", [2, 2, D])
        fnw = sb(late, "fnw", [D])
        tmpd = sb(late, "tmpd", [HW])
        norm2 = ExitStack()
        xn = sb(norm2, "xn", [NT, D])
        hf2 = sb(norm2, "hf2", [2, T])
        row_l = sb(norm2, "row_l", [2, HW])
        norm2.close()
        a_hi = sb(late, "a_hi", [8, T], F32R)
        a_lo = sb(late, "a_lo", [8, T], F32R)
        padf = sb(late, "padf", [2, 2, PAD])
        cf = sb(late, "cf", [2, CONV])
        actf = sb(late, "actf", [T])
        late.close()

        ps = ctx.enter_context(nc.psum_tensor("ps", [P, 8, 512], F32))

        def v(name, i=0, n=1):
            return vec[:, VEC[name] + i:VEC[name] + i + n]

        def banks(b, n=T, off=0):
            return ap(ps, b * 512 + off, [(1, n)])

        def linker(eng, own):
            count = {}

            def link(ins, name=None):
                name = name or own
                count[name] = count.get(name, 0) + 1
                ins.then_inc(sem(name), 1)
                eng.wait_ge(sem(name), count[name])
            return link

        def arrived(eng, s):
            eng.wait_ge(sem(f"raw_in{s % RAWS}"), 16 * (s // RAWS + 1))

        def unit_free(eng, n):
            name, value = UNIT_LAST[n]
            eng.wait_ge(sem(name), value)

        ada_before = [sum(IS_ADA[:s + 1]) for s in range(NSLOT)]
        units_before = [sum(SLOT_UNITS[i] for i in range(s + 1) if not IS_ADA[i]) for s in range(NSLOT)]
        NH = 2 * len(TILES)

        def half_bank(n):
            return n % 4 if n < NH else 5 + (n - NH) % 3

        def step_at(n):
            return divmod(n - FIRST_STEP, STEPS) if FIRST_STEP <= n < FIRST_STEP + HEADS * STEPS else None

        ADA_ROWS = [row_e] * 4 + [row_h] * 4 + [row_l] * 2
        ROW_BANK = (2, 2, 0, 1, 6, 5, 6, 5, 6, 5)
        V_BANKS = (2, 3, 0, 1, 4)

        def fine_rows(f):
            return ap(ktok, f * HW, [(1, HW)])[0:4]

        def ahead(n):
            t = n // 2
            if t <= MIXED - IV:
                return (tile_unit(t) + 1, tile_unit(t) + 2)
            return (tile_unit(t) + 2,) if t < len(TILES) - 2 else ()

        def sizes(i):
            return ap((part, arg)[i % 2], 0, [(HW, 2), (1, HW)])

        def score_bank(j):
            return 6 if j and j % 2 else 4

        def y_parts(i):
            return (slice(0, HW), slice(HW, D)) if i == NT - 1 else (slice(0, D),)

        def x_rows(i):
            return io["x_sample"][0][i * P:(i + 1) * P, :] if i < TS // P else io["x_prompt"][0]

        block = ctx.enter_context(nc.Block())

        @block.sync
        def _(eng):
            def load(dst, src, name):
                eng.dma_start(dst, src).then_inc(sem(name), 16)

            def slot(s):
                if s >= RAWS:
                    o = s - RAWS
                    if IS_ADA[o]:
                        eng.wait_ge(sem("ada_used"), ada_before[o])
                    else:
                        eng.wait_ge(sem("hi_ready"), units_before[o])
                        eng.wait_ge(sem("lo_ready"), units_before[o])
                n = SLOT_UNITS[s] * UNIT
                load(raw[:, s % RAWS, 0:n], io["slots"][s, :, 0:n], f"raw_in{s % RAWS}")

            def store_state(h):
                eng.wait_ge(sem("new_states"), h + 1)
                load(io["new_state"][0, 0].rearrange("d h k w -> h k d w")[h], newst[:, :, :], "stored")

            load(feats[0:NEMB, :], io["feats"], "ld_filt")
            load(w1[0:NEMB, :], io["hy_w1"][0], "ld_filt")
            load(vec[:, :], io["vec"], "ld_vec")
            slot(0)
            load(w2[0:NHID, :], io["hy_w2"][0], "ld_hid")
            load(w3[0:NHID, :], io["hy_w3"][0], "ld_hid")
            for s in range(1, RAWS):
                slot(s)
            load(ident[:, :], io["ident"], "ld_ident")
            load(decay[:, :, :], io["decay"], "ld_decay")
            for s in range(RAWS, 2 * RAWS):
                slot(s)
            for i in range(NT):
                load(xin[:, i, :], x_rows(i), f"ld_x{i}")
            for s in range(2 * RAWS, ADA1):
                slot(s)
            load(ktab[:, :, :, :, :], io["ktab"], "ld_ktab")
            load(ptab_k[:, :, :], io["ptab"][:, 0], "ld_ktab")
            for s in range(ADA1, ADA1 + RAWS):
                slot(s)
            eng.wait_ge(sem("h_split"), KD)
            eng.wait_ge(sem("kspec_ready"), 5)
            load(ap(QQ, 0, [(P, LEVELS), (1, P)]).bitcast(U32), io["masks"], "ld_hg")
            load(eyes[:, :], io["diag"], "ld_hg")
            load(state0[:, :, :, :], io["state_hgrn"][0, 0].rearrange("d h k w -> k d h w"), "ld_hg")
            for s in range(ADA1 + RAWS, SLOT_ADA2 + 2):
                slot(s)
                if s - SLOT_PROJ in (10, 13):
                    store_state((s - SLOT_PROJ - 10) // 3)
            store_state(2)
            eng.wait_ge(sem("head_steps"), (HEADS - 1) * STEPS + KTURN + 1)
            eng.wait_ge(sem("scores_taken"), HEADS * 8)
            load(utab[:, :, :, :, :], io["utab"], "ld_utab")
            store_state(HEADS - 1)
            eng.wait_ge(sem("head_steps"), (HEADS - 1) * STEPS + OUT + 1)
            load(itab[:, :, :, :, :], io["itab"], "ld_itab")
            load(ptab[:, :, :, :], io["ptab"][:, 1:3], "ld_itab")
            for s in range(SLOT_ADA2 + 2, SLOT_WOUT + WOUT):
                slot(s)
            eng.wait_ge(sem("merged"), 2)
            eng.wait_ge(sem("ada_cols"), 8)
            for i in range(NT):
                load(x1[:, i, :], x_rows(i), "ld_res")
            load(fnw[:, :], io["final_norm_w"].partition_broadcast(P), "ld_fnw")
            for s in range(SLOT_WOUT + WOUT, NSLOT):
                slot(s)
            stores = [(i, cols) for i in range(NT) for cols in y_parts(i)]
            for n, (i, cols) in enumerate(stores):
                eng.wait_ge(sem("y_ready"), n + 1)
                dst = io["y_sample"][0][i * P:(i + 1) * P, cols] if i < TS // P else io["y_prompt"][0][:, cols]
                load(dst, x1[:, i, cols], "stored")
            eng.wait_ge(sem("stored"), 16 * (len(stores) + HEADS))

        @block.scalar
        def _(eng):
            link = linker(eng, "act_own")
            A = nc.scalar.activation

            def split_hi(n):
                if n >= NU:
                    return
                s, u = UNITS[n]
                arrived(eng, s)
                if n >= SPLITS:
                    unit_free(eng, n - SPLITS)
                A(w_hi[:, n % SPLITS, :], raw[:, s % RAWS, u * UNIT:(u + 1) * UNIT],
                  ACT.Copy).then_inc(sem("hi_ready"), 1)

            def spread(src, pad, half, name):
                if half == 0:
                    A(pad[:, 1:1 + 5 * PADROW].rearrange("p (r c) -> p r c", c=PADROW)[:, :, 0:GRID],
                      src.rearrange("p (r c) -> p r c", c=GRID), ACT.Copy).then_inc(sem(name), 1)
                else:
                    A(pad[:, 1 + 5 * PADROW:1 + PADS].rearrange("p (r c) -> p r c", c=PADROW)[:, :, 0:GRID],
                      src[:, 0:3 * GRID].rearrange("p (r c) -> p r c", c=GRID), ACT.Copy)
                    A(pad[:, 1 + PADS:1 + CONV], src[:, 3 * GRID:HT], ACT.Copy).then_inc(sem(name), 1)

            def ada_row(b):
                eng.wait_ge(sem("ada_used"), 2 * b + 2)
                if b >= 2:
                    eng.wait_ge(sem("ada_cols"), b - 1)
                A(ADA_ROWS[b][0:2, b % 2, :], ps[0:2, ROW_BANK[b], :], ACT.Copy).then_inc(sem("ada_row"), 1)

            def row_norm(which, i, x, junk):
                link(A(ap(junk, 0, [(1, D)]), x[:, i, :], ACT.Square, accum_out=stat[:, which, 0, i:i + 1]))
                A(stat[:, which, 1, i:i + 1], stat[:, which, 0, i:i + 1], ACT.Sqrt, scale=1.0 / D,
                  bias=eps[:, :]).then_inc(sem("norm_ready"), 1)

            def modulate(which, k):
                buf, sh, b = (hfull, hf2)[which], 3 * KD * which + k, 2 * (k % 2)
                eng.wait_ge(sem("h_turned"), KD * which + k + 1)
                if k >= 2:
                    eng.wait_ge(sem("h_split"), KD * which + k - 1)
                A(buf[:, k % 2, 0:TS], ps[:, b, :], ACT.Identity,
                  scale=gain[:, which, k, 0:1], bias=mod[:, sh, 0:1])
                A(buf[:, k % 2, TS:T], ps[:, b + 1, 0:TP], ACT.Identity,
                  scale=gain[:, which, k, 1:2], bias=mod[:, sh, 1:2]).then_inc(sem("h_full"), 1)

            eng.wait_ge(sem("ones_ready"), 2)
            eng.wait_ge(sem("ld_vec"), 16)
            A(silu_c[:, :, 0], v("c", 0, KD), ACT.Silu)
            A(silu_c[:, :, 1], v("c_ctx", 0, KD), ACT.Silu).then_inc(sem("silu_c"), 1)
            eng.wait_ge(sem("bound_in"), 1)
            A(bound[:, 1, :], bound[:, 0, :], ACT.Exp).then_inc(sem("bound_exp"), 1)
            for i in range(2):
                eng.wait_ge(sem("arg_ready"), i + 1)
                A(hid[0:NHID, i, :], arg[0:NHID, 0, :], ACT.Sin).then_inc(sem("hid_ready"), 1)
                if i == 0:
                    ada_row(0)

            def tap_sizes(i):
                eng.wait_ge(sem("taps_ready"), i + 1)
                if i >= 2:
                    eng.wait_ge(sem("sides_ready"), i - 1)
                A(sizes(i), filt[:, :, i, :], ACT.Abs).then_inc(sem("abs_ready"), 1)

            def norm1(i):
                eng.wait_ge(sem(f"ld_x{i}"), 16)
                row_norm(0, i, xin, hfull)

            tap_sizes(0)
            tap_sizes(1)
            tap_sizes(2)
            ada_row(1)
            tap_sizes(3)
            norm1(0)
            tap_sizes(4)
            norm1(1)
            ada_row(2)
            for i in range(2, NT):
                norm1(i)
            ada_row(3)
            split_hi(0)
            split_hi(1)
            eng.wait_ge(sem("gain_ready"), 1)
            def take_odd(n):
                cs = n % 2
                eng.wait_ge(sem("kdft"), (1, 2, 3, 5)[n])
                if n >= 2:
                    eng.wait_ge(sem("kspec_ready"), n - 1)
                A(part[:, cs, :], ps[:, 4 + 2 * cs + 1, :], ACT.Copy).then_inc(sem("kodd"), 1)

            for k in range(KD):
                modulate(0, k)
                if k == 4:
                    take_odd(0)
            for n in range(1, 4):
                take_odd(n)
            for n in range(2, 2 * IV + 1):
                split_hi(n)
            eng.wait_ge(sem("kspec_ready"), 5)
            for i in range(NT):
                eng.wait_ge(sem("v_bank"), i + 1)
                A(vtok[:, i, :], ps[:, V_BANKS[i], :], ACT.Copy).then_inc(sem("v_ready"), 1)

            def fine_row(f):
                eng.wait_ge(sem("fine_used"), 4 * f + 4)
                A(fine_rows(f), ps[0:4, 6 + f, :], ACT.Copy).then_inc(sem("fine_row"), 1)

            fine_row(0)

            def step(h, j):
                if j < KTURN - 1:
                    eng.wait_ge(sem("k_next"), 8 * h + j + 1)
                    if j:
                        eng.wait_ge(sem("head_steps"), h * STEPS + j)
                    A(kc[:, j % 2, :], ap(KK, 0, [(2 << j, T >> (j + 1)), (T + (1 << j), 2), (1, 1 << j)]),
                      ACT.Copy).then_inc(sem("kc_ready"), 1)
                if j == KTURN:
                    eng.wait_ge(sem("head_steps"), h * STEPS + KTURN + 1)
                    A(ktok[:, :, :, :], banks(4, 2 * 512), ACT.Copy).then_inc(sem("ktok_ready"), 1)
                if j == OUT:
                    eng.wait_ge(sem("head_steps"), h * STEPS + OUT + 1)
                    A(o_hg[:, h, :], banks(6), ACT.Square).then_inc(sem("osq_ready"), 1)
                if j == NORM:
                    eng.wait_ge(sem("head_steps"), h * STEPS + NORM + 1)
                    A(o_hg[:, h, :], banks(4), ACT.Sqrt, scale=1.0 / P, bias=eps[:, :]).then_inc(sem("rms_ready"), 1)

            for n in range(NH):
                kind, i = TILES[n // 2]
                half = n % 2
                c0 = half * HT
                src = ps[:, half_bank(n), 0:HT]
                if half == 0:
                    for unit in ahead(n):
                        split_hi(unit)
                if n == 2 * (MIXED - IV):
                    fine_row(1)
                eng.wait_ge(sem("half_made"), n + 1)
                if kind == "q":
                    if i:
                        eng.wait_ge(sem("head_steps"), (i - 1) * STEPS + DIAG + 1)
                    A(qs[:, c0:c0 + HT], src, ACT.Silu).then_inc(sem("half_free"), 1)
                elif kind == "g":
                    if i >= 2:
                        eng.wait_ge(sem("heads_done"), i - 1)
                    A(gs[:, i % 2, c0:c0 + HT], src, ACT.Silu).then_inc(sem("half_free"), 1)
                elif kind in ("ff", "fb"):
                    d = int(kind == "ff")
                    if i:
                        eng.wait_ge(sem("scores_taken"), (i - 1) * 8 + 8)
                        eng.wait_ge(sem("head_steps"), (i - 1) * STEPS + KTURN + 1)
                    A(TT[0][:, d * T + c0:d * T + c0 + HT], src, ACT.Sigmoid)
                    A(KK[:, 1 - d, c0:c0 + HT], src, ACT.Sigmoid, scale=-1.0).then_inc(sem("half_free"), 1)
                else:
                    if i < 2:
                        eng.wait_ge(sem("pad_zero"), 1)
                    else:
                        eng.wait_ge(sem("hy_conv"), i - 1)
                    spread(src, padm[:, i % 2, :], half, "half_free")
                if step_at(n):
                    step(*step_at(n))
            def take_u(i):
                eng.wait_ge(sem("u_turned"), i + 1)
                A(ut[:, i, :], ps[:, i, :], ACT.Copy).then_inc(sem("ut_ready"), 1)

            for n in range(NH, FIRST_STEP + HEADS * STEPS):
                if step_at(n)[1] == NORM:
                    for i in range(4):
                        take_u(i)
                step(*step_at(n))
            take_u(4)
            eng.wait_ge(sem("heads_done"), HEADS)
            eng.wait_ge(sem("hy_conv"), 3 * NC)
            eng.wait_ge(sem("stored"), 16 * HEADS)
            for m in range(2):
                for cs in range(2):
                    n = 2 * m + cs
                    eng.wait_ge(sem("udft"), n + 1)
                    if m:
                        eng.wait_ge(sem("uspec_ready"), n - 1)
                    A(prod[:, cs, 0, :], ps[:, 4 * m + 2 * cs + 1, :], ACT.Copy).then_inc(sem("uodd"), 1)
            eng.wait_ge(sem("udft"), 5)
            A(Up[:, :, :], banks(0, 2 * 512), ACT.Copy).then_inc(sem("up_ready"), 1)
            for b in range(4, 8):
                ada_row(b)
            for c in range(NC):
                b = 2 * (c % 2)
                eng.wait_ge(sem("z_made"), c + 1)
                if c:
                    eng.wait_ge(sem("yhy_ready"), c)
                else:
                    eng.wait_ge(sem("zc_zero"), 1)
                A(ap(zc, 0, [(1, 2), (PADROW, ROWS), (2, GRID // 2)]),
                  ps[:, b, :].rearrange("p (e r c) -> p e r c", e=2, r=ROWS), ACT.Copy, scale=knorm[:, 1, c:c + 1])
                A(zc[:, PADS:CONV], ps[:, b + 1, 0:TP], ACT.Copy,
                  scale=knorm[:, 1, NC + c:NC + c + 1]).then_inc(sem("z_ready"), 1)
                eng.wait_ge(sem("yhy_ready"), c + 1)
                if c:
                    eng.wait_ge(sem("ysq_used"), c)
                A(sq[:, :], x2[:, c, :], ACT.Square).then_inc(sem("ysq_ready"), 1)
                if c < 2:
                    split_hi(UNIT_WOUT + c)
            eng.wait_ge(sem("ysq_used"), NC)
            A(ap(sq, 0, [(CONV // 2, 2), (1, CONV // 2)]), ap(ps, 4 * 512, [(512, 2), (1, CONV // 2)]), ACT.Sqrt,
              scale=1.0 / HW, bias=eps[:, :]).then_inc(sem("rms_ready"), 1)

            def gate_row(r):
                eng.wait_ge(sem("row_made"), r + 1)
                A(grow[:, r // 4, (r // 2) % 2, (r % 2) * 512:(r % 2 + 1) * 512], ps[:, 5 + r % 3, :],
                  ACT.Copy).then_inc(sem("row_ready"), 1)

            split_hi(UNIT_WOUT + 2)
            split_hi(UNIT_WOUT + 3)
            eng.wait_ge(sem("merged"), 2)
            for r in range(4):
                gate_row(r)
            for n in range(4, 2 * WOUT):
                split_hi(UNIT_WOUT + n)
            for i in range(NT):
                eng.wait_ge(sem("x1_ready"), NT + i + 1)
                row_norm(1, i, x1, hf2)
                if i == 2:
                    ada_row(8)
            split_hi(UNIT_FFN)
            split_hi(UNIT_FFN + 1)
            ada_row(9)
            eng.wait_ge(sem("gain_ready"), 2)
            for k in range(KD):
                modulate(1, k)
                if k in (1, 2, 3, 5):
                    gate_row((4, 5, 6, 0, 7)[k - 1])
            eng.wait_ge(sem("padf_zero"), 1)
            unit, t = UNIT_FFN, 0
            for r, (f0, nf) in enumerate(ROUNDS):
                for f in range(nf):
                    for gv in range(2):
                        split_hi(unit + 2)
                        unit += 1
                        for half in range(2):
                            n = NH + 4 * t + 2 * gv + half
                            eng.wait_ge(sem("half_made"), n + 1)
                            if t >= 2 and half == 0:
                                eng.wait_ge(sem("fconv"), 2 * (t - 2) + gv + 1)
                            spread(ps[:, half_bank(n), 0:HT], padf[:, t % 2, gv, :], half, "half_free")
                        if gv == 0:
                            eng.wait_ge(sem("fconv"), 2 * t + 1)
                            A(cf[:, 0, :], cf[:, 0, :], ACT.Silu).then_inc(sem("silu_done"), 1)
                    eng.wait_ge(sem("act_ready"), t + 1)
                    if r and f == 0:
                        eng.wait_ge(sem("down_made"), 2 * r * NT)
                    A(a_hi[:, f, :], actf[:, :], ACT.Copy).then_inc(sem("ahi_ready"), 1)
                    t += 1
                for k in range(nf):
                    split_hi(unit + 2)
                    unit += 1
            for i in range(NT):
                eng.wait_ge(sem("down_added"), 4 * NT + i + 1)
                link(A(ap(cf, 0, [(1, HW)]), x1[:, i, 0:HW], ACT.Square, accum_out=stat[:, 2, 0, i:i + 1]))
                link(A(stat[:, 0, 0, i:i + 1], stat[:, 2, 0, i:i + 1], ACT.Identity, scale=1.0 / D, bias=eps[:, :]))
            for i in range(NT):
                eng.wait_ge(sem("down_added"), 5 * NT + i + 1)
                link(A(ap(cf, 0, [(1, HW)]), x1[:, i, HW:D], ACT.Square, accum_out=stat[:, 0, 1, i:i + 1]))
                A(stat[:, 2, 1, i:i + 1], stat[:, 0, 1, i:i + 1], ACT.Sqrt, scale=1.0 / D,
                  bias=stat[:, 0, 0, i:i + 1]).then_inc(sem("norm_ready"), 1)

        @block.vector
        def _(eng):
            link = linker(eng, "dve_own")
            V = nc.vector

            def split_lo(n):
                if n >= NU:
                    return
                s, u = UNITS[n]
                eng.wait_ge(sem("hi_ready"), n + 1)
                if n >= SPLITS:
                    unit_free(eng, n - SPLITS)
                V.tensor_tensor(w_lo[:, n % SPLITS, :], raw[:, s % RAWS, u * UNIT:(u + 1) * UNIT],
                                w_hi[:, n % SPLITS, :].bitcast(F32), ALU.subtract).then_inc(sem("lo_ready"), 1)

            def split_h(which, k):
                buf = (hfull, hf2)[which][:, k % 2, :]
                eng.wait_ge(sem("h_full"), KD * which + k + 1)
                link(V.tensor_copy(h_hi[:, k, :], buf))
                link(V.tensor_tensor(h_lo[:, k, :], buf, h_hi[:, k, :].bitcast(F32), ALU.subtract), "h_split")

            def conv(pad, out, taps, name=None):
                link(V.tensor_scalar(out, pad[:, 1:1 + CONV], taps[1], None, ALU.mult))
                link(V.scalar_tensor_tensor(out=out, in0=pad[:, 0:CONV], scalar=taps[0], in1=out,
                                            op0=ALU.mult, op1=ALU.add))
                link(V.scalar_tensor_tensor(out=out, in0=pad[:, 2:2 + CONV], scalar=taps[2], in1=out,
                                            op0=ALU.mult, op1=ALU.add), name)

            V.memset(ones[:, :], 1.0).then_inc(sem("ones_ready"), 1)
            V.memset(eps[:, :], EPS).then_inc(sem("ones_ready"), 1)
            eng.wait_ge(sem("ld_vec"), 16)
            lb = v("lb_f", 0, 2 * NC)
            link(V.tensor_tensor(bound[:, 0, :], lb, lb, ALU.subtract), "bound_in")
            eng.wait_ge(sem("bound_exp"), 1)
            link(V.reciprocal(bound[:, 2, :], bound[:, 1, :]))
            link(V.tensor_tensor(bound[:, 2, :], bound[:, 1, :], bound[:, 2, :], ALU.mult))
            link(V.tensor_tensor(bound[:, 3, :], bound[:, 2, :], bound[:, 2, :], ALU.subtract))
            link(V.tensor_scalar(bound[:, 4, :], bound[:, 3, :], -1.0, 1.0, ALU.mult, ALU.add))

            eng.wait_ge(sem("silu_c"), 1)
            link(V.tensor_copy(silu_parts[:, :, 0:2], silu_c[:, :, :]))
            link(V.tensor_tensor(silu_parts[:, :, 2:4], silu_c[:, :, :], silu_parts[:, :, 0:2].bitcast(F32), ALU.subtract))

            two_pi = 2.0 * math.pi
            c1 = 6.28125
            c2 = float(np.float32(two_pi - c1))
            c3 = two_pi - c1 - c2
            a, q = arg[0:NHID, 0, :], arg[0:NHID, 1, :]
            for i in range(2):
                eng.wait_ge(sem("hid_made"), i + 1)
                if i:
                    eng.wait_ge(sem("hid_ready"), i)
                link(V.tensor_scalar(a, banks(0)[0:NHID, :], v(f"b{i + 1}")[0:NHID, :],
                                     v(f"fr{i + 1}")[0:NHID, :], ALU.add, ALU.mult))
                link(V.tensor_scalar(q, a, 1.0 / two_pi, 12582912.0, ALU.mult, ALU.add))
                link(V.tensor_scalar(q, q, 12582912.0, None, ALU.subtract))
                for cc in (c1, c2, c3):
                    link(V.scalar_tensor_tensor(out=a, in0=q, scalar=-cc, in1=a, op0=ALU.mult, op1=ALU.add))
                link(V.tensor_scalar(a, a, -3.1415925, 3.1415925, ALU.max, ALU.min), "arg_ready")
            eng.wait_ge(sem("ld_decay"), 16)
            def damp(i):
                eng.wait_ge(sem("taps_made"), i + 1)
                b, first = 4 + 2 * (i % 2), i in (0, NT - 1)
                link(V.tensor_tensor(filt[:, :, i, :], ps[:, b:b + 2, :],
                                     ap(decay, i * HW, [(0, 2), (1, HW)]), ALU.mult), None if first else "taps_ready")
                if first:
                    link(V.memset(filt[0:1, 1, i, :], 0.0), "taps_ready")

            def sides(i):
                link(V.tensor_tensor(decay[:, i, :], filt[:, 0, i, :], filt[:, 1, i, :], ALU.subtract))
                eng.wait_ge(sem("abs_ready"), i + 1)
                link(V.tensor_tensor(filt[:, 0, i, :], filt[:, 0, i, :], filt[:, 1, i, :], ALU.add))
                total, size = tapsum[:, i // (NT - 1), :], (part, arg)[i % 2]
                forth, back = ap(size, 0, [(1, HW)]), ap(size, HW, [(1, HW)])
                if i not in (0, NT - 1):
                    link(V.tensor_tensor(total, forth, total, ALU.add))
                    forth = total
                link(V.tensor_tensor(total, forth, back, ALU.add), "sides_ready")

            damp(0)
            for i in range(NT):
                if i + 1 < NT:
                    damp(i + 1)
                sides(i)
            for i in range(NT):
                eng.wait_ge(sem("norm_ready"), i + 1)
                link(V.reciprocal(stat[:, 0, 1, i:i + 1], stat[:, 0, 1, i:i + 1]))
                link(V.tensor_scalar(xin[:, i, :], xin[:, i, :], stat[:, 0, 1, i:i + 1], None, ALU.mult), "x_scaled")
            eng.wait_ge(sem("tapsums"), 1)
            link(V.tensor_scalar(knorm[:, 0, :], ps[:, 4, 0:2 * NC], EPS, None, ALU.add))
            link(V.reciprocal(knorm[:, 1, :], knorm[:, 0, :]), "knorm_ready")
            eng.wait_ge(sem("ada_cols"), 4)
            link(V.tensor_tensor(mod[:, 0:2 * KD, :], ap(ps, 3 * 512, [(2, 2 * KD), (1, 2)]),
                                 ap(vec, VEC["ada_b"], [(1, 2 * KD), (0, 2)]), ALU.add))
            link(V.scalar_tensor_tensor(out=gain[:, 0, :, :], in0=mod[:, KD:2 * KD, :], scalar=1.0,
                                        in1=ap(vec, VEC["norm1"], [(1, KD), (0, 2)]), op0=ALU.add, op1=ALU.mult), "gain_ready")
            def join(n):
                m, cs = 1 - n // 2, n % 2
                eng.wait_ge(sem("kodd"), n + 1)
                even = ps[:, 4 + 2 * cs, :]
                link(V.tensor_tensor(kspec[:, m, 0, cs, :], even, part[:, cs, :], ALU.add))
                first, second = (even, part[:, 0, :]) if cs == 0 else (part[:, 1, :], even)
                link(V.tensor_tensor(kspec[:, m, 1, cs, :], first, second, ALU.subtract), "kspec_ready")

            for k in range(KD):
                split_h(0, k)
                if k == 4:
                    join(0)
            for n in range(1, 4):
                if n == 3:
                    eng.wait_ge(sem("kdft"), 4)
                    link(V.tensor_copy(kspec_p[:, :, :], ps[:, 0:2, :]), "kspec_ready")
                join(n)
                if n < 3:
                    split_lo(n - 1)
            for n in range(2, 2 * IV + 1):
                split_lo(n)

            def bound_gates(h, d):
                t0 = TT[0][:, (1 - d) * T:(2 - d) * T]
                fb = NC * d + h
                link(V.tensor_scalar(t0, t0, bound[:, 4, fb:fb + 1], bound[:, 3, fb:fb + 1], ALU.mult, ALU.add))
                link(V.tensor_scalar(KK[:, d, :], KK[:, d, :], bound[:, 4, fb:fb + 1], None, ALU.mult),
                     "k_next" if d else None)

            def start_head(h):
                link(V.tensor_tensor(kdiag, KK[:, 0, :], KK[:, 1, :], ALU.add))
                if h:
                    eng.wait_ge(sem("head_steps"), (h - 1) * STEPS + OUT + 1)
                link(V.scalar_tensor_tensor(out=QQ[:, :, :], in0=ap(qs, 0, [(0, 2), (1, T)]), scalar=SCALE,
                                            in1=ap(TT[0], 0, [(T, 2), (1, T)]), op0=ALU.mult, op1=ALU.mult), "qk_next")

            def pass_k(h, j):
                if not LEVEL0 <= j < KTURN:
                    return
                l = j - LEVEL0
                s, t = 1 << l, TT[l % 2]
                nb, n = T // (2 * s), T // s
                both = ap(KK, 0, [(2 * s, nb), (T + s, 2), (1, s)])
                eng.wait_ge(sem("kc_ready"), LEVELS * h + l + 1)
                link(V.tensor_tensor(both, both, ap(t, n + 1, [(2, nb), (-n - 1, 2), (0, s)]), ALU.mult), "k_next")

            def take_level(h, j):
                if j == DIAG:
                    eng.wait_ge(sem("head_steps"), h * STEPS + j + 1)
                    link(V.tensor_tensor(scores[:, :], banks(score_bank(j)), ap(eyes, 0, [(0, NT), (1, P)]), ALU.mult), "scores_taken")
                    return
                l = j - LEVEL0
                s = 1 << l
                nb, n = T // (2 * s), T // s
                t, t2 = TT[l % 2], TT[(l + 1) % 2]
                both = [(2 * s, nb), (T + s, 2), (1, s)]
                eng.wait_ge(sem("head_steps"), h * STEPS + j + 1)
                link(V.tensor_tensor(ap(QQ, 0, both), ap(QQ, 0, both), ap(t, 1, [(2, nb), (n - 1, 2), (0, s)]), ALU.mult), "qk_next")
                link(V.tensor_tensor(ap(t2, 0, [(nb, 2), (1, nb)]), ap(t, 0, [(n, 2), (2, nb)]),
                                     ap(t, 1, [(n, 2), (2, nb)]), ALU.mult))
                link(V.copy_predicated(scores[:, :], ap(masks, l * P, [(0, NT), (1, P)]), banks(score_bank(j))), "scores_taken")

            def make_states(h):
                eng.wait_ge(sem("head_steps"), h * STEPS + KV + 1)
                t7 = TT[LEVELS % 2]
                for d in range(2):
                    for n in range(3):
                        c = n if d == 0 else 3 - n
                        at = (0, 1, 2)[n] if d == 0 else 2 - n
                        idx = c if d == 0 else c - 1
                        prev = state0[:, d, h, :] if n == 0 else states[:, d, at - 1 if d == 0 else at + 1, :]
                        col = (NT + c) if d == 0 else c
                        link(V.scalar_tensor_tensor(out=states[:, d, at, :], in0=prev, scalar=t7[:, col:col + 1],
                                                    in1=ps[:, 4 + d, idx * P:(idx + 1) * P], op0=ALU.mult, op1=ALU.add))
                if h:
                    eng.wait_ge(sem("stored"), 16 * h)
                link(V.tensor_copy(newst[:, :, :], ap(ps, 4 * 512 + 3 * P, [(512, 2), (1, P)])), "new_states")

            def finish_head(h):
                eng.wait_ge(sem("rms_ready"), h + 1)
                link(V.reciprocal(o_hg[:, h, :], o_hg[:, h, :]))
                link(V.scalar_tensor_tensor(out=o_hg[:, h, :], in0=banks(6), scalar=v("hg_norm", h),
                                            in1=o_hg[:, h, :], op0=ALU.mult, op1=ALU.mult))
                link(V.tensor_tensor(o_hg[:, h, :], o_hg[:, h, :], gs[:, h % 2, :], ALU.mult), "heads_done")

            def step(h, j):
                if j < KTURN:
                    take_level(h, j)
                elif j == KV:
                    make_states(h)
                elif j == NORM:
                    finish_head(h)

            eng.wait_ge(sem("v_bank"), NT)
            eng.wait_ge(sem("ld_hg"), 48)
            link(V.tensor_copy(masks[:, :, :], ap(QQ, 0, [(P, LEVELS), (1, P)]).bitcast(U32)))
            for i in range(2):
                link(V.memset(padm[:, i, :], 0.0), "pad_zero" if i else None)
            for n in range(NH):
                kind, i = TILES[n // 2]
                if step_at(n):
                    pass_k(*step_at(n))
                if n % 2 == 0:
                    for unit in ahead(n):
                        split_lo(unit)
                if n == 2 * (MIXED - IV) + 1:
                    eng.wait_ge(sem("fine_cols"), 2)
                    scale2 = mod[:, 4 * FINE[0]:4 * FINE[0] + 4 * len(FINE), :]
                    link(V.tensor_tensor(scale2, ap(ps, 5 * 512, [(4, 4 * len(FINE)), (1, 2)]),
                                         ap(vec, VEC["ada_b"] + 4 * FINE[0], [(1, 4 * len(FINE)), (0, 2)]), ALU.add))
                    link(V.tensor_tensor(scale2, ap(ps, 5 * 512 + 2, [(4, 4 * len(FINE)), (1, 2)]), scale2, ALU.add))
                    link(V.scalar_tensor_tensor(out=gain[:, 1, :, :], in0=scale2, scalar=1.0,
                                                in1=ap(vec, VEC["norm2"], [(1, KD), (0, 2)]),
                                                op0=ALU.add, op1=ALU.mult), "gain_ready")
                if n % 2 and kind in ("ff", "fb"):
                    eng.wait_ge(sem("half_free"), n + 1)
                    bound_gates(i, int(kind == "fb"))
                if step_at(n):
                    step(*step_at(n))
                if n % 2 and kind == "fb":
                    start_head(i)
                if n % 2 and kind == "hy":
                    eng.wait_ge(sem("half_free"), n + 1)
                    c, what = divmod(i, 3)
                    taps = [v("hy_conv", (w * 3 + what) * NC + c) for w in range(3)]
                    out = (cv[:, 0, :], cv[:, 1, :], x2[:, c, :])[what]
                    conv(padm[:, i % 2, :], out, taps, "hy_conv")
                    if what == 1:
                        link(V.tensor_tensor(rows64(u_hy[:, c, 0:TS]), grid(cv, 0), grid(cv, CONV), ALU.mult))
                        link(V.tensor_tensor(u_hy[:, c, TS:T], cv[:, 0, PADS:CONV], cv[:, 1, PADS:CONV], ALU.mult), "u_ready")
            for n in range(NH, FIRST_STEP + HEADS * STEPS):
                pass_k(*step_at(n))
                step(*step_at(n))

            def ada_columns(b0, b1, bank):
                eng.wait_ge(sem("ada_cols"), ADA_BLOCKS.index(b1 - 1) + 1)
                link(V.tensor_tensor(mod[:, 4 * b0:4 * b1, :], ap(ps, bank * 512 + 8 * b0, [(2, 4 * (b1 - b0)), (1, 2)]),
                                     ap(vec, VEC["ada_b"] + 4 * b0, [(1, 4 * (b1 - b0)), (0, 2)]), ALU.add), "mod_ready")

            eng.wait_ge(sem("stored"), 16 * HEADS)
            for m in range(2):
                for cs in range(2):
                    eng.wait_ge(sem("uodd"), 2 * m + cs + 1)
                    even, odd = ps[:, 4 * m + 2 * cs, :], prod[:, cs, 0, :]
                    link(V.tensor_tensor(U[:, m, 0, cs, :], even, odd, ALU.add))
                    link(V.tensor_tensor(U[:, m, 1, 1 - cs, :], even, odd, ALU.subtract), "uspec_ready")
            for m in range(2):
                C, S = U[:, m, :, 0, :], U[:, m, :, 1, :]
                Kr, Ks = kspec[:, m, :, 0, :], kspec[:, m, :, 1, :]
                r, t = prod[:, 0, :, :], prod[:, 1, :, :]
                link(V.tensor_tensor(r, C, Kr, ALU.mult))
                link(V.tensor_tensor(t, S, Ks, ALU.mult))
                link(V.tensor_tensor(r, r, t, ALU.subtract))
                link(V.tensor_tensor(t, C, Ks, ALU.mult))
                link(V.tensor_tensor(S, S, Kr, ALU.mult))
                link(V.tensor_tensor(S, S, t, ALU.add))
                link(V.tensor_tensor(U[:, m, 0, 0, :], r[:, 0, :], U[:, m, 1, 1, :], ALU.add))
                link(V.tensor_tensor(U[:, m, 1, 0, :], r[:, 1, :], U[:, m, 0, 1, :], ALU.add))
                link(V.tensor_tensor(U[:, m, 1, 1, :], r[:, 0, :], U[:, m, 1, 1, :], ALU.subtract))
                link(V.tensor_tensor(U[:, m, 0, 1, :], U[:, m, 0, 1, :], r[:, 1, :], ALU.subtract), "zspec_ready")
            eng.wait_ge(sem("up_ready"), 1)
            r, t = prod[:, 0, 0, :], prod[:, 1, 0, :]
            link(V.tensor_tensor(r, Up[:, 0, :], kspec_p[:, 0, :], ALU.mult))
            link(V.tensor_tensor(t, Up[:, 1, :], kspec_p[:, 1, :], ALU.mult))
            link(V.tensor_tensor(r, r, t, ALU.subtract))
            link(V.tensor_tensor(t, Up[:, 0, :], kspec_p[:, 1, :], ALU.mult))
            link(V.tensor_tensor(Up[:, 1, :], Up[:, 1, :], kspec_p[:, 0, :], ALU.mult))
            link(V.tensor_tensor(Up[:, 1, :], Up[:, 1, :], t, ALU.add))
            link(V.tensor_copy(Up[:, 0, :], r), "zspec_ready")
            link(V.memset(zc[:, :], 0.0), "zc_zero")
            eng.wait_ge(sem("half_made"), NH)
            link(V.tensor_copy(h_hi[:, 0:NC, :], o_hg[:, :, :]))
            link(V.tensor_tensor(h_lo[:, 0:NC, :], o_hg[:, :, :], h_hi[:, 0:NC, :].bitcast(F32), ALU.subtract), "heads_split")
            ada_columns(4, 8, 7)
            for c in range(NC):
                eng.wait_ge(sem("z_ready"), c + 1)
                link(V.scalar_tensor_tensor(out=grid(zc, 0), in0=rows64(u_hy[:, c, 0:TS]), scalar=v("hy_d", c),
                                            in1=grid(zc, 0), op0=ALU.mult, op1=ALU.add))
                link(V.scalar_tensor_tensor(out=zc[:, PADS:CONV], in0=u_hy[:, c, TS:T], scalar=v("hy_d", c),
                                            in1=zc[:, PADS:CONV], op0=ALU.mult, op1=ALU.add))
                link(V.tensor_tensor(x2[:, c, :], x2[:, c, :], zc[:, :], ALU.mult), "yhy_ready")
                if c in (1, 2):
                    split_lo(UNIT_WOUT + c - 1)
            eng.wait_ge(sem("rms_ready"), HEADS + 1)
            link(V.reciprocal(sq[:, :], sq[:, :]))
            for pair in range(2):
                cs = (2 * pair, 2 * pair + 1)
                for c in cs:
                    link(V.scalar_tensor_tensor(out=x2[:, c, :], in0=x2[:, c, :], scalar=v("hy_norm", c),
                                                in1=sq[:, :], op0=ALU.mult, op1=ALU.mult))
                at, src_at = (NC + cs[0]) * T, cs[0] * CONV
                latent = [(T, 2), (GRID, ROWS), (1, GRID)]
                context = [(T, 2), (1, TP)]
                x_lat = ap(x2, src_at, [(CONV, 2), (PADROW, ROWS), (1, GRID)])
                x_ctx = ap(x2, src_at + PADS, [(CONV, 2), (1, TP)])
                link(V.tensor_copy(ap(h_hi, at, latent), x_lat))
                link(V.tensor_copy(ap(h_hi, at + TS, context), x_ctx))
                link(V.tensor_tensor(ap(h_lo, at, latent), x_lat, ap(h_hi, at, latent).bitcast(F32), ALU.subtract))
                link(V.tensor_tensor(ap(h_lo, at + TS, context), x_ctx, ap(h_hi, at + TS, context).bitcast(F32),
                                     ALU.subtract), "merged")
                split_lo(UNIT_WOUT + 2 + pair)

            def add(which, i, n, name_taken, name_done):
                s = int(i == NT - 1)
                link(V.tensor_tensor(tmpd[:, :], ps[:, i, :], grow[:, which, s, n * HW:(n + 1) * HW], ALU.mult), name_taken)
                xs = x1[:, i, n * HW:(n + 1) * HW]
                link(V.tensor_tensor(xs, xs, tmpd[:, :], ALU.add), name_done)

            def norm_rows(i):
                eng.wait_ge(sem("norm_ready"), NT + i + 1)
                link(V.reciprocal(stat[:, 1, 1, i:i + 1], stat[:, 1, 1, i:i + 1]))
                link(V.tensor_scalar(xn[:, i, :], x1[:, i, :], stat[:, 1, 1, i:i + 1], None, ALU.mult), "x_scaled")

            for n in range(2):
                for k in range(2):
                    split_lo(UNIT_WOUT + WOUT + 2 * n + k)
                if n == 0:
                    eng.wait_ge(sem("ld_res"), 16 * NT)
                    eng.wait_ge(sem("row_ready"), 4)
                for i in range(NT):
                    eng.wait_ge(sem("mixed"), NT * n + i + 1)
                    add(0, i, n, "mixed_taken", "x1_ready")
                    if n and i:
                        norm_rows(i - 1)
            norm_rows(NT - 1)
            split_lo(UNIT_FFN)
            split_lo(UNIT_FFN + 1)
            ada_columns(10, 12, 7)
            for k in range(KD):
                split_h(1, k)
            for i in range(2):
                for gv in range(2):
                    link(V.memset(padf[:, i, gv, :], 0.0), "padf_zero" if i and gv else None)
            def final_norm(i):
                if i == 0:
                    eng.wait_ge(sem("ld_fnw"), 16)
                eng.wait_ge(sem("norm_ready"), 2 * NT + i + 1)
                link(V.reciprocal(stat[:, 2, 1, i:i + 1], stat[:, 2, 1, i:i + 1]))
                for cols in y_parts(i):
                    link(V.scalar_tensor_tensor(out=x1[:, i, cols], in0=x1[:, i, cols], scalar=stat[:, 2, 1, i:i + 1],
                                                in1=fnw[:, cols], op0=ALU.mult, op1=ALU.mult), "y_ready")

            unit, t = UNIT_FFN, 0
            for r, (f0, nf) in enumerate(ROUNDS):
                for f in range(nf):
                    for gv in range(2):
                        split_lo(unit + 2)
                        unit += 1
                        eng.wait_ge(sem("half_free"), NH + 4 * t + 2 * gv + 2)
                        taps = [v("ffn_conv", (w * 2 + gv) * NF + f0 + f) for w in range(3)]
                        conv(padf[:, t % 2, gv, :], cf[:, gv, :], taps, "fconv")
                    eng.wait_ge(sem("silu_done"), t + 1)
                    link(V.tensor_tensor(rows64(actf[:, 0:TS]), grid(cf, 0), grid(cf, CONV), ALU.mult))
                    link(V.tensor_tensor(actf[:, TS:T], cf[:, 0, PADS:CONV], cf[:, 1, PADS:CONV], ALU.mult), "act_ready")
                    eng.wait_ge(sem("ahi_ready"), t + 1)
                    link(V.tensor_tensor(a_lo[:, f, :], actf[:, :], a_hi[:, f, :].bitcast(F32), ALU.subtract), "a_ready")
                    t += 1
                for n in range(2):
                    for k in range(nf // 2):
                        split_lo(unit + 2)
                        unit += 1
                    for i in range(NT):
                        eng.wait_ge(sem("down_made"), (2 * r + n) * NT + i + 1)
                        last_half = n and r == len(ROUNDS) - 1
                        if last_half and i == NT - 1:
                            final_norm(i - 1)
                        add(1, i, n, "down_taken", "down_added")
                        if last_half and 0 < i < NT - 1:
                            final_norm(i - 1)
            final_norm(NT - 1)

        @block.tensor
        def _(eng):
            mm = nc.tensor.matmul

            def split_product(out, lhs, rhs, first, last):
                mm(out, lhs[0], rhs[0], start=first, stop=False)
                mm(out, lhs[0], rhs[1], start=False, stop=False)
                return mm(out, lhs[1], rhs[0], start=False, stop=last)

            def unit_ready(n):
                eng.wait_ge(sem("hi_ready"), n + 1)
                eng.wait_ge(sem("lo_ready"), n + 1)
                return w_hi[:, n % SPLITS, :], w_lo[:, n % SPLITS, :]

            def ada_block(b, parts=(0, 1)):
                bank = ROW_BANK[b]
                if 0 in parts and bank in ROW_BANK[:b]:
                    eng.wait_ge(sem("ada_row"), b - ROW_BANK[:b][::-1].index(bank))
                for i in parts:
                    slot = ADA_SLOTS[2 * b + i]
                    arrived(eng, slot)
                    for kk in range(4):
                        k = 4 * i + kk
                        last = mm(ps[0:2, bank, :], silu_c[:, k, :], raw[:, slot % RAWS, kk * HW:(kk + 1) * HW],
                                  start=(k == 0), stop=(k == KD - 1))
                    last.then_inc(sem("ada_used"), 1)

            def ada_turn(b, bank):
                eng.wait_ge(sem("ada_row"), b + 1)
                for k in range(4):
                    col = 8 * ADA_BLOCKS[b] + 2 * k
                    last = nc.tensor.transpose(ps[:, bank, col:col + 2], ADA_ROWS[b][0:2, b % 2, k * P:(k + 1) * P],
                                               ident[0:2, 0:2])
                last.then_inc(sem("ada_cols"), 1)

            def ada_blocks(b0, b1):
                for b in range(b0, b1):
                    ada_block(b)
                    if b > b0:
                        ada_turn(b - 1, 7)
                ada_turn(b1 - 1, 7)

            def taps(i):
                if i >= 2:
                    eng.wait_ge(sem("taps_ready"), i - 1)
                for d in range(2):
                    last = mm(ps[:, 4 + 2 * (i % 2) + d, :], hid[0:NHID, 1, i * P:(i + 1) * P],
                              w3[0:NHID, d * HW:(d + 1) * HW], start=True, stop=True)
                last.then_inc(sem("taps_made"), 1)

            eng.wait_ge(sem("ld_filt"), 32)
            mm(ps[0:NHID, 0, :], w1[0:NEMB, :], feats[0:NEMB, 0:TS], start=True, stop=True)
            mm(ps[0:NHID, 1, 0:TP], w1[0:NEMB, :], feats[0:NEMB, TS:T], start=True, stop=True).then_inc(sem("hid_made"), 1)
            eng.wait_ge(sem("silu_c"), 1)
            ada_block(0, (0,))
            eng.wait_ge(sem("ld_hid"), 32)
            eng.wait_ge(sem("hid_ready"), 1)
            mm(ps[0:NHID, 0, :], w2[0:NHID, :], hid[0:NHID, 0, 0:TS], start=True, stop=True)
            mm(ps[0:NHID, 1, 0:TP], w2[0:NHID, :], hid[0:NHID, 0, TS:T], start=True, stop=True).then_inc(sem("hid_made"), 1)
            ada_block(0, (1,))
            ada_block(1, (0,))
            eng.wait_ge(sem("hid_ready"), 2)
            taps(0)
            taps(1)
            taps(2)
            ada_block(1, (1,))
            eng.wait_ge(sem("ld_ident"), 16)
            ada_turn(0, 3)
            taps(3)
            ada_block(2, (0,))
            taps(4)
            ada_turn(1, 3)
            ada_block(2, (1,))
            ada_block(3)
            ada_turn(2, 3)
            eng.wait_ge(sem("ones_ready"), 2)
            eng.wait_ge(sem("sides_ready"), NT)
            for s in range(2):
                for c in range(NC):
                    last = mm(ps[:, 4, s * NC + c:s * NC + c + 1], tapsum[:, s, c * P:(c + 1) * P], ones[:, 0:1],
                              start=True, stop=True)
            last.then_inc(sem("tapsums"), 1)
            ada_turn(3, 3)

            def turn(src, which, before, between):
                for k in range(KD):
                    if k >= 2:
                        eng.wait_ge(sem("h_full"), KD * which + k - 1)
                    if k == 1 and before:
                        for name, value in before:
                            eng.wait_ge(sem(name), value)
                    b = 2 * (k % 2)
                    for i in range(NT):
                        if k == 0:
                            eng.wait_ge(sem("x_scaled"), NT * which + i + 1)
                        dst = ps[:, b, i * P:(i + 1) * P] if i < 4 else ps[:, b + 1, 0:P]
                        last = nc.tensor.transpose(dst, src[:, i, k * P:(k + 1) * P], ident[:, :])
                    last.then_inc(sem("h_turned"), 1)
                    between(k)

            def filter_dft(n, cs, e, k):
                rhs = filt[:, 0, 2 * e + k, :] if cs == 0 else decay[:, 2 * e + k, :]
                m = 1 - n // 2
                last = mm(ps[:, 4 + 2 * cs + e, :], ktab[:, cs, e, k, m * P:(m + 1) * P], rhs, start=(k == 0), stop=(k == 1))
                if e and k:
                    last.then_inc(sem("kdft"), 1)

            eng.wait_ge(sem("ld_ktab"), 32)
            eng.wait_ge(sem("hid_ready"), 2)

            def filter_between(k):
                if k == 0:
                    eng.wait_ge(sem("knorm_ready"), 1)
                filter_dft(k // 4, k // 4, (k // 2) % 2, k % 2)

            turn(xin, 0, (("gain_ready", 1),), filter_between)
            for n in range(2, 4):
                eng.wait_ge(sem("kspec_ready"), n - 1)
                for e in range(2):
                    for k in range(2):
                        filter_dft(n, n % 2, e, k)
                if n == 2:
                    eng.wait_ge(sem("h_full"), KD)
                    mm(ps[:, 0, :], ptab_k[:, 0, :], filt[:, 0, NT - 1, :], start=True, stop=True)
                    mm(ps[:, 1, :], ptab_k[:, 1, :], decay[:, NT - 1, :], start=True, stop=True).then_inc(sem("kdft"), 1)

            def fine_unit(j):
                hi, lo = unit_ready(2 * j + 1)
                for kk in range(2):
                    k = 2 * (j % 4) + kk
                    for n, w in enumerate((hi, lo)):
                        last = mm(ps[0:4, 6 + j // 4, :], silu_parts[:, k, :], w[:, kk * HW:(kk + 1) * HW],
                                  start=(k == 0 and n == 0), stop=(k == KD - 1 and n == 1))
                last.then_inc(sem("fine_used"), 1)

            def fine_turn(f):
                eng.wait_ge(sem("fine_row"), f + 1)
                for k in range(4):
                    col = 16 * f + 4 * k
                    last = nc.tensor.transpose(ps[:, 5, col:col + 4], fine_rows(f)[:, k * P:(k + 1) * P], ident[0:4, 0:4])
                last.then_inc(sem("fine_cols"), 1)

            def token_major(unit0, pairs, lhs, name, before, bank=range(NT), part=None, tiles_first=False, mixed=False):
                steps = [(p, i) for p in part or range(pairs) for i in range(NT)]
                if tiles_first:
                    steps.sort(key=lambda step: (step[1] // 2, step[1] < 2 and step[0] == pairs - 1, step[1]))
                for p, i in steps:
                    unit = unit0 + (2 if mixed else 1) * p
                    if i == 0:
                        unit_ready(unit)
                    hi, lo = (w[:, unit % SPLITS, :] for w in (w_hi, w_lo))
                    for kk in range(2):
                        k = 2 * p + kk
                        before(p, i, k)
                        last = split_product(ps[:, bank[i], :], [x[:, k, i * P:(i + 1) * P] for x in lhs],
                                             [x[:, kk * HW:(kk + 1) * HW] for x in (hi, lo)],
                                             k == 0, k == 2 * pairs - 1)
                    if p == pairs - 1:
                        last.then_inc(sem(name), 1)
                    elif i == NT - 1:
                        last.then_inc(sem("unit_done"), 1)
                    if mixed and i == NT - 1:
                        fine_unit(p)

            def before_v(p, i, k):
                if i == 0:
                    eng.wait_ge(sem("h_split"), k + 1)
                if p == 0 and i == 2 and k == 0:
                    eng.wait_ge(sem("kspec_ready"), 5)

            token_major(0, IV, (h_hi, h_lo), "v_bank", before_v, V_BANKS, mixed=True)

            def chunk(j, c):
                b = score_bank(j)
                return ps[:, b, c * P:(c + 1) * P] if c < 4 else ps[:, b + 1, 0:P]

            def step(h, j):
                if j == DIAG:
                    eng.wait_ge(sem("qk_next"), 8 * h + 1)
                    if h:
                        eng.wait_ge(sem("rms_ready"), h)
                    for c in range(NT):
                        last = mm(chunk(j, c), kdiag[:, c * P:(c + 1) * P], qs[:, c * P:(c + 1) * P], start=True, stop=True)
                elif j < KTURN:
                    l = j - LEVEL0
                    s = 1 << l
                    eng.wait_ge(sem("kc_ready"), LEVELS * h + l + 1)
                    eng.wait_ge(sem("qk_next"), 8 * h + 1 + l)
                    if j == 1 and h:
                        eng.wait_ge(sem("heads_done"), h)
                    if j >= 2:
                        eng.wait_ge(sem("scores_taken"), 8 * h + j - 1)
                    for c in range(NT):
                        last = mm(chunk(j, c), kc[:, l % 2, c * P:(c + 1) * P],
                                  ap(QQ, c * P, [(2 * s, P // (2 * s)), (T + s, 2), (1, s)]), start=True, stop=True)
                elif j == KTURN:
                    eng.wait_ge(sem("k_next"), 8 * h + 8)
                    eng.wait_ge(sem("scores_taken"), 8 * h + 7)
                    for d in range(2):
                        for n, c in enumerate((0, 1, 2, 4) if d == 0 else (1, 2, 3, 4)):
                            last = nc.tensor.transpose(ps[:, 4 + d, n * P:(n + 1) * P], KK[:, d, c * P:(c + 1) * P], ident[:, :])
                elif j == KV:
                    eng.wait_ge(sem("ktok_ready"), h + 1)
                    for d in range(2):
                        for n, c in enumerate((0, 1, 2, 4) if d == 0 else (1, 2, 3, 4)):
                            last = mm(ps[:, 4 + d, n * P:(n + 1) * P], ktok[:, d, n, :], vtok[:, c, h * P:(h + 1) * P],
                                      start=True, stop=True)
                elif j == OUT:
                    eng.wait_ge(sem("new_states"), h + 1)
                    eng.wait_ge(sem("scores_taken"), 8 * h + 8)
                    for c in range(NT):
                        out = ps[:, 6, c * P:(c + 1) * P] if c < 4 else ps[:, 7, 0:P]
                        cols = slice(c * P, (c + 1) * P)
                        last = mm(out, vtok[:, c, h * P:(h + 1) * P], scores[:, cols], start=True, stop=(c == 4))
                        if c < 4:
                            sf = state0[:, 0, h, :] if c == 0 else states[:, 0, c - 1, :]
                            sbk = state0[:, 1, h, :] if c == 3 else states[:, 1, c, :]
                            mm(out, sf, QQ[:, 1, cols], start=False, stop=False)
                            last = mm(out, sbk, QQ[:, 0, cols], start=False, stop=True)
                elif j == NORM:
                    eng.wait_ge(sem("osq_ready"), h + 1)
                    mm(ps[:, 4, :], ones[:, :], o_hg[:, h, 0:TS], start=True, stop=True)
                    last = mm(ps[:, 5, 0:TP], ones[:, :], o_hg[:, h, TS:T], start=True, stop=True)
                last.then_inc(sem("head_steps"), 1)

            def half_product(n, unit, half):
                bank = half_bank(n)
                hi, lo = unit_ready(unit)
                for k in range(KD):
                    if n == NH:
                        eng.wait_ge(sem("h_split"), KD + k + 1)
                    cols = slice(half * HT, (half + 1) * HT)
                    last = split_product(ps[:, bank, 0:HT], [x[:, k * P:(k + 1) * P] for x in (hi, lo)],
                                         (h_hi[:, k, cols], h_lo[:, k, cols]), k == 0, k == KD - 1)
                last.then_inc(sem("half_made"), 1)

            for n in range(NH):
                if n < 4:
                    eng.wait_ge(sem("v_ready"), V_BANKS.index(n) + 1)
                elif n == 4:
                    eng.wait_ge(sem("v_ready"), NT)
                if n >= 4:
                    eng.wait_ge(sem("half_free"), n - 3)
                half_product(n, tile_unit(n // 2), n % 2)
                if n % 2 and n // 2 < MIXED - IV:
                    fine_unit(IV + n // 2)
                if n == 1:
                    fine_turn(0)
                if n == 2 * (MIXED - IV):
                    fine_turn(1)
                if n == 2 * (MIXED - IV) + 1:
                    eng.wait_ge(sem("gain_ready"), 2)
                if step_at(n):
                    step(*step_at(n))
            def turn_u(i):
                for c in range(NC):
                    if i < 4:
                        e, k = divmod(i, 2)
                        src = ap(u_hy, c * T + 2 * P * k + e, [(2, P)])
                    else:
                        src = u_hy[:, c, TS:T]
                    last = nc.tensor.transpose(ps[:, i, c * P:(c + 1) * P], src, ident[:, :])
                last.then_inc(sem("u_turned"), 1)

            for n in range(NH, FIRST_STEP + HEADS * STEPS):
                if step_at(n)[1] == NORM:
                    eng.wait_ge(sem("half_free"), NH)
                    eng.wait_ge(sem("u_ready"), NC)
                    for i in range(4):
                        turn_u(i)
                step(*step_at(n))
            eng.wait_ge(sem("ut_ready"), 4)
            eng.wait_ge(sem("ld_utab"), 16)
            for m in range(2):
                if m:
                    eng.wait_ge(sem("heads_done"), HEADS)
                    eng.wait_ge(sem("ut_ready"), NT)
                for cs in range(2):
                    if (m, cs) == (0, 1):
                        eng.wait_ge(sem("rms_ready"), HEADS)
                        turn_u(4)
                    for e in range(2):
                        for k in range(2):
                            last = mm(ps[:, 4 * m + 2 * cs + e, :], utab[:, cs, e, k, m * P:(m + 1) * P],
                                      ut[:, 2 * e + k, :], start=(k == 0), stop=(k == 1))
                    last.then_inc(sem("udft"), 1)
            eng.wait_ge(sem("uspec_ready"), 1)
            eng.wait_ge(sem("ld_itab"), 32)
            mm(ps[:, 0, :], ptab[:, 0, 0, :], ut[:, NT - 1, :], start=True, stop=True)
            mm(ps[:, 1, :], ptab[:, 0, 1, :], ut[:, NT - 1, :], start=True, stop=True).then_inc(sem("udft"), 1)
            eng.wait_ge(sem("uspec_ready"), 4)
            ada_blocks(4, 8)
            eng.wait_ge(sem("zspec_ready"), 3)

            def sum_channels(c):
                eng.wait_ge(sem("ysq_ready"), c + 1)
                for half in range(2):
                    last = mm(ps[:, 4 + half, 0:CONV // 2], ones[:, :], sq[:, half * (CONV // 2):(half + 1) * (CONV // 2)],
                              start=(c == 0), stop=(c == NC - 1))
                last.then_inc(sem("ysq_used"), 1)

            for c in range(NC):
                b = 2 * (c % 2)
                if c >= 2:
                    eng.wait_ge(sem("z_ready"), c - 1)
                cols = slice(c * P, (c + 1) * P)
                for e in range(2):
                    for n, (m, cs) in enumerate(((0, 0), (0, 1), (1, 0), (1, 1))):
                        lhs = U[:, m, cs, 0, cols] if e == 0 else U[:, m, 1 - cs, 1, cols]
                        mm(ps[:, b, e * 256:(e + 1) * 256], lhs, itab[:, m, cs, e, :], start=(n == 0), stop=(n == 3))
                for cs in range(2):
                    last = mm(ps[:, b + 1, 0:TP], Up[:, cs, cols], ptab[:, 1, cs, :], start=(cs == 0), stop=(cs == 1))
                last.then_inc(sem("z_made"), 1)
                if c:
                    sum_channels(c - 1)
            def gate_part(r, k):
                which, s, half = r // 4, (r // 2) % 2, r % 2
                if r >= 3 and k == 0:
                    eng.wait_ge(sem("row_ready"), r - 2)
                col = (2 + 3 * which) * KD + 4 * half + k
                last = mm(ps[:, 5 + r % 3, k * P:(k + 1) * P], ap(mod, 2 * col + s, [(0, P)]), ident[:, :],
                          start=True, stop=True)
                if k == 3:
                    last.then_inc(sem("row_made"), 1)

            def before_mixed(p, i, k):
                if p == 0 and i == 2 and k == 0:
                    sum_channels(NC - 1)
                if p == 0 and i == NT - 1 and k == 0:
                    eng.wait_ge(sem("rms_ready"), HEADS + 1)

            def before_mixed2(p, i, k):
                if k == 0:
                    eng.wait_ge(sem("mixed_taken"), i + 1)

            eng.wait_ge(sem("heads_split"), 1)
            eng.wait_ge(sem("z_ready"), NC)
            token_major(UNIT_WOUT, WOUT, (h_hi, h_lo), "mixed", before_mixed, part=range(2))
            eng.wait_ge(sem("mod_ready"), 1)
            for r in range(3):
                for k in range(4):
                    gate_part(r, k)
            eng.wait_ge(sem("merged"), 1)
            token_major(UNIT_WOUT, WOUT, (h_hi, h_lo), "mixed", before_mixed, part=range(2, 3))
            for k in range(4):
                gate_part(3, k)
            eng.wait_ge(sem("merged"), 2)
            token_major(UNIT_WOUT, WOUT, (h_hi, h_lo), "mixed", before_mixed, part=range(3, 4))
            token_major(UNIT_WOUT + WOUT, WOUT, (h_hi, h_lo), "mixed", before_mixed2)
            eng.wait_ge(sem("row_ready"), 4)
            ada_blocks(8, 10)

            def gate_between(k):
                if k == 0:
                    eng.wait_ge(sem("mod_ready"), 2)
                for part in range(3 * k, min(3 * k + 3, 16)):
                    gate_part(4 + part // 4, part % 4)

            eng.wait_ge(sem("mixed_taken"), 2 * NT)
            turn(xn, 1, (), gate_between)
            eng.wait_ge(sem("row_ready"), 8)
            unit, n = UNIT_FFN, NH
            for r, (f0, nf) in enumerate(ROUNDS):
                for t in range(2 * nf):
                    for half in range(2):
                        if n >= NH + 3:
                            eng.wait_ge(sem("half_free"), n - 2)
                        half_product(n, unit, half)
                        n += 1
                    unit += 1
                for half in range(2):
                    x = 2 * r + half

                    def before_down(p, i, k, f0=f0, half=half, x=x):
                        if half == 0 and i == 0:
                            eng.wait_ge(sem("a_ready"), f0 + k + 1)
                        if x and k == 0:
                            eng.wait_ge(sem("down_taken"), (x - 1) * NT + i + 1)

                    token_major(unit, nf // 2, (a_hi, a_lo), "down_made", before_down,
                                tiles_first=x == 2 * len(ROUNDS) - 1)
                    unit += nf // 2


def grid(t, offset):
    return ap(t, offset, [(PADROW, ROWS), (1, GRID)])


def rows64(t):
    return t.rearrange("p (r c) -> p r c", c=GRID)


def lay_out(x):
    cols = np.zeros((P, NVEC), np.float32)

    def put(name, a):
        a = np.asarray(a).reshape(-1)
        n = -(-a.size // P)
        for i in range(n):
            part = a[i * P:(i + 1) * P]
            cols[:part.size, VEC[name] + i] = part

    for name, key in (("c", "c"), ("c_ctx", "c_ctx"), ("norm1", "norm1_w"), ("norm2", "norm2_w"), ("ada_b", "ada_b"),
                      ("lb_f", "hg_lb_fwd"), ("lb_b", "hg_lb_bwd"), ("hg_norm", "hg_norm_w"), ("hy_d", "hy_d"),
                      ("hy_norm", "hy_norm_w"), ("hy_conv", "hy_conv_w"), ("ffn_conv", "ffn_conv_w"),
                      ("b1", "hy_b1"), ("fr1", "hy_freq1"), ("b2", "hy_b2"), ("fr2", "hy_freq2")):
        put(name, x[key])

    def cut(w, r0, nr, c0, ncol):
        return w[r0:r0 + nr * P, c0:c0 + ncol].reshape(nr, P, ncol).transpose(1, 0, 2).reshape(P, nr * ncol)

    ada, w_in, w_out = x["ada_w"][0], x["w_in"][0], x["w_out"][0]
    up, down = x["ffn_w_up"][0], x["ffn_w_down"][0]
    slots = np.zeros((NSLOT, P, RAW * UNIT), np.float32)
    s = 0

    def slot(*parts):
        nonlocal s
        at = 0
        for p in parts:
            slots[s, :, at:at + p.shape[1]] = p
            at += p.shape[1]
        s += 1

    def ada_blocks(b0, b1):
        for b in ADA_BLOCKS[b0:b1]:
            for i in range(2):
                slot(cut(ada, i * HW, 4, b * HW, HW))

    def tile(t):
        return cut(w_in, 0, KD, tile_column(TILES[t]), P)

    ada_blocks(0, 4)
    for j in range(MIXED):
        slot(cut(w_in, 2 * j * P, 2, 3 * HW, HW) if j < IV else tile(j - IV),
             cut(ada, 2 * (j % 4) * P, 2, FINE[j // 4] * HW, HW))
    for t in range(MIXED - IV, len(TILES), 2):
        slot(tile(t), tile(t + 1))
    ada_blocks(4, 8)
    for n in range(2):
        for i in range(2):
            slot(cut(w_out, i * HW, 4, n * HW, HW))
    ada_blocks(8, 10)
    for f0, nf in ROUNDS:
        for f in range(f0, f0 + nf):
            slot(cut(up, 0, KD, f * P, P), cut(up, 0, KD, F + f * P, P))
        for n in range(2):
            for f in range(f0, f0 + nf, 4):
                slot(cut(down, f * P, min(4, f0 + nf - f), n * HW, HW))
    return cols, slots


OUTS = [("y_prompt", (1, TP, D)), ("y_sample", (1, TS, D)), ("new_state", (1, 1, 2, HEADS, P, P))]


def kernel(**inputs):
    import concourse.bacc as bacc
    from concourse.bass_utils import run_bass_kernel_spmd

    x = {k: np.ascontiguousarray(a) for k, a in inputs.items()}
    given = {k: x[k] for k in ("x_prompt", "x_sample", "state_hgrn", "hy_w1", "hy_w2", "hy_w3", "final_norm_w")}
    given["vec"], given["slots"] = lay_out(x)
    given.update(constants())
    nc = bacc.Bacc("TRN2", target_bir_lowering=False, num_devices=1)
    io, arrays = {}, {}
    for name, a in given.items():
        arrays[f"in_{name}"] = np.ascontiguousarray(a)
        io[name] = nc.dram_tensor(f"in_{name}", a.shape, mybir.dt.from_np(a.dtype), kind="ExternalInput").ap()
    for name, shape in OUTS:
        io[name] = nc.dram_tensor(f"out_{name}", shape, F32, kind="ExternalOutput").ap()
    build(nc, io)
    r = run_bass_kernel_spmd(nc, [arrays], core_ids=[0])
    return tuple(r.results[0][f"out_{name}"] for name, _ in OUTS)
```
